# Optimizing a Trainium2 kernel written in Bass

```python
import jax, jax.numpy as jnp
from jax import lax
import numpy as np

D_MODEL = 1024
BATCH = 1
SEQ = 256
DEPTH = 1
DEC_BATCH = 8
DEC_SEQ = 4
PAST_LEN = 2048
PAGE_SIZE = 128

N_META = 16
D_MIX = D_MODEL
D_A = 3 * D_MIX // 8
D_B = D_MIX // 4
D_C = D_MIX - D_A - D_B
N_BLK_A = 8
BLK_A = D_A // N_BLK_A
CONV_A = 4
RG_C = 8.0
CONV_B = 31
N_HEADS_C = 4
DV_C = D_C // N_HEADS_C
DK_C = DV_C // 2
D_QK_C = N_HEADS_C * DK_C
GATE_RANK = 16
GATE_TAU = 16.0
CHUNK_C = 64
D_IN = 2 * D_A + 2 * D_B + 2 * D_QK_C + 2 * D_C + GATE_RANK
N_EXPERTS = 32
TOP_K = 4
D_FF = D_MODEL
SWIGLU_LIMIT = 7.0
SWIGLU_ALPHA = 1.702
MOE_BLOCK = 128
DEEPNORM_ALPHA = (2 * DEPTH) ** 0.25
DEEPNORM_BETA = (8 * DEPTH) ** -0.25
LN_EPS = 1e-5

kernel_name = "hymba_rglru_conformer_gla_moe_step"

def layer_norm(x, g, b):
    xf = x.astype(jnp.float32)
    mu = jnp.mean(xf, axis=-1, keepdims=True)
    var = jnp.mean(jnp.square(xf - mu), axis=-1, keepdims=True)
    y = (xf - mu) * lax.rsqrt(var + LN_EPS) * g.astype(jnp.float32) + b.astype(jnp.float32)
    return y.astype(x.dtype)

def causal_depthwise_conv(x, buf, w, b):
    width = w.shape[0]
    xp = jnp.concatenate([buf.astype(x.dtype), x], axis=1)
    y = lax.conv_general_dilated(xp, w.astype(x.dtype)[:, None, :], window_strides=(1,), padding="VALID",
                                 dimension_numbers=("NWC", "WIO", "NWC"), feature_group_count=x.shape[-1])
    return y + b, xp[:, -(width - 1):]

def _linear_recurrence_combine(e1, e2):
    a1, b1 = e1
    a2, b2 = e2
    return a1 * a2, a2 * b1 + b2

def rglru(xc, h0, w_rg, b_rg, w_ig, b_ig, lru_lambda):
    bsz, t, _ = xc.shape
    xh = xc.reshape(bsz, t, N_BLK_A, BLK_A)
    r = jax.nn.sigmoid(jnp.einsum("bthi,hij->bthj", xh, w_rg).reshape(bsz, t, D_A) + b_rg)
    i = jax.nn.sigmoid(jnp.einsum("bthi,hij->bthj", xh, w_ig).reshape(bsz, t, D_A) + b_ig)
    log_a = -RG_C * jax.nn.softplus(-lru_lambda.astype(jnp.float32)) * r.astype(jnp.float32)
    a = jnp.exp(log_a)
    u = jnp.sqrt(-jnp.expm1(2.0 * log_a)) * (i * xc).astype(jnp.float32)
    u = u.at[:, 0].add(a[:, 0] * h0.astype(jnp.float32))
    _, h = lax.associative_scan(_linear_recurrence_combine, (a, u), axis=1)
    return h.astype(xc.dtype), h[:, -1].astype(xc.dtype)

def gla_chunk_scan(q, k, v, g, s0, chunk):
    bsz, t, h, dk = q.shape
    dv = v.shape[-1]
    n = t // chunk

    def to_chunks(z):
        return z.reshape(bsz, n, chunk, *z.shape[2:]).swapaxes(0, 1)

    mask = jnp.tril(jnp.ones((chunk, chunk), dtype=bool))[None, :, :, None, None]

    def step(s, inp):
        qc, kc, vc, gc = inp
        gcum = jnp.cumsum(gc, axis=1)
        g_last = gcum[:, -1]
        o_inter = jnp.einsum("bthd,bhde->bthe", qc * jnp.exp(gcum), s)
        diff = gcum[:, :, None] - gcum[:, None, :]
        decay = jnp.where(mask, jnp.exp(jnp.where(mask, diff, 0.0)), 0.0)
        scores = jnp.einsum("bthd,bshd,btshd->bhts", qc, kc, decay)
        o_intra = jnp.einsum("bhts,bshe->bthe", scores, vc)
        s_new = jnp.exp(g_last)[..., None] * s + jnp.einsum("bshd,bshe->bhde", kc * jnp.exp(g_last[:, None] - gcum), vc)
        return s_new, o_inter + o_intra

    s, o = lax.scan(step, s0, (to_chunks(q), to_chunks(k), to_chunks(v), to_chunks(g)))
    return o.swapaxes(0, 1).reshape(bsz, t, h, dv), s

def mixer(x, state, gla_segments, lp):
    conv_a_buf, h0, conv_b_buf, s0 = state
    bsz, t, _ = x.shape
    f32 = jnp.float32
    sizes = (D_A, D_A, D_B, D_B, D_QK_C, D_QK_C, D_C, D_C)
    xa, ga, vb, gb, qc, kc, vc, rc, zc = jnp.split(x @ lp["w_in"], np.cumsum(sizes).tolist(), axis=-1)
    xa_conv, conv_a_new = causal_depthwise_conv(xa, conv_a_buf, lp["conv_a_w"], lp["conv_a_b"])
    h, h_last = rglru(xa_conv, h0, lp["w_rg"], lp["b_rg"], lp["w_ig"], lp["b_ig"], lp["lru_lambda"])
    y_a = h * jax.nn.gelu(ga, approximate=True)
    u = vb * jax.nn.sigmoid(gb)
    uc, conv_b_new = causal_depthwise_conv(u, conv_b_buf, lp["conv_b_w"], lp["conv_b_b"])
    y_b = jax.nn.silu(layer_norm(uc, lp["ln_b_g"], lp["ln_b_b"]))
    q = qc.reshape(bsz, t, N_HEADS_C, DK_C).astype(f32) * (DK_C ** -0.5)
    k = kc.reshape(bsz, t, N_HEADS_C, DK_C).astype(f32)
    v = vc.reshape(bsz, t, N_HEADS_C, DV_C).astype(f32)
    g = jax.nn.log_sigmoid((zc @ lp["w_gate2"] + lp["b_gate"]).astype(f32)).reshape(bsz, t, N_HEADS_C, DK_C) / GATE_TAU
    s = s0.astype(f32)
    outs = []
    start = 0
    for seg_len, chunk in gla_segments:
        sl = slice(start, start + seg_len)
        o_seg, s = gla_chunk_scan(q[:, sl], k[:, sl], v[:, sl], g[:, sl], s, chunk)
        outs.append(o_seg)
        start += seg_len
    o = jnp.concatenate(outs, axis=1)
    o = o * lax.rsqrt(jnp.mean(jnp.square(o), axis=-1, keepdims=True) + LN_EPS) * lp["gla_norm_g"].astype(f32)
    y_c = o.reshape(bsz, t, D_C).astype(x.dtype) * jax.nn.silu(rc)
    y = jnp.concatenate([y_a, y_b, y_c], axis=-1) @ lp["w_out"]
    return y, (conv_a_new, h_last, conv_b_new, s.astype(x.dtype))

def moe(h, lp):
    bsz, t, d = h.shape
    xf = h.reshape(-1, d)
    n = xf.shape[0]
    m = n * TOP_K
    logits = (xf @ lp["router_w"] + lp["router_b"]).astype(jnp.float32)
    top_val, top_idx = lax.top_k(logits, TOP_K)
    gates = jax.nn.softmax(top_val, axis=-1).astype(h.dtype)
    flat_e = top_idx.reshape(-1)
    order = jnp.argsort(flat_e)
    sorted_e = flat_e[order]
    tok = order // TOP_K
    counts = jnp.bincount(flat_e, length=N_EXPERTS)
    padded = (counts + MOE_BLOCK - 1) // MOE_BLOCK * MOE_BLOCK
    pad_end = jnp.cumsum(padded)
    pad_start = pad_end - padded
    start = jnp.cumsum(counts) - counts
    dest = pad_start[sorted_e] + jnp.arange(m) - start[sorted_e]
    n_blocks = -(-m // MOE_BLOCK) + N_EXPERTS
    buf = jnp.zeros((n_blocks * MOE_BLOCK, d), h.dtype).at[dest].set(xf[tok])
    block_e = jnp.minimum(jnp.searchsorted(pad_end, jnp.arange(n_blocks) * MOE_BLOCK, side="right"), N_EXPERTS - 1)

    def expert_block(args):
        xb, e = args
        hid = xb @ lp["moe_w1"][e] + lp["moe_b1"][e]
        gate = jnp.minimum(hid[:, :D_FF], SWIGLU_LIMIT)
        lin = jnp.clip(hid[:, D_FF:], -SWIGLU_LIMIT, SWIGLU_LIMIT)
        act = gate * jax.nn.sigmoid(SWIGLU_ALPHA * gate) * (lin + 1.0)
        return act @ lp["moe_w2"][e] + lp["moe_b2"][e]

    out = lax.map(expert_block, (buf.reshape(n_blocks, MOE_BLOCK, d), block_e)).reshape(-1, d)
    rows = out[dest] * gates.reshape(-1)[order][:, None]
    y = jax.ops.segment_sum(rows, tok, num_segments=n)
    return y.reshape(bsz, t, d)

def trunk_layer(x, state, gla_segments, lp):
    y_mix, new_state = mixer(x, state, gla_segments, lp)
    h = layer_norm(DEEPNORM_ALPHA * x + y_mix, lp["ln1_g"], lp["ln1_b"])
    out = layer_norm(DEEPNORM_ALPHA * h + moe(h, lp), lp["ln2_g"], lp["ln2_b"])
    return out, new_state

def setup_inputs(seed: int = 0) -> dict:
    key = jax.random.key(seed)
    k = jax.random.split(key, 40)
    f32 = jnp.float32

    def nrm(i, shape, scale):
        return jax.random.normal(k[i], shape, f32) * scale

    a0 = jax.random.uniform(k[16], (DEPTH, D_A), f32, 0.9, 0.999)
    return {
        "x_prompt": nrm(0, (BATCH, SEQ, D_MODEL), 1.0),
        "x_sample": nrm(1, (DEC_BATCH, DEC_SEQ, D_MODEL), 1.0),
        "state_conv_a": nrm(2, (DEPTH, DEC_BATCH, CONV_A - 1, D_A), 1.0),
        "state_rglru": nrm(3, (DEPTH, DEC_BATCH, D_A), 0.5),
        "state_conv_b": nrm(4, (DEPTH, DEC_BATCH, CONV_B - 1, D_B), 1.0),
        "state_gla": nrm(5, (DEPTH, DEC_BATCH, N_HEADS_C, DK_C, DV_C), 0.5),
        "meta_tokens": nrm(6, (N_META, D_MODEL), 1.0),
        "ln0_g": 1.0 + nrm(7, (D_MODEL,), 0.05),
        "ln0_b": nrm(8, (D_MODEL,), 0.02),
        "w_in": nrm(9, (DEPTH, D_MODEL, D_IN), D_MODEL ** -0.5),
        "conv_a_w": nrm(10, (DEPTH, CONV_A, D_A), CONV_A ** -0.5),
        "conv_a_b": nrm(11, (DEPTH, D_A), 0.02),
        "w_rg": nrm(12, (DEPTH, N_BLK_A, BLK_A, BLK_A), BLK_A ** -0.5),
        "b_rg": nrm(13, (DEPTH, D_A), 0.02),
        "w_ig": nrm(14, (DEPTH, N_BLK_A, BLK_A, BLK_A), BLK_A ** -0.5),
        "b_ig": nrm(15, (DEPTH, D_A), 0.02),
        "lru_lambda": jnp.log(a0) - jnp.log1p(-a0),
        "conv_b_w": nrm(17, (DEPTH, CONV_B, D_B), CONV_B ** -0.5),
        "conv_b_b": nrm(18, (DEPTH, D_B), 0.02),
        "ln_b_g": 1.0 + nrm(19, (DEPTH, D_B), 0.05),
        "ln_b_b": nrm(20, (DEPTH, D_B), 0.02),
        "w_gate2": nrm(21, (DEPTH, GATE_RANK, D_QK_C), GATE_RANK ** -0.5),
        "b_gate": nrm(22, (DEPTH, D_QK_C), 0.02),
        "gla_norm_g": 1.0 + nrm(23, (DEPTH, DV_C), 0.05),
        "w_out": nrm(24, (DEPTH, D_MIX, D_MODEL), DEEPNORM_BETA * D_MIX ** -0.5),
        "ln1_g": 1.0 + nrm(25, (DEPTH, D_MODEL), 0.05),
        "ln1_b": nrm(26, (DEPTH, D_MODEL), 0.02),
        "router_w": nrm(27, (DEPTH, D_MODEL, N_EXPERTS), D_MODEL ** -0.5),
        "router_b": nrm(28, (DEPTH, N_EXPERTS), 0.01),
        "moe_w1": nrm(29, (DEPTH, N_EXPERTS, D_MODEL, 2 * D_FF), D_MODEL ** -0.5),
        "moe_b1": nrm(30, (DEPTH, N_EXPERTS, 2 * D_FF), 0.02),
        "moe_w2": nrm(31, (DEPTH, N_EXPERTS, D_FF, D_MODEL), DEEPNORM_BETA * D_FF ** -0.5),
        "moe_b2": nrm(32, (DEPTH, N_EXPERTS, D_MODEL), 0.02),
        "ln2_g": 1.0 + nrm(33, (DEPTH, D_MODEL), 0.05),
        "ln2_b": nrm(34, (DEPTH, D_MODEL), 0.02),
    }

def reference(x_prompt, x_sample, state_conv_a, state_rglru, state_conv_b, state_gla, meta_tokens, ln0_g, ln0_b,
              w_in, conv_a_w, conv_a_b, w_rg, b_rg, w_ig, b_ig, lru_lambda, conv_b_w, conv_b_b, ln_b_g, ln_b_b,
              w_gate2, b_gate, gla_norm_g, w_out, ln1_g, ln1_b, router_w, router_b, moe_w1, moe_b1, moe_w2, moe_b2,
              ln2_g, ln2_b):
    dt = x_prompt.dtype
    bp, seq = x_prompt.shape[0], x_prompt.shape[1]
    dseq = x_sample.shape[1]
    meta = jnp.broadcast_to(meta_tokens.astype(dt)[None], (bp, N_META, D_MODEL))
    hp = layer_norm(jnp.concatenate([meta, x_prompt], axis=1), ln0_g, ln0_b)
    hs = layer_norm(x_sample, ln0_g, ln0_b)
    prompt_segments = ((N_META, N_META), (seq, CHUNK_C))
    sample_segments = ((dseq, dseq),)
    zero_state = (jnp.zeros((bp, CONV_A - 1, D_A), dt), jnp.zeros((bp, D_A), dt),
                  jnp.zeros((bp, CONV_B - 1, D_B), dt), jnp.zeros((bp, N_HEADS_C, DK_C, DV_C), dt))
    new_p = ([], [], [], [])
    new_s = ([], [], [], [])
    for l in range(DEPTH):
        lp = {"w_in": w_in[l], "conv_a_w": conv_a_w[l], "conv_a_b": conv_a_b[l], "w_rg": w_rg[l], "b_rg": b_rg[l],
              "w_ig": w_ig[l], "b_ig": b_ig[l], "lru_lambda": lru_lambda[l], "conv_b_w": conv_b_w[l],
              "conv_b_b": conv_b_b[l], "ln_b_g": ln_b_g[l], "ln_b_b": ln_b_b[l], "w_gate2": w_gate2[l],
              "b_gate": b_gate[l], "gla_norm_g": gla_norm_g[l], "w_out": w_out[l], "ln1_g": ln1_g[l],
              "ln1_b": ln1_b[l], "router_w": router_w[l], "router_b": router_b[l], "moe_w1": moe_w1[l],
              "moe_b1": moe_b1[l], "moe_w2": moe_w2[l], "moe_b2": moe_b2[l], "ln2_g": ln2_g[l], "ln2_b": ln2_b[l]}
        hp, st_p = trunk_layer(hp, zero_state, prompt_segments, lp)
        hs, st_s = trunk_layer(hs, (state_conv_a[l], state_rglru[l], state_conv_b[l], state_gla[l]), sample_segments, lp)
        for j in range(4):
            new_p[j].append(st_p[j])
            new_s[j].append(st_s[j])
    return (hp[:, N_META:], hs,
            jnp.stack(new_p[0]), jnp.stack(new_p[1]), jnp.stack(new_p[2]), jnp.stack(new_p[3]),
            jnp.stack(new_s[0]), jnp.stack(new_s[1]), jnp.stack(new_s[2]), jnp.stack(new_s[3]))


_drawn_inputs = setup_inputs


def setup_inputs(seed=0):
    import zlib

    import numpy as np

    out = dict(_drawn_inputs(seed))
    spreads = {}
    factors = {'b_rg': 7.251,
     'b_ig': 6.767,
     'ln_b_b': 8.0,
     'b_gate': 7.171,
     'moe_b1': 8.0,
     'moe_b2': 6.465,
     'ln2_b': 2.854,
     'conv_b_b': 3.956,
     'router_b': 3.558}
    for name, (base, spread) in spreads.items():
        noise = np.random.default_rng([zlib.crc32(name.encode()), seed]).standard_normal(out[name].shape)
        drawn = base * np.exp(spread * noise) if base else spread * noise
        out[name] = __import__('jax').numpy.asarray(drawn.astype(out[name].dtype))
    for name, factor in factors.items():
        out[name] = (out[name] * factor).astype(out[name].dtype)
    return out
```

```python
from contextlib import ExitStack

import concourse.bass as bass
from concourse import mybir
from concourse.alu_op_type import AluOpType as ALU

F32 = mybir.dt.float32
I32 = mybir.dt.int32
U32 = mybir.dt.uint32
ACT = mybir.ActivationFunctionType
AX = mybir.AxisListType

P = 128
D = 1024
KT = D // P
SEQ, META = 256, 16
NSEQ, DSEQ = 8, 4
SAMP = NSEQ * DSEQ
TOUT = SEQ + SAMP
TALL = TOUT + META
T2 = SAMP + META
DA, DB, DC = 384, 256, 384
MA, MB, MC = DA // P, DB // P, DC // P
WA, WB = 4, 31
BLK = 48
NH, DK, DV = 4, 48, 96
DQK = NH * DK
RANK = 16
TAU = 16.0
NE, TOPK = 32, 4
DF = 1024
LIMIT, SALPHA = 7.0, 1.702
ALPHA = 2.0 ** 0.25
EPS = 1e-5
RG_C = 8.0

C_XA, C_GA, C_VB, C_GB = 0, DA, 2 * DA, 2 * DA + DB
C_Q = 2 * DA + 2 * DB
C_K = C_Q + DQK
C_V = C_K + DQK
C_R = C_V + DC
C_Z = C_R + DC
DIN = C_Z + RANK

SLOTS = 12
SLOT = 2048
CAP = 64
PASSES = -(-TOUT // CAP)
PAIRS = NE // 2

JOBS = (["LNC", "X0a", "X0b", "X1a", "X1b", "X2", "SA", "SB", "SS", "Z", "Q0", "G0", "G1", "Q1", "K0", "K1",
         "XA0", "XA1", "XA2", "GB0", "VB0", "GB1", "VB1", "V2", "V0", "RG0", "RG1", "RG2", "IG0", "IG1", "IG2",
         "V1", "R2", "R0", "R1", "KT2", "SC2e", "SC2o", "MU", "GA0", "STM", "KT0", "SC0e", "SC0o", "VAR", "GA1",
         "O0e", "O0o", "KT1", "ST0", "SC1e", "SC1o", "GA2", "O2e", "O2o", "O1e", "O1o", "ST1", "OA", "OB",
         "W00", "W01", "YC0", "YC2", "W10", "W11", "YC1",
         "P00", "P01", "P10", "P11", "P20", "P21",
         "H0a", "H0b", "H1a", "H1b", "H2", "LG", "POS", "GT",
         "Y00", "Y01", "Y10", "Y11", "Y20", "Y21"])
J = {name: n for n, name in enumerate(JOBS)}


ST_OUT = 1 + 2 * NH + 4 + 1 + NSEQ


class Steps:

    def __init__(self, eng, own):
        self.eng, self.own, self.count, self.last = eng, own, {}, None

    def do(self, ins, sem=None):
        if isinstance(sem, tuple):
            ins.then_inc(sem[0], 1)
            self.last = sem
            return
        sem = self.own if sem is None else sem
        ins.then_inc(sem, 1)
        self.count[id(sem)] = self.count.get(id(sem), 0) + 1
        self.last = (sem, self.count[id(sem)])

    def settle(self):
        self.eng.wait_ge(*self.last)

    def then(self, ins, sem=None):
        self.do(ins, sem)
        self.settle()


def build_kernel(nc, x_prompt, x_sample, state_conv_a, state_rglru, state_conv_b, state_gla, meta_tokens, ln0_g, ln0_b,
                 w_in, conv_a_w, conv_a_b, w_rg, b_rg, w_ig, b_ig, lru_lambda, conv_b_w, conv_b_b, ln_b_g, ln_b_b,
                 w_gate2, b_gate, gla_norm_g, w_out, ln1_g, ln1_b, router_w, router_b, moe_w1, moe_b1, moe_w2, moe_b2,
                 ln2_g, ln2_b, y_prompt, y_sample, o_conv_a_p, o_rglru_p, o_conv_b_p, o_gla_p, o_conv_a_s, o_rglru_s,
                 o_conv_b_s, o_gla_s):
    with ExitStack() as ctx:
        def sb(name, shape, dt=F32):
            return ctx.enter_context(nc.sbuf_tensor(name, shape, dt))

        def sem(name):
            return ctx.enter_context(nc.semaphore(name))

        ring = sb("ring", [P, SLOTS * SLOT])
        xt = sb("xt", [P, 3, D])
        lnbc = sb("lnbc", [P, 2, D])
        hT = sb("hT", [P, KT, TALL])
        ident = sb("ident", [P, P])
        ones = sb("ones", [P, P])
        upper = sb("upper", [P, P])
        smask = sb("smask", [SAMP, SAMP])
        sseq = sb("sseq", [SAMP, NSEQ])
        stat = sb("stat", [P, 3, 2, 6])
        mv = sb("mv", [P, 3, 2])
        rst = sb("rst", [P, 3, 2])
        npass_f = sb("npass_f", [P, 8])
        npass = sb("npass", [P, 1], I32)

        W_MIX = 19400
        mix = sb("mix", [P, W_MIX])
        top = {"mixer": 0, "moe": 0}

        def part(phase, *shape):
            n = 1
            for s in shape:
                n *= s
            a = top[phase]
            top[phase] = a + n
            assert top[phase] <= W_MIX, (phase, top[phase])
            v = mix[:, a:a + n]
            if len(shape) == 2:
                v = v.rearrange("p (a b) -> p a b", b=shape[1])
            if len(shape) == 3:
                v = v.rearrange("p (a b c) -> p a b c", b=shape[1], c=shape[2])
            return v

        yT = part("mixer", KT, TOUT)
        colA = part("mixer", MA, 40)
        colB = part("mixer", MB, 34)
        lncol = part("mixer", 16)
        wbd_flat = part("mixer", 2 * MA * DA)
        wbd = wbd_flat.rearrange("p (g k c) -> p g k c", g=2, k=MA)
        o_sb = wbd_flat[:, 0:MC * DC].rearrange("p (t c) -> p t c", t=3)
        r_sb = wbd_flat[:, MC * DC:2 * MC * DC].rearrange("p (t c) -> p t c", t=3)
        tsq = part("mixer", MA, TALL)
        tsq_flat = tsq.rearrange("p a b -> p (a b)")
        cneg = part("mixer", 4, MA)
        uP = part("mixer", MB, WB - 1 + META + SEQ)
        uS = part("mixer", MB, NSEQ, WB - 1 + DSEQ)
        uc = part("mixer", MB, TOUT)
        sgb = part("mixer", MB, TALL)
        brst = part("mixer", TOUT)
        q_sb = part("mixer", 2, TOUT)
        k_sb = part("mixer", 2, TALL)
        gl = part("mixer", 2, TALL)
        G = part("mixer", 2, TALL)
        qc = part("mixer", 2, TOUT)
        kc = part("mixer", 2, TOUT)
        qm = part("mixer", 2, NSEQ * (SAMP + DSEQ))
        vm_at = top["mixer"] - 2 * TOUT * 2 - 2 * NSEQ * (SAMP + DSEQ)
        vm = mix[:, vm_at:vm_at + 2 * NSEQ * DV].rearrange("p (q s e) -> p q s e", q=2, s=NSEQ)
        kT_sb = part("mixer", 3, 2, P)
        v_sb = part("mixer", 3, DC)
        sc = part("mixer", NH, P)
        sc2 = part("mixer", NH, SAMP)
        S0 = part("mixer", 2, NSEQ, DV)
        Sp = part("mixer", 2, DV)
        e_flat = part("mixer", 4 * TALL)
        E = [e_flat[:, n * 2 * TALL:(n + 1) * 2 * TALL].rearrange("p (a b) -> p a b", a=2) for n in range(2)]
        packA = e_flat[0:40, 0:DA]
        packB = e_flat[0:34, DA:DA + DB]
        packS = e_flat[0:120, DA + DB:DA + 3 * DB].rearrange("p (a b) -> p a b", a=2)
        wg2 = part("mixer", DQK + 16)
        bg = part("mixer", 2)
        gcol = part("mixer", 2, 8)
        eg = part("mixer", 2, 2 + NSEQ)
        gnorm = part("mixer", DV)
        rsq = part("mixer", 3, NH)
        rmask = part("mixer", TALL)
        zT = part("mixer", TALL)
        lnrow = part("mixer", P)
        packOA = e_flat[0:36, 0:DA]
        packOB = e_flat[0:62, DA:DA + DB]
        oaT = e_flat[:, DA + DB:DA + DB + MA * 36].rearrange("p (a b) -> p a b", a=MA)
        obT = e_flat[:, DA + DB + MA * 36:DA + DB + MA * 36 + MB * 62].rearrange("p (a b) -> p a b", a=MB)
        at = [10 * SLOT]

        def in_ring(*shape):
            n = 1
            for s in shape:
                n *= s
            a = at[0]
            at[0] += n
            assert at[0] <= SLOTS * SLOT
            v = ring[:, a:a + n]
            if len(shape) == 2:
                return v.rearrange("p (a b) -> p a b", b=shape[1])
            return v.rearrange("p (a b c) -> p a b c", b=shape[1], c=shape[2])

        xaP = in_ring(MA, WA - 1 + META + SEQ)
        xaS = in_ring(MA, NSEQ, WA - 1 + DSEQ)
        xc = in_ring(MA, TALL)
        ra = in_ring(MA, TALL)
        iu = in_ring(MA, TALL)
        blocks = [("z", C_Z, RANK), ("qk", C_Q, 2 * DQK + 16), ("xa", C_XA, DA), ("vbgb", C_VB, 2 * DB),
                  ("vr", C_V, 2 * DC), ("ga", C_GA, DA)]
        win, off = {}, 0
        for name, c0, n in blocks:
            win[name] = ring[:, off:off + KT * n].rearrange("p (k n) -> p k n", n=n)
            off += KT * n
        assert off <= 10 * SLOT
        wout = ring[:, 8 * SLOT:12 * SLOT].rearrange("p (k n) -> p k n", n=D)

        Y = part("moe", 3, D)
        xT = part("moe", 2, KT * CAP)
        xTk = xT.rearrange("p a (k c) -> p a k c", c=CAP)
        pick = part("moe", 3, CAP)
        put = part("moe", 3, 2 * CAP)
        putT = part("moe", 3 * P)
        eout = part("moe", 2, 512)
        g1 = part("moe", 512)
        l1 = part("moe", 512)
        sg = part("moe", 512)
        act_sb = part("moe", 512)
        actT = part("moe", 4, P)
        b1_sb = part("moe", 2 * DF)
        bsel = part("moe", 2, CAP)
        posm = part("moe", 3, PASSES * NE + 1)
        gates = part("moe", 3, NE)
        selx = part("moe", NE + 1)
        b2_sb = part("moe", D)
        gT = part("moe", 3 * P)
        wr = part("moe", KT, NE)
        rb = part("moe", NE)
        lg = part("moe", 3, NE)
        v8 = part("moe", 3, 8)
        i8 = part("moe", 3 * 8)
        i8u = i8.bitcast(U32).rearrange("p (a b) -> p a b", a=3)
        i8f = part("moe", 3, TOPK)
        e4 = part("moe", 3, TOPK)
        sm = part("moe", 3, 4)
        oh = part("moe", 3, TOPK * NE)
        ohg = part("moe", 3, TOPK * NE)
        M = part("moe", 3, NE)
        valid = part("moe", 3)
        io32 = part("moe", NE)
        io64 = part("moe", CAP)
        iraw = part("moe", CAP).bitcast(I32)
        nmx = part("moe", 4)

        bank = [ctx.enter_context(nc.psum_tensor(f"bank{n}", [P, 512], F32)) for n in range(8)]

        bank_full = sem("bank_full")
        bank_read = [sem(f"bank_read{n}") for n in range(8)]
        dve_step, act_step, pool_step = sem("dve_step"), sem("act_step"), sem("pool_step")
        zeroed_x2 = sem("zeroed_x2")
        consts_ready = sem("consts_ready")
        ld_x = [sem(f"ld_x{t}") for t in range(3)]
        ld_ln = sem("ld_ln")
        ld_lncol = sem("ld_lncol")
        ld_packA, ld_packB, ld_packS = sem("ld_packA"), sem("ld_packB"), sem("ld_packS")
        ld_gate = sem("ld_gate")
        ld_wbd, ld_S0 = sem("ld_wbd"), sem("ld_S0")
        ld_win = {name: sem(f"ld_win_{name}") for name, _, _ in blocks}
        ld_wout = [sem("ld_wout0"), sem("ld_wout1")]
        ld_moe = sem("ld_moe")
        w_full = [sem(f"w_full{s}") for s in range(SLOTS)]
        w_used = sem("w_used")
        var_ready, std_ready = sem("var_ready"), sem("std_ready")
        ln0_stats, xhat_ready, h0_ready = sem("ln0_stats"), sem("xhat_ready"), sem("h0_ready")
        cleared = sem("cleared")
        colA_moved = sem("colA_moved")
        softplus_done, G_ready = sem("softplus_done"), sem("G_ready")
        exp_ready, exp_used = sem("exp_ready"), sem("exp_used")
        qk_decayed = sem("qk_decayed")
        eg_ready = sem("eg_ready")
        xc_ready, lam_in, lam_exp, lam_ready = sem("xc_ready"), sem("lam_in"), sem("lam_exp"), sem("lam_ready")
        rg_root_in, rg_root = sem("rg_root_in"), sem("rg_root")
        b_root, o_root_in, o_root = sem("b_root"), sem("o_root_in"), sem("o_root")
        a_ready, h_ready = sem("a_ready"), sem("h_ready")
        uc_ready, sq_ready, dn_ready, yb_ready = sem("uc_ready"), sem("sq_ready"), sem("dn_ready"), sem("yb_ready")
        vm_ready, ya_ready, o_ready = sem("vm_ready"), sem("ya_ready"), sem("o_ready")
        outcols_ready = sem("outcols_ready")
        ln1_stats, xhat1_ready, h1_ready = sem("ln1_stats"), sem("xhat1_ready"), sem("h1_ready")
        top_ready, top_exp = sem("top_ready"), sem("top_exp")
        mask_ready, gates_ready, routed = sem("mask_ready"), sem("gates_ready"), sem("routed")
        moe_consts = sem("moe_consts")
        st_out, out_stored = sem("st_out"), sem("out_stored")
        pick_ready, bsel_ready, put_ready = sem("pick_ready"), sem("bsel_ready"), sem("put_ready")
        gather_full, xT_ready = sem("gather_full"), sem("xT_ready")
        g1_ready, l1_ready, t_done = sem("g1_ready"), sem("l1_ready"), sem("t_done")
        sg_ready, act_ready = sem("sg_ready"), sem("act_ready")
        actT_full, actT_ready = sem("actT_full"), sem("actT_ready")
        putT_full, putT_ready = sem("putT_full"), sem("putT_ready")
        out_ready = sem("out_ready")
        comb_full, y_added = sem("comb_full"), sem("y_added")
        y_scaled, ln2_stats, y_hat, y_done = sem("y_scaled"), sem("ln2_stats"), sem("y_hat"), sem("y_done")

        def filled(eng, job):
            eng.wait_ge(bank_full, J[job] + 1)

        def copied(eng, job):
            eng.wait_ge(bank_read[J[job] % 8], J[job] // 8 + 1)

        def bk(job):
            return bank[J[job] % 8]

        def read_of(job):
            return bank_read[J[job] % 8], J[job] // 8 + 1

        blk = nc.Block()
        block = ctx.enter_context(blk)

        rows = [P, P, SAMP]
        rows0 = [P, P, T2]
        cols = [(0, P), (P, 2 * P), (2 * P, 2 * P + SAMP)]

        def head(h):
            return 64 * (h % 2), h // 2

        def w1_piece(e, s):
            return moe_w1[0, bass.ds(e, 1), s * P:(s + 1) * P, :].rearrange("a p c -> p (a c)")

        def w2_piece(e, s):
            r = (s - 8) * 2 * P
            return moe_w2[0, bass.ds(e, 1), r:r + 2 * P, :].rearrange("a (t p) c -> p (a t) c", p=P)

        @block.sync
        def _(sp):
            sp.dma_start(xt[:, 0, :], x_prompt[0, 0:P, :]).then_inc(ld_x[0], 16)
            sp.dma_start(xt[:, 1, :], x_prompt[0, P:2 * P, :]).then_inc(ld_x[1], 16)
            sp.wait_ge(zeroed_x2, 1)
            sp.dma_start(xt[0:SAMP, 2, :], x_sample.rearrange("b t c -> (b t) c")).then_inc(ld_x[2], 16)
            sp.dma_start(xt[SAMP:T2, 2, :], meta_tokens).then_inc(ld_x[2], 16)
            for name, c0, n in blocks:
                sp.dma_start(win[name], w_in[0, :, c0:c0 + n].rearrange("(k p) n -> p k n", p=P)).then_inc(ld_win[name], 16)
            filled(sp, "GA2")
            sp.dma_start(wout[:, 0:4, :], w_out[0, 0:4 * P, :].rearrange("(k p) n -> p k n", p=P)).then_inc(ld_wout[0], 16)
            sp.wait_ge(ya_ready, MA)
            sp.wait_ge(outcols_ready, 2)
            sp.dma_start(wout[:, 4:8, :], w_out[0, 4 * P:8 * P, :].rearrange("(k p) n -> p k n", p=P)).then_inc(ld_wout[1], 16)
            for s in range(8):
                sp.dma_start(ring[:, s * SLOT:(s + 1) * SLOT], moe_w1[0, 0, s * P:(s + 1) * P, :]).then_inc(w_full[s], 16)
            filled(sp, "P21")
            for s in range(8, SLOTS):
                sp.dma_start(ring[:, s * SLOT:(s + 1) * SLOT].rearrange("p (t c) -> p t c", t=2),
                             moe_w2[0, 0, (s - 8) * 2 * P:(s - 7) * 2 * P, :].rearrange("(t p) c -> p t c", p=P)
                             ).then_inc(w_full[s], 16)

            def load_expert(e, n):
                e = sp.snap(e)
                for s in range(SLOTS):
                    src = w1_piece(e, s) if s < 8 else w2_piece(e, s)
                    dst = ring[:, s * SLOT:(s + 1) * SLOT]
                    if s >= 8:
                        dst = dst.rearrange("p (t c) -> p t c", t=2)
                    sp.wait_ge(w_used, SLOTS * (n - 1) + s + 1)
                    sp.dma_start(dst, src).then_inc(w_full[s], 16)

            load_expert(1, 1)
            with sp.Fori(1, PAIRS) as p:
                load_expert(2 * p, 2 * p)
                load_expert(2 * p + 1, 2 * p + 1)
            sp.wait_ge(routed, 2)
            n_pass = sp.value_load(npass[0:1, 0:1], min_val=1, max_val=PASSES)
            with sp.If(n_pass > 1):
                with sp.Fori(1, n_pass) as r:
                    with sp.Fori(0, PAIRS) as p:
                        load_expert(2 * p, NE * r + 2 * p)
                        load_expert(2 * p + 1, NE * r + 2 * p + 1)
            for t in range(3):
                sp.wait_ge(y_done, t + 1)
                dst = y_prompt[0, t * P:(t + 1) * P, :] if t < 2 else y_sample.rearrange("b t c -> (b t) c")
                sp.dma_start(dst, Y[0:rows[t], t, :]).then_inc(out_stored, 16)
            sp.wait_ge(out_stored, 48)
            sp.wait_ge(st_out, 16 * ST_OUT)

        @block.gpsimd
        def _(pool):
            st = Steps(pool, pool_step)
            st.do(pool.memset(xt[:, 2, :], 0.0), zeroed_x2)
            st.do(pool.memset(ident[:, :], 0.0))
            st.do(pool.memset(ones[:, :], 1.0))
            st.do(pool.memset(wbd_flat[:, :], 0.0))
            st.then(pool.memset(wg2[:, :], 0.0))
            st.then(pool.affine_select(out=ident[:, :], in_=ident[:, :], compare_op=ALU.not_equal, fill=1.0, base=0,
                                       pattern=[[-1, P]], channel_multiplier=1), consts_ready)
            for g, w in enumerate((w_rg, w_ig)):
                for h in range(NH * 2):
                    r0 = h * BLK
                    while r0 < (h + 1) * BLK:
                        r1 = min((h + 1) * BLK, (r0 // P + 1) * P)
                        pool.dma_start(wbd[r0 % P:r0 % P + r1 - r0, g, r0 // P, h * BLK:(h + 1) * BLK],
                                       w[0, h, r0 - h * BLK:r1 - h * BLK, :]).then_inc(ld_wbd, 16)
                        r0 = r1
            st.do(pool.memset(bg[:, :], 0.0), cleared)
            st.do(pool.memset(S0[:, :, :, :], 0.0), cleared)
            st.do(pool.memset(xaP[:, :, 0:WA - 1], 0.0), cleared)
            st.do(pool.memset(uP[:, :, 0:WB - 1], 0.0), cleared)
            st.do(pool.memset(qm[:, :, :], 0.0), cleared)
            st.then(pool.memset(rmask[:, :], 1.0), cleared)
            pool.dma_start(wg2[0:RANK, 0:DQK], w_gate2[0]).then_inc(ld_gate, 16)
            for h in range(NH):
                b, p = head(h)
                pool.dma_start(bg[b:b + DK, p:p + 1], b_gate[0, h * DK:(h + 1) * DK].rearrange("(a b) -> a b", b=1)
                               ).then_inc(ld_gate, 16)
                pool.dma_start(S0[b:b + DK, p, :, :], state_gla[0, :, h, :, :].rearrange("s d e -> d s e")
                               ).then_inc(ld_S0, 16)
            pool.dma_start(gnorm[:, :], gla_norm_g[0:1, :].to_broadcast([P, DV])).then_inc(ld_gate, 16)
            st.do(pool.memset(rmask[:, 0:2 * P:P], 0.0), cleared)
            st.do(pool.memset(rmask[:, 2 * P:TOUT:DSEQ], 0.0), cleared)
            st.do(pool.memset(rmask[:, TOUT:TOUT + 1], 0.0), cleared)
            st.do(pool.memset(upper[:, :], 1.0))
            st.do(pool.memset(smask[:, :], 1.0))
            st.then(pool.memset(sseq[:, :], 1.0))
            st.do(pool.affine_select(out=upper[:, :], in_=upper[:, :], compare_op=ALU.is_ge, fill=0.0, base=0,
                                     pattern=[[1, P]], channel_multiplier=-1), consts_ready)
            v = smask[:, :].rearrange("p (a b) -> p a b", b=DSEQ)
            st.then(pool.affine_select(out=v, in_=v, compare_op=ALU.is_ge, fill=0.0, base=0,
                                       pattern=[[DSEQ, NSEQ], [1, DSEQ]], channel_multiplier=-1))
            st.do(pool.affine_select(out=v, in_=v, compare_op=ALU.is_ge, fill=0.0, base=0,
                                     pattern=[[-DSEQ, NSEQ], [0, DSEQ]], channel_multiplier=1), consts_ready)
            st.then(pool.affine_select(out=sseq[:, :], in_=sseq[:, :], compare_op=ALU.is_ge, fill=0.0, base=0,
                                       pattern=[[-DSEQ, NSEQ]], channel_multiplier=1))
            st.then(pool.affine_select(out=sseq[:, :], in_=sseq[:, :], compare_op=ALU.is_ge, fill=0.0, base=DSEQ - 1,
                                       pattern=[[DSEQ, NSEQ]], channel_multiplier=-1), consts_ready)
            pool.wait_ge(ld_ln, 32)
            for t in range(3):
                pool.wait_ge(xhat_ready, t + 1)
                for half in ("X%da" % t, "X%db" % t) if t < 2 else ("X2",):
                    filled(pool, half)
                n = rows0[t]
                st.then(pool.tensor_tensor(xt[0:n, t, :], xt[0:n, t, :], lnbc[0:n, 0, :], ALU.mult))
                st.do(pool.tensor_tensor(xt[0:n, t, :], xt[0:n, t, :], lnbc[0:n, 1, :], ALU.add), h0_ready)
            copied(pool, "SA")
            st.do(pool.tensor_copy(xaS[:, :, :, 0:WA - 1], colA[:, :, 16:40].rearrange("p m (s k) -> p m s k", k=WA - 1)),
                  colA_moved)
            pool.wait_ge(h_ready, 1)
            pool.wait_ge(qk_decayed, 4)
            st.do(pool.tensor_copy(oaT[:, :, 0:1], xc[:, :, META + SEQ - 1:META + SEQ]))
            st.do(pool.tensor_copy(oaT[:, :, 1:1 + NSEQ], xc[:, :, META + SEQ + DSEQ - 1:TALL:DSEQ]))
            st.do(pool.tensor_copy(oaT[:, :, 9:12], xaP[:, :, META + SEQ:META + SEQ + WA - 1]))
            st.do(pool.tensor_copy(oaT[:, :, 12:36].rearrange("p m (s k) -> p m s k", k=WA - 1), xaS[:, :, :, DSEQ:DSEQ + WA - 1]),
                  outcols_ready)
            st.do(pool.tensor_copy(obT[:, :, 0:WB - 1], uP[:, :, META + SEQ:META + SEQ + WB - 1]))
            st.do(pool.tensor_copy(obT[:, :, WB - 1:62].rearrange("p m (s k) -> p m s k", k=DSEQ), uS[:, :, :, WB - 1:WB - 1 + DSEQ]),
                  outcols_ready)
            pool.dma_start(o_conv_b_s[0, :, 0:WB - 1 - DSEQ, :], state_conv_b[0, :, DSEQ:WB - 1, :]).then_inc(st_out, 16)
            copied(pool, "ST1")
            copied(pool, "W11")
            for h in range(NH):
                b, p = head(h)
                pool.dma_start(o_gla_p[0, 0, h, :, :], Sp[b:b + DK, p, :]).then_inc(st_out, 16)
                pool.dma_start(o_gla_s[0, :, h, :, :].rearrange("s d e -> d s e"), S0[b:b + DK, p, :, :]).then_inc(st_out, 16)
            copied(pool, "OA")
            pool.dma_start(o_rglru_p[0, :, :], packOA[0:1, :]).then_inc(st_out, 16)
            pool.dma_start(o_rglru_s[0, :, :], packOA[1:1 + NSEQ, :]).then_inc(st_out, 16)
            pool.dma_start(o_conv_a_p[0, 0, :, :], packOA[9:12, :]).then_inc(st_out, 16)
            pool.dma_start(o_conv_a_s[0].rearrange("s k c -> (s k) c"), packOA[12:36, :]).then_inc(st_out, 16)
            copied(pool, "OB")
            pool.dma_start(o_conv_b_p[0, 0, :, :], packOB[0:WB - 1, :]).then_inc(st_out, 16)
            for n in range(NSEQ):
                r = WB - 1 + n * DSEQ
                pool.dma_start(o_conv_b_s[0, n, WB - 1 - DSEQ:WB - 1, :], packOB[r:r + DSEQ, :]).then_inc(st_out, 16)
            pool.wait_ge(st_out, 16 * ST_OUT)
            filled(pool, "P21")
            st.do(pool.memset(posm[:, :, PASSES * NE:PASSES * NE + 1], -1.0), moe_consts)
            st.do(pool.memset(lg[:, 2, :], 0.0), moe_consts)
            st.do(pool.memset(b1_sb[:, :], 0.0), moe_consts)
            st.then(pool.memset(valid[:, :], 1.0))
            st.then(pool.memset(valid[:, 2:3], 0.0))
            st.do(pool.memset(valid[0:SAMP, 2:3], 1.0), moe_consts)
            st.then(pool.iota(iraw[:, 0:CAP], pattern=[[1, CAP]], base=0, channel_multiplier=0))
            st.do(pool.tensor_copy(io64[:, :], iraw[:, 0:CAP]), moe_consts)
            st.do(pool.tensor_copy(io32[:, :], iraw[:, 0:NE]), moe_consts)
            st.do(pool.tensor_copy(selx[:, 0:NE], ident[:, 0:NE]), moe_consts)
            st.do(pool.tensor_copy(selx[:, NE:NE + 1], ident[:, 0:1]), moe_consts)

        @block.scalar
        def _(act):
            st = Steps(act, act_step)

            def root(n, t, k):
                act.wait_ge(var_ready, 3 * k + t + 1)
                st.do(act.activation(rst[0:n, t, 0:1], rst[0:n, t, 0:1], ACT.Sqrt), std_ready)

            act.dma_start(lnrow[0:8, :], ln0_g.rearrange("(k p) -> k p", p=P)).then_inc(ld_lncol, 16)
            act.dma_start(lnrow[8:16, :], ln0_b.rearrange("(k p) -> k p", p=P)).then_inc(ld_lncol, 16)
            act.dma_start(packA[0:4, :], conv_a_w[0]).then_inc(ld_packA, 16)
            for n, a in enumerate((conv_a_b, b_rg, b_ig, lru_lambda)):
                act.dma_start(packA[4 + n:5 + n, :], a).then_inc(ld_packA, 16)
            act.dma_start(packA[8:16, :], state_rglru[0]).then_inc(ld_packA, 16)
            act.dma_start(packA[16:40, :], state_conv_a[0].rearrange("s k c -> (s k) c")).then_inc(ld_packA, 16)
            act.dma_start(packB[0:WB, :], conv_b_w[0]).then_inc(ld_packB, 16)
            for n, a in enumerate((conv_b_b, ln_b_g, ln_b_b)):
                act.dma_start(packB[WB + n:WB + n + 1, :], a).then_inc(ld_packB, 16)
            act.dma_start(packS, state_conv_b[0].rearrange("(a s) k c -> (s k) a c", a=2)).then_inc(ld_packS, 16)
            act.dma_start(lnbc[:, 0, :], ln0_g.rearrange("(a c) -> a c", a=1).to_broadcast([P, D])).then_inc(ld_ln, 16)
            act.dma_start(lnbc[:, 1, :], ln0_b.rearrange("(a c) -> a c", a=1).to_broadcast([P, D])).then_inc(ld_ln, 16)
            for t in range(3):
                n = rows0[t]
                root(n, t, 0)
                act.wait_ge(ln0_stats, t + 1)
                st.do(act.activation(xt[0:n, t, :], xt[0:n, t, :], ACT.Identity, bias=rst[0:n, t, 1:2], scale=rst[0:n, t, 0:1]),
                      xhat_ready)
            copied(act, "LNC")
            for job, t, k0 in (("X0a", 0, 0), ("X1a", 1, 0)):
                filled(act, job)
                for k in range(4):
                    st.do(act.activation(hT[:, k0 + k, cols[t][0]:cols[t][1]], bk(job)[:, k * P:(k + 1) * P], ACT.Identity,
                                         bias=lncol[:, 8 + k0 + k:9 + k0 + k], scale=lncol[:, k0 + k:k0 + k + 1]),
                          read_of(job) if k == 3 else None)
            act.wait_ge(cleared, 9)
            filled(act, "SS")
            v = bk("SS")[:, 0:480].rearrange("p (a m s k) -> p a m s k", a=2, m=MB, k=WB - 1)
            for n in range(4):
                a, m = divmod(n, 2)
                st.do(act.activation(uS[:, m, 4 * a:4 * a + 4, 0:WB - 1], v[:, a, m, :, :], ACT.Copy),
                      read_of("SS") if n == 3 else None)
            filled(act, "Z")
            st.do(act.activation(zT[0:RANK, :], bk("Z")[0:RANK, 0:TALL], ACT.Copy), read_of("Z"))
            filled(act, "Q0")
            st.do(act.activation(q_sb[:, 0, :], bk("Q0")[:, 0:TOUT], ACT.Copy, scale=DK ** -0.5), read_of("Q0"))
            copied(act, "G0")
            copied(act, "G1")
            st.then(act.activation(E[0], gl, ACT.Abs))
            st.then(act.activation(E[0], E[0], ACT.Exp, scale=-1.0))
            st.do(act.activation(E[0], E[0], ACT.Ln, bias=1.0), softplus_done)
            act.wait_ge(lam_in, 1)
            st.then(act.activation(cneg[:, 2, :], cneg[:, 2, :], ACT.Exp, scale=-1.0))
            st.do(act.activation(cneg[:, 2, :], cneg[:, 2, :], ACT.Ln, bias=1.0), lam_exp)
            filled(act, "Q1")
            st.do(act.activation(q_sb[:, 1, :], bk("Q1")[:, 0:TOUT], ACT.Copy, scale=DK ** -0.5), read_of("Q1"))
            for p in range(2):
                filled(act, f"K{p}")
                st.do(act.activation(k_sb[:, p, :], bk(f"K{p}")[:, 0:TALL], ACT.Copy), read_of(f"K{p}"))
            for m in range(MA):
                b = bk(f"XA{m}")
                filled(act, f"XA{m}")
                st.do(act.activation(xaP[:, m, WA - 1:WA - 1 + META], b[:, TOUT:TALL], ACT.Copy))
                st.do(act.activation(xaP[:, m, WA - 1 + META:], b[:, 0:SEQ], ACT.Copy))
                st.do(act.activation(xaS[:, m, :, WA - 1:], b[:, SEQ:TOUT].rearrange("p (s t) -> p s t", t=DSEQ), ACT.Copy),
                      read_of(f"XA{m}"))
            act.wait_ge(G_ready, 1)
            it = 1.0 / TAU

            def exps(e, sign, biased, bias0, whole):
                for p in range(2):
                    for n, (c0, c1) in enumerate(biased):
                        st.do(act.activation(e[:, p, c0:c1], G[:, p, c0:c1], ACT.Exp, bias=gcol[:, p, bias0 + n:bias0 + n + 1],
                                             scale=sign * it))
                st.do(act.activation(e[:, :, whole[0]:whole[1]], G[:, :, whole[0]:whole[1]] if whole[2] is None else whole[2],
                                     ACT.Exp, scale=sign * it if whole[2] is None else it), exp_ready)

            exps(E[0], 1.0, cols[0:2], 0, (SEQ, TOUT, None))
            exps(E[1], -1.0, cols[0:2], 2, (SEQ, TOUT, None))
            act.wait_ge(exp_used, 1)
            st.do(act.activation(E[0][:, :, 0:TOUT], G[:, :, 0:TOUT], ACT.Exp, scale=it), exp_ready)
            st.do(act.activation(eg[:, :, 0:2], G[:, :, P - 1:2 * P:P], ACT.Exp, scale=it))
            st.do(act.activation(eg[:, :, 2:], G[:, :, SEQ + DSEQ - 1:TOUT:DSEQ], ACT.Exp, scale=it), eg_ready)
            act.wait_ge(exp_used, 2)
            exps(E[1], -1.0, cols[0:2] + [(TOUT, TALL)], 4, (SEQ, TOUT, gl[:, :, SEQ:TOUT]))
            for m in range(MB):
                filled(act, f"GB{m}")
                st.do(act.activation(sgb[:, m, :], bk(f"GB{m}")[:, 0:TALL], ACT.Sigmoid), read_of(f"GB{m}"))
            filled(act, "V2")
            st.do(act.activation(v_sb[0:T2, 2, :], bk("V2")[0:T2, 0:DC], ACT.Copy), read_of("V2"))
            filled(act, "V0")
            st.do(act.activation(v_sb[:, 0, :], bk("V0")[:, 0:DC], ACT.Copy), read_of("V0"))
            for g, dst in (("RG", ra), ("IG", iu)):
                for m in range(MA):
                    filled(act, f"{g}{m}")
                    c = 5 if g == "RG" else 6
                    st.do(act.activation(dst[:, m, :], bk(f"{g}{m}")[:, 0:TALL], ACT.Sigmoid, bias=colA[:, m, c:c + 1]),
                          read_of(f"{g}{m}"))
            filled(act, "V1")
            st.do(act.activation(v_sb[:, 1, :], bk("V1")[:, 0:DC], ACT.Copy), read_of("V1"))
            act.wait_ge(lam_ready, 1)
            st.settle()
            for m in range(MA):
                st.do(act.activation(tsq[:, m, :], ra[:, m, :], ACT.Tanh, scale=cneg[:, 1, m:m + 1]))
            st.settle()
            for m in range(MA):
                st.do(act.activation(ra[:, m, :], ra[:, m, :], ACT.Exp, scale=cneg[:, 0, m:m + 1]), a_ready)
            act.wait_ge(rg_root_in, 1)
            st.do(act.activation(tsq[:, :, :], tsq[:, :, :], ACT.Sqrt), rg_root)
            for t in (2, 0, 1):
                filled(act, f"R{t}")
                st.do(act.activation(r_sb[0:rows[t], t, :], bk(f"R{t}")[0:rows[t], 0:DC], ACT.Silu), read_of(f"R{t}"))
            copied(act, "MU")
            st.do(act.activation(sgb[:, :, 0:TOUT], uc[:, :, :], ACT.Square), sq_ready)

            def gelu(m):
                filled(act, f"GA{m}")
                st.do(act.activation(yT[:, m, :], bk(f"GA{m}")[:, 0:TOUT], ACT.Gelu_apprx_tanh), read_of(f"GA{m}"))

            def transposed_o(t):
                filled(act, f"YC{t}")
                st.do(act.activation(yT[:, MA + MB:, cols[t][0]:cols[t][1]],
                                     bk(f"YC{t}")[:, 0:MC * P].rearrange("p (k c) -> p k c", c=P)[:, :, 0:rows[t]], ACT.Copy),
                      read_of(f"YC{t}"))

            for m in range(MA):
                gelu(m)
            copied(act, "VAR")
            st.do(act.activation(brst[:, :], brst[:, :], ACT.Sqrt), b_root)
            act.wait_ge(o_root_in, 1)
            st.do(act.activation(rsq[:, :, :], rsq[:, :, :], ACT.Sqrt), o_root)
            act.wait_ge(dn_ready, 1)
            for m in range(MB):
                st.do(act.activation(yT[:, MA + m, :], uc[:, m, :], ACT.Silu, scale=colB[:, m, WB + 1:WB + 2],
                                     bias=colB[:, m, WB + 2:WB + 3]), yb_ready)
            for job, dst, n, w in (("OA", packOA, 36, DA), ("OB", packOB, 62, DB)):
                filled(act, job)
                st.do(act.activation(dst, bk(job)[0:n, 0:w], ACT.Copy), read_of(job))
            for t in (0, 2, 1):
                transposed_o(t)
            act.wait_ge(h0_ready, 3)
            act.dma_start(lnbc[:, 0, :], ln1_g.to_broadcast([P, D])).then_inc(ld_ln, 16)
            act.dma_start(lnbc[:, 1, :], ln1_b.to_broadcast([P, D])).then_inc(ld_ln, 16)
            for t in range(3):
                n = rows[t]
                root(n, t, 1)
                act.wait_ge(ln1_stats, t + 1)
                st.do(act.activation(xt[0:n, t, :], xt[0:n, t, :], ACT.Identity, bias=rst[0:n, t, 1:2], scale=rst[0:n, t, 0:1]),
                      xhat1_ready)
            act.wait_ge(moe_consts, 8)
            act.dma_start(wr[:, :, :], router_w[0].rearrange("(k p) e -> p k e", p=P)).then_inc(ld_moe, 16)
            act.dma_start(rb[:, :], router_b.to_broadcast([P, NE])).then_inc(ld_moe, 16)
            act.dma_start(b2_sb[0:NE, :], moe_b2[0]).then_inc(ld_moe, 16)
            act.dma_start(b1_sb[0:NE, :], moe_b1[0]).then_inc(ld_moe, 16)
            for job, t, k0, nk in (("H0a", 0, 0, 4), ("H0b", 0, 4, 4), ("H1a", 1, 0, 4), ("H1b", 1, 4, 4), ("H2", 2, 0, 8)):
                filled(act, job)
                w = rows[t]
                st.do(act.activation(hT[:, k0:k0 + nk, cols[t][0]:cols[t][1]],
                                     bk(job)[:, 0:nk * w].rearrange("p (k c) -> p k c", c=w), ACT.Copy), read_of(job))
            act.wait_ge(h1_ready, 3)
            act.dma_start(lnbc[:, 0, :], ln2_g.to_broadcast([P, D])).then_inc(ld_ln, 16)
            act.dma_start(lnbc[:, 1, :], ln2_b.to_broadcast([P, D])).then_inc(ld_ln, 16)
            act.wait_ge(top_ready, 1)
            for t in range(3):
                st.do(act.activation(e4[:, t, :], v8[:, t, 0:TOPK], ACT.Exp, bias=sm[:, t, 0:1]), top_exp)
            filled(act, "GT")
            st.do(act.activation(gT[0:NE, :], bk("GT")[0:NE, 0:3 * P], ACT.Copy), read_of("GT"))
            for t in range(3):
                for c in range(2):
                    job = f"Y{t}{c}"
                    filled(act, job)
                    st.do(act.activation(Y[0:rows[t], t, c * 512:(c + 1) * 512], bk(job)[0:rows[t], :], ACT.Copy), read_of(job))
            act.wait_ge(routed, 2)
            n_pass = act.value_load(npass[0:1, 0:1], min_val=1, max_val=PASSES)
            with act.Fori(0, n_pass) as r:
                with act.Fori(0, PAIRS) as p:
                    pi = r * PAIRS + p
                    for j in range(2):
                        n = 2 * pi + j
                        act.wait_ge(g1_ready, n + 1)
                        act.activation(sg[:, :], g1[:, :], ACT.Sigmoid, scale=SALPHA).then_inc(sg_ready, 1)
                        if j == 1:
                            act.wait_ge(putT_full, pi + 1)
                            act.activation(putT[:, :], bank[5][:, 0:3 * P], ACT.Copy).then_inc(putT_ready, 1)
                        act.wait_ge(actT_full, n + 1)
                        act.activation(actT[:, :, :], bank[3][:, :].rearrange("p (k c) -> p k c", c=P), ACT.Copy
                                       ).then_inc(actT_ready, 1)
                        act.wait_ge(w_used, SLOTS * n + SLOTS)
                        for h in range(2):
                            act.activation(eout[64 * j:64 * j + 64, h, :], bank[4][64 * h:64 * h + 64, :], ACT.Copy
                                           ).then_inc(out_ready, 1)
            for t in range(3):
                n = rows[t]
                root(n, t, 2)
                act.wait_ge(ln2_stats, t + 1)
                act.activation(Y[0:n, t, :], Y[0:n, t, :], ACT.Identity, bias=rst[0:n, t, 1:2], scale=rst[0:n, t, 0:1]
                               ).then_inc(y_hat, 1)

        @block.vector
        def _(dve):
            st = Steps(dve, dve_step)

            def row_stats(src, t, n, signal):
                for c in range(2):
                    st.do(dve.bn_stats(stat[0:n, t, c, :], src[0:n, t, c * 512:(c + 1) * 512]))
                st.settle()
                st.then(dve.bn_aggr(mv[0:n, t, :], stat[0:n, t, :, :].rearrange("p a b -> p (a b)")))
                st.do(dve.tensor_scalar(rst[0:n, t, 0:1], mv[0:n, t, 1:2], EPS, None, ALU.add), var_ready)
                dve.wait_ge(std_ready, st.count[id(var_ready)])
                st.then(dve.reciprocal(rst[0:n, t, 0:1], rst[0:n, t, 0:1]))
                st.do(dve.scalar_tensor_tensor(rst[0:n, t, 1:2], mv[0:n, t, 0:1], -1.0, rst[0:n, t, 0:1], ALU.mult, ALU.mult),
                      signal)

            st.do(dve.memset(rsq[:, :, :], 1.0))
            for t in range(3):
                dve.wait_ge(ld_x[t], 16 if t < 2 else 32)
                row_stats(xt, t, rows0[t], ln0_stats)
            filled(dve, "LNC")
            st.then(dve.tensor_copy(lncol[:, :], bk("LNC")[:, 0:16]), read_of("LNC"))

            def scaled(job, t, k0, nk, w):
                filled(dve, job)
                c0 = cols[t][0]
                for k in range(nk):
                    st.do(dve.tensor_scalar(hT[:, k0 + k, c0:c0 + w], bk(job)[:, k * w:(k + 1) * w],
                                            lncol[:, k0 + k:k0 + k + 1], lncol[:, 8 + k0 + k:9 + k0 + k], ALU.mult, ALU.add),
                          read_of(job) if k == nk - 1 else None)

            scaled("X0b", 0, 4, 4, P)
            scaled("X1b", 1, 4, 4, P)
            scaled("X2", 2, 0, 8, T2)
            filled(dve, "SA")
            st.then(dve.tensor_copy(colA[:, :, :], bk("SA")[:, 0:MA * 40].rearrange("p (m c) -> p m c", m=MA)), read_of("SA"))
            filled(dve, "SB")
            st.then(dve.tensor_copy(colB[:, :, :], bk("SB")[:, 0:MB * 34].rearrange("p (m c) -> p m c", m=MB)), read_of("SB"))
            lam = colA[:, :, 7]
            st.then(dve.tensor_scalar(cneg[:, 3, :], lam, -1.0, 0.0, ALU.mult, ALU.max))
            st.do(dve.scalar_tensor_tensor(cneg[:, 2, :], cneg[:, 3, :], 2.0, lam, ALU.mult, ALU.add), lam_in)
            dve.wait_ge(ld_gate, 16 * 6)
            for p in range(2):
                filled(dve, f"G{p}")
                st.do(dve.tensor_scalar(gl[:, p, :], bk(f"G{p}")[:, 0:TALL], bg[:, p:p + 1], None, ALU.add), read_of(f"G{p}"))
            dve.wait_ge(softplus_done, 1)
            st.then(dve.scalar_tensor_tensor(gl[:, :, :], gl[:, :, :], 0.0, E[0], ALU.min, ALU.subtract))
            dve.wait_ge(cleared, 9)
            for p in range(2):
                st.do(dve.tensor_tensor_scan(G[:, p, :], rmask[:, :], gl[:, p, :], 0.0, ALU.mult, ALU.add))
            st.settle()
            it = 1.0 / TAU
            st.do(dve.tensor_scalar(gcol[:, :, 0:2], G[:, :, 63:192:P], -it, None, ALU.mult))
            st.do(dve.tensor_scalar(gcol[:, :, 2:4], G[:, :, 63:192:P], it, None, ALU.mult))
            st.do(dve.tensor_scalar(gcol[:, :, 4:6], G[:, :, P - 1:2 * P:P], it, None, ALU.mult))
            st.do(dve.tensor_scalar(gcol[:, :, 6:7], G[:, :, TALL - 1:TALL], it, None, ALU.mult))
            for p in range(2):
                last = G[:, p, SEQ + DSEQ - 1:TOUT:DSEQ]
                st.do(dve.tensor_tensor(gl[:, p, SEQ:TOUT].rearrange("p (s t) -> p s t", t=DSEQ),
                                        last.unsqueeze(2).to_broadcast([P, NSEQ, DSEQ]),
                                        G[:, p, SEQ:TOUT].rearrange("p (s t) -> p s t", t=DSEQ), ALU.subtract),
                      G_ready if p else None)
            dve.wait_ge(lam_exp, 1)
            st.then(dve.tensor_tensor(cneg[:, 2, :], cneg[:, 2, :], cneg[:, 3, :], ALU.add))
            st.do(dve.tensor_scalar(cneg[:, 0, :], cneg[:, 2, :], -RG_C, None, ALU.mult))
            st.do(dve.tensor_scalar(cneg[:, 1, :], cneg[:, 2, :], RG_C, None, ALU.mult), lam_ready)
            dve.wait_ge(colA_moved, 1)
            for m in range(MA):
                copied(dve, f"XA{m}")
                dp, ds_ = xc[:, m, 0:META + SEQ], xc[:, m, META + SEQ:].rearrange("p (s t) -> p s t", t=DSEQ)
                for k in range(WA):
                    w = colA[:, m, k:k + 1]
                    sp_, ss_ = xaP[:, m, k:k + META + SEQ], xaS[:, m, :, k:k + DSEQ]
                    if k == 0:
                        st.do(dve.tensor_scalar(dp, sp_, w, colA[:, m, 4:5], ALU.mult, ALU.add))
                        st.do(dve.tensor_scalar(ds_, ss_, w, colA[:, m, 4:5], ALU.mult, ALU.add))
                    else:
                        st.do(dve.scalar_tensor_tensor(dp, sp_, w, dp, ALU.mult, ALU.add))
                        st.do(dve.scalar_tensor_tensor(ds_, ss_, w, ds_, ALU.mult, ALU.add), xc_ready if k == WA - 1 else None)
                    st.settle()
            dve.wait_ge(exp_ready, 1)
            copied(dve, "Q0")
            copied(dve, "Q1")
            st.do(dve.tensor_tensor(qc[:, :, :], q_sb[:, :, :], E[0][:, :, 0:TOUT], ALU.mult), exp_used)
            dve.wait_ge(exp_ready, 2)
            copied(dve, "K0")
            copied(dve, "K1")
            st.then(dve.tensor_tensor(kc[:, :, :], k_sb[:, :, 0:TOUT], E[1][:, :, 0:TOUT], ALU.mult), exp_used)
            dve.wait_ge(exp_ready, 3)
            st.then(dve.tensor_tensor(q_sb[:, :, :], q_sb[:, :, :], E[0][:, :, 0:TOUT], ALU.mult), qk_decayed)
            for p in range(2):
                st.do(dve.tensor_copy(qm[:, p, :].rearrange("p (s c) -> p s c", s=NSEQ)[:, :, 0:DSEQ],
                                      q_sb[:, p, SEQ:TOUT].rearrange("p (s t) -> p s t", t=DSEQ)), qk_decayed)
            dve.wait_ge(exp_ready, 4)
            st.then(dve.tensor_tensor(k_sb[:, :, :], k_sb[:, :, :], E[1], ALU.mult), qk_decayed)
            for m in range(MB):
                b = bk(f"VB{m}")
                filled(dve, f"VB{m}")
                copied(dve, f"GB{m}")
                st.do(dve.tensor_tensor(uP[:, m, WB - 1:WB - 1 + META], b[:, TOUT:TALL], sgb[:, m, TOUT:TALL], ALU.mult))
                st.do(dve.tensor_tensor(uP[:, m, WB - 1 + META:], b[:, 0:SEQ], sgb[:, m, 0:SEQ], ALU.mult))
                st.do(dve.tensor_tensor(uS[:, m, :, WB - 1:], b[:, SEQ:TOUT].rearrange("p (s t) -> p s t", t=DSEQ),
                                        sgb[:, m, SEQ:TOUT].rearrange("p (s t) -> p s t", t=DSEQ), ALU.mult), read_of(f"VB{m}"))
            st.settle()

            def taps(k0, k1):
                for k in range(k0, k1):
                    for m in range(MB):
                        src, w = uP[:, m, META + k:META + k + SEQ], colB[:, m, k:k + 1]
                        if k == 0:
                            st.do(dve.tensor_scalar(uc[:, m, 0:SEQ], src, w, colB[:, m, WB:WB + 1], ALU.mult, ALU.add))
                        else:
                            if m == 0:
                                st.settle()
                            st.do(dve.scalar_tensor_tensor(uc[:, m, 0:SEQ], src, w, uc[:, m, 0:SEQ], ALU.mult, ALU.add),
                                  uc_ready if (k, m) == (WB - 1, MB - 1) else None)
                st.settle()

            copied(dve, "SS")
            st.settle()
            for m in range(MB):
                for t in range(DSEQ):
                    prod = brst[:, 0:NSEQ * WB].rearrange("p (s k) -> p s k", k=WB)
                    st.then(dve.tensor_tensor(prod, uS[:, m, :, t:t + WB],
                                              colB[:, m, 0:WB].unsqueeze(1).to_broadcast([P, NSEQ, WB]), ALU.mult))
                    st.then(dve.tensor_reduce(uc[:, m, SEQ + t:TOUT:DSEQ], prod, AX.X, ALU.add))
                st.do(dve.tensor_scalar(uc[:, m, SEQ:TOUT], uc[:, m, SEQ:TOUT], colB[:, m, WB:WB + 1], None, ALU.add))
            taps(0, 10)
            copied(dve, "IG2")
            st.then(dve.tensor_tensor(iu[:, :, :], iu[:, :, :], xc[:, :, :], ALU.mult))
            dve.wait_ge(a_ready, MA)
            st.then(dve.tensor_tensor(xc[:, :, :], ra[:, :, :], ra[:, :, :], ALU.mult))
            st.then(dve.scalar_tensor_tensor(tsq[:, :, :], xc[:, :, :], 1.0, tsq[:, :, :], ALU.add, ALU.mult), rg_root_in)
            taps(10, 16)
            dve.wait_ge(rg_root, 1)
            st.then(dve.tensor_tensor(iu[:, :, :], iu[:, :, :], tsq[:, :, :], ALU.mult))
            starts = slice(META + SEQ, TALL, DSEQ)
            st.then(dve.tensor_tensor(tsq[:, :, 0:NSEQ], ra[:, :, starts], colA[:, :, 8:16], ALU.mult))
            st.then(dve.tensor_tensor(iu[:, :, starts], iu[:, :, starts], tsq[:, :, 0:NSEQ], ALU.add))
            st.do(dve.memset(ra[:, :, starts], 0.0))
            st.then(dve.memset(ra[:, :, 0:1], 0.0))
            st.then(dve.tensor_tensor_scan(xc.rearrange("p m t -> p (m t)"), ra.rearrange("p m t -> p (m t)"),
                                           iu.rearrange("p m t -> p (m t)"), 0.0, ALU.mult, ALU.add), h_ready)

            taps(16, WB)

            def keys_out(c):
                filled(dve, f"KT{c}")
                n = rows0[c]
                st.do(dve.tensor_copy(kT_sb[0:n, c, :, :], bk(f"KT{c}")[0:n, 0:2 * P].rearrange("p (a b) -> p a b", a=2)),
                      read_of(f"KT{c}"))

            def scores_out(c):
                for par, o in (("e", 0), ("o", 1)):
                    job = f"SC{c}{par}"
                    filled(dve, job)
                    if c < 2:
                        dst = sc[:, o::2, :]
                        src = bk(job)[:, 0:2 * P].rearrange("p (a b) -> p a b", a=2)
                        msk = upper[:, :].unsqueeze(1).to_broadcast([P, 2, P])
                    else:
                        dst = sc2[0:SAMP, o::2, :]
                        src = bk(job)[0:SAMP, 0:2 * SAMP].rearrange("p (a b) -> p a b", a=2)
                        msk = smask[:, :].unsqueeze(1).to_broadcast([SAMP, 2, SAMP])
                    st.do(dve.tensor_tensor(dst, src, msk, ALU.mult), read_of(job))

            def state_out(job, c):
                filled(dve, job)
                for p in range(2):
                    src = bk(job)[:, p * DV:(p + 1) * DV]
                    if c is None:
                        ins = dve.tensor_copy(Sp[:, p, :], src)
                    else:
                        ins = dve.scalar_tensor_tensor(Sp[:, p, :], Sp[:, p, :], eg[:, p, c:c + 1], src, ALU.mult, ALU.add)
                    st.do(ins, read_of(job) if p else None)

            def outputs_out(c):
                n = rows[c]
                for par, o in (("e", 0), ("o", 1)):
                    job = f"O{c}{par}"
                    filled(dve, job)
                    st.do(dve.tensor_copy(o_sb[0:n, c, :].rearrange("p (a b e) -> p a b e", b=2, e=DV)[:, :, o, :],
                                          bk(job)[0:n, 0:2 * DV].rearrange("p (a e) -> p a e", a=2)), read_of(job))

            def mean_squares():
                for c in (0, 2, 1):
                    n = rows[c]
                    o4 = o_sb[0:n, c, :].rearrange("p (h e) -> p h e", e=DV)
                    v4 = tsq_flat[0:n, 0:DC].rearrange("p (h e) -> p h e", e=DV)
                    st.then(dve.tensor_tensor(v4, o4, o4, ALU.mult))
                    st.then(dve.tensor_reduce(rsq[0:n, c, :], v4, AX.X, ALU.add))
                st.then(dve.tensor_scalar(rsq[:, :, :], rsq[:, :, :], 1.0 / DV, EPS, ALU.mult, ALU.add), o_root_in)

            def finish_outputs(c):
                n = rows[c]
                o4 = o_sb[0:n, c, :].rearrange("p (h e) -> p h e", e=DV)
                st.then(dve.tensor_tensor(o4, o4, rsq[0:n, c, :].unsqueeze(2).to_broadcast([n, NH, DV]), ALU.mult))
                st.then(dve.tensor_tensor(o4, o4, gnorm[0:n, :].unsqueeze(1).to_broadcast([n, NH, DV]), ALU.mult))
                copied(dve, f"R{c}")
                st.do(dve.tensor_tensor(o_sb[0:n, c, :], o_sb[0:n, c, :], r_sb[0:n, c, :], ALU.mult), o_ready)

            def values_by_sequence(p):
                for q in range(2):
                    h = 2 * p + q
                    st.do(dve.tensor_tensor(vm[0:SAMP, q, :, :],
                                            v_sb[0:SAMP, 2, h * DV:(h + 1) * DV].unsqueeze(1).to_broadcast([SAMP, NSEQ, DV]),
                                            sseq[:, :].unsqueeze(2).to_broadcast([SAMP, NSEQ, DV]), ALU.mult),
                          vm_ready if q else None)

            def sample_state_out(p):
                for a in range(2):
                    job = f"W{p}{a}"
                    filled(dve, job)
                    v = S0[:, p, 4 * a:4 * a + 4, :]
                    st.do(dve.tensor_tensor(v, v, bk(job)[:, 0:4 * DV].rearrange("p (s e) -> p s e", e=DV), ALU.add),
                          read_of(job))

            keys_out(2)
            dve.wait_ge(consts_ready, 4)
            scores_out(2)
            filled(dve, "MU")
            for m in range(MB):
                st.do(dve.scalar_tensor_tensor(uc[:, m, :], bk("MU")[:, 0:TOUT], -1.0 / DB, uc[:, m, :], ALU.mult, ALU.add),
                      read_of("MU") if m else None)
            state_out("STM", None)
            keys_out(0)
            scores_out(0)
            filled(dve, "VAR")
            st.then(dve.tensor_scalar(brst[:, :], bk("VAR")[:, 0:TOUT], 1.0 / DB, EPS, ALU.mult, ALU.add), read_of("VAR"))
            dve.wait_ge(eg_ready, 1)
            outputs_out(0)
            keys_out(1)
            state_out("ST0", 0)
            scores_out(1)
            outputs_out(2)
            for p in range(2):
                st.do(dve.tensor_tensor(S0[:, p, :, :], S0[:, p, :, :], eg[:, p, 2:].unsqueeze(2).to_broadcast([P, NSEQ, DV]),
                                        ALU.mult))
            outputs_out(1)
            dve.wait_ge(consts_ready, 4)
            values_by_sequence(0)
            state_out("ST1", 1)
            st.settle()
            mean_squares()
            for m in range(MA):
                copied(dve, f"GA{m}")
                st.do(dve.tensor_tensor(yT[:, m, :], yT[:, m, :], xc[:, m, META:], ALU.mult), ya_ready)
            dve.wait_ge(b_root, 1)
            st.then(dve.reciprocal(brst[:, :], brst[:, :]))
            st.do(dve.tensor_tensor(uc[:, :, :], uc[:, :, :], brst[:, :].unsqueeze(1).to_broadcast([P, MB, TOUT]), ALU.mult),
                  dn_ready)
            dve.wait_ge(o_root, 1)
            st.then(dve.reciprocal(rsq[:, :, :], rsq[:, :, :]))
            finish_outputs(0)
            sample_state_out(0)
            values_by_sequence(1)
            finish_outputs(2)
            finish_outputs(1)
            sample_state_out(1)

            for t in range(3):
                n = rows[t]
                dve.wait_ge(h0_ready, t + 1)
                for c in range(2):
                    job, w = f"P{t}{c}", slice(c * 512, (c + 1) * 512)
                    filled(dve, job)
                    st.do(dve.scalar_tensor_tensor(xt[0:n, t, w], xt[0:n, t, w], ALPHA, bk(job)[0:n, :], ALU.mult, ALU.add),
                          read_of(job))
                st.settle()
                row_stats(xt, t, n, ln1_stats)
                dve.wait_ge(xhat1_ready, t + 1)
                dve.wait_ge(ld_ln, 64)
                st.then(dve.tensor_tensor(xt[0:n, t, :], xt[0:n, t, :], lnbc[0:n, 0, :], ALU.mult))
                st.do(dve.tensor_tensor(xt[0:n, t, :], xt[0:n, t, :], lnbc[0:n, 1, :], ALU.add), h1_ready)

            dve.wait_ge(moe_consts, 8)
            dve.wait_ge(ld_moe, 64)
            filled(dve, "LG")
            for t in range(3):
                n = rows[t]
                st.do(dve.tensor_tensor(lg[0:n, t, :], bk("LG")[0:n, t * NE:(t + 1) * NE], rb[0:n, :], ALU.add),
                      read_of("LG") if t == 2 else None)
            st.settle()
            for t in range(3):
                st.do(dve.max(v8[:, t, :], lg[:, t, :]))
            st.settle()
            st.do(dve.tensor_scalar(sm[:, :, 0:1], v8[:, :, 0:1], -1.0, None, ALU.mult), top_ready)
            for t in range(3):
                st.do(dve.max_index(i8u[:, t, :], v8[:, t, :], lg[:, t, :]))
            st.settle()
            st.then(dve.tensor_copy(i8f[:, :, :], i8u[:, :, 0:TOPK]))
            oh3 = oh.rearrange("p t (k e) -> p (t k) e", e=NE)
            ohg3 = ohg.rearrange("p t (k e) -> p (t k) e", e=NE)
            st.then(dve.tensor_tensor(oh3, io32[:, :].unsqueeze(1).to_broadcast([P, 3 * TOPK, NE]),
                                      i8f.rearrange("p t k -> p (t k)").unsqueeze(2).to_broadcast([P, 3 * TOPK, NE]),
                                      ALU.is_equal))
            st.then(dve.tensor_reduce(M[:, :, :], oh.rearrange("p t (k e) -> p t e k", e=NE), AX.X, ALU.add))
            st.do(dve.tensor_tensor(M[:, :, :], M[:, :, :], valid[:, :].unsqueeze(2).to_broadcast([P, 3, NE]), ALU.mult),
                  mask_ready)
            dve.wait_ge(top_exp, 3)
            st.then(dve.tensor_reduce(sm[:, :, 1], e4[:, :, :], AX.X, ALU.add))
            st.then(dve.reciprocal(sm[:, :, 2], sm[:, :, 1]))
            st.then(dve.tensor_tensor(e4[:, :, :], e4[:, :, :], sm[:, :, 2:3].to_broadcast([P, 3, TOPK]), ALU.mult))
            st.then(dve.tensor_tensor(ohg3, oh3, e4.rearrange("p t k -> p (t k)").unsqueeze(2).to_broadcast([P, 3 * TOPK, NE]),
                                      ALU.mult))
            st.then(dve.tensor_reduce(gates[:, :, :], ohg.rearrange("p t (k e) -> p t e k", e=NE), AX.X, ALU.add))
            st.do(dve.tensor_tensor(gates[:, :, :], gates[:, :, :], valid[:, :].unsqueeze(2).to_broadcast([P, 3, NE]), ALU.mult),
                  gates_ready)
            filled(dve, "POS")
            st.do(dve.tensor_tensor(M[:, :, :], bk("POS")[:, 0:3 * NE].rearrange("p (t e) -> p t e", e=NE), M[:, :, :],
                                    ALU.mult))
            st.then(dve.reduce_max(nmx[:, 0:1], bk("POS")[:, 3 * NE:4 * NE], AX.X), read_of("POS"))
            for r in range(PASSES):
                st.do(dve.tensor_scalar(posm[:, :, r * NE:(r + 1) * NE], M[:, :, :], -1.0 - CAP * r, None, ALU.add),
                      routed if r == PASSES - 1 else None)
            for r in range(1, PASSES):
                st.do(dve.tensor_scalar(npass_f[:, r:r + 1], nmx[:, 0:1], float(CAP * r), None, ALU.is_gt))
            st.settle()
            st.then(dve.tensor_reduce(npass_f[:, 0:1], npass_f[:, 1:PASSES], AX.X, ALU.add))
            st.then(dve.tensor_scalar(npass_f[:, 0:1], npass_f[:, 0:1], 1.0, None, ALU.add))
            st.then(dve.tensor_copy(npass[:, :], npass_f[:, 0:1]), routed)

            def make_pick(m):
                for t in range(3):
                    ins = dve.tensor_scalar(pick[:, t, :], io64[:, :], posm[:, t, bass.ds(m, 1)], None, ALU.is_equal)
                ins.then_inc(pick_ready, 1)

            def make_bsel(e, j):
                dve.tensor_scalar(bsel[:, j, :], ones[:, 0:CAP], selx[:, bass.ds(e, 1)], None, ALU.mult).then_inc(bsel_ready, 1)

            make_pick(0)
            make_bsel(0, 0)
            dve.wait_ge(gather_full, 1)
            dve.tensor_copy(xT[:, 0, :], bank[2][:, :]).then_inc(xT_ready, 1)
            copied(dve, "Y21")
            n_pass = dve.value_load(npass[0:1, 0:1], min_val=1, max_val=PASSES)
            with dve.Fori(0, n_pass) as r:
                with dve.Fori(0, PAIRS) as p:
                    pi = r * PAIRS + p
                    for j in range(2):
                        n, e = 2 * pi + j, 2 * p + j
                        dve.wait_ge(gather_full, n + 1)
                        make_pick(n + 1)
                        make_bsel(e + 1, 1 - j)
                        for t in range(3):
                            ins = dve.tensor_scalar(put[:, t, j * CAP:(j + 1) * CAP], io64[:, :], posm[:, t, bass.ds(n, 1)],
                                                    gates[:, t, bass.ds(e, 1)], ALU.is_equal, ALU.mult)
                        ins.then_inc(put_ready, 1)
                        dve.wait_ge(w_used, SLOTS * n + KT)
                        dve.tensor_scalar(g1[:, :], bank[0][:, :], LIMIT, None, ALU.min).then_inc(g1_ready, 1)
                        dve.tensor_scalar(l1[:, :], bank[1][:, :], LIMIT, -LIMIT, ALU.min, ALU.max).then_inc(l1_ready, 1)
                        dve.wait_ge(l1_ready, n + 1)
                        dve.scalar_tensor_tensor(l1[:, :], l1[:, :], 1.0, g1[:, :], ALU.add, ALU.mult).then_inc(t_done, 1)
                        dve.wait_ge(t_done, n + 1)
                        dve.wait_ge(sg_ready, n + 1)
                        dve.tensor_tensor(act_sb[:, :], l1[:, :], sg[:, :], ALU.mult).then_inc(act_ready, 1)
                        dve.wait_ge(gather_full, n + 2)
                        dve.tensor_copy(xT[:, 1 - j, :], bank[2][:, :]).then_inc(xT_ready, 1)
                    for q in range(6):
                        t, c = divmod(q, 2)
                        dst = Y[0:rows[t], t, c * 512:(c + 1) * 512]
                        dve.wait_ge(comb_full, 6 * pi + q + 1)
                        dve.tensor_tensor(dst, dst, bank[6 + q % 2][0:rows[t], :], ALU.add).then_inc(y_added, 1)
            dve.wait_ge(y_added, n_pass * (6 * PAIRS))
            for t in range(3):
                n = rows[t]
                st.then(dve.scalar_tensor_tensor(Y[0:n, t, :], xt[0:n, t, :], ALPHA, Y[0:n, t, :], ALU.mult, ALU.add))
                row_stats(Y, t, n, ln2_stats)
            dve.wait_ge(ld_ln, 96)
            for t in range(3):
                n = rows[t]
                dve.wait_ge(y_hat, t + 1)
                st.then(dve.tensor_tensor(Y[0:n, t, :], Y[0:n, t, :], lnbc[0:n, 0, :], ALU.mult))
                st.do(dve.tensor_tensor(Y[0:n, t, :], Y[0:n, t, :], lnbc[0:n, 1, :], ALU.add), y_done)

        @block.tensor
        def _(pe):
            def job(name, emit):
                n = J[name]
                assert n == job.n, name
                job.n += 1
                if n >= 8:
                    copied(pe, JOBS[n - 8])
                emit(bk(name)).then_inc(bank_full, 1)

            job.n = 0

            def chain(out, pairs):
                for n, (a, b) in enumerate(pairs):
                    ins = pe.matmul(out, a, b, start=n == 0, stop=n == len(pairs) - 1)
                return ins

            def transposes(parts):
                for out, src, k in parts:
                    ins = pe.transpose(out, src, ident[0:k, 0:k])
                return ins

            pe.wait_ge(consts_ready, 1)
            pe.wait_ge(ld_lncol, 32)
            job("LNC", lambda b: transposes([(b[:, 0:16], lnrow[0:16, :], 16)]))

            def x_job(name, t, k0, nk, w):
                pe.wait_ge(xhat_ready, t + 1)
                job(name, lambda b: transposes([(b[:, k * w:(k + 1) * w], xt[0:w, t, (k0 + k) * P:(k0 + k + 1) * P], w)
                                                for k in range(nk)]))

            x_job("X0a", 0, 0, 4, P)
            x_job("X0b", 0, 4, 4, P)
            x_job("X1a", 1, 0, 4, P)
            x_job("X1b", 1, 4, 4, P)
            x_job("X2", 2, 0, 8, T2)
            pe.wait_ge(ld_packA, 16 * 7)
            job("SA", lambda b: transposes([(b[:, m * 40:(m + 1) * 40], packA[:, m * P:(m + 1) * P], 40) for m in range(MA)]))
            pe.wait_ge(ld_packB, 16 * 4)
            job("SB", lambda b: transposes([(b[:, m * 34:(m + 1) * 34], packB[:, m * P:(m + 1) * P], 34) for m in range(MB)]))
            pe.wait_ge(ld_packS, 16)
            job("SS", lambda b: transposes([(b[:, (2 * a + m) * 120:(2 * a + m + 1) * 120], packS[:, a, m * P:(m + 1) * P], 120)
                                            for a in range(2) for m in range(MB)]))
            for name in ("X0a", "X0b", "X1a", "X1b", "X2"):
                copied(pe, name)

            def project(name, block_, c, w, n):
                job(name, lambda b: chain(b[0:w, 0:n], [(win[block_][:, k, c:c + w], hT[:, k, 0:n]) for k in range(KT)]))

            def project_heads(name, c, n):
                def emit(b):
                    for k in range(KT):
                        for q in range(2):
                            cc = c + q * DK
                            ins = pe.matmul(b[64 * q:64 * q + 64, 0:n], win["qk"][:, k, cc:cc + 64], hT[:, k, 0:n],
                                            start=k == 0, stop=k == KT - 1)
                    return ins
                job(name, emit)

            def project_rows(name, t, c):
                c0 = cols[t][0]
                n = T2 if name == "V2" else rows[t]
                job(name, lambda b: chain(b[0:n, 0:DC], [(hT[:, k, c0:c0 + n], win["vr"][:, k, c:c + DC]) for k in range(KT)]))

            pe.wait_ge(ld_win["z"], 16)
            project("Z", "z", 0, RANK, TALL)
            pe.wait_ge(ld_win["qk"], 16)
            project_heads("Q0", 0, TOUT)
            copied(pe, "Z")
            pe.wait_ge(ld_gate, 16 * 6)
            for p in range(2):
                def emit(b, p=p):
                    for q in range(2):
                        c = (2 * p + q) * DK
                        ins = pe.matmul(b[64 * q:64 * q + 64, 0:TALL], wg2[0:RANK, c:c + 64], zT[0:RANK, :], start=True, stop=True)
                    return ins
                job(f"G{p}", emit)
            project_heads("Q1", 2 * DK, TOUT)
            project_heads("K0", DQK, TALL)
            project_heads("K1", DQK + 2 * DK, TALL)
            pe.wait_ge(ld_win["xa"], 16)
            for m in range(MA):
                project(f"XA{m}", "xa", m * P, P, TALL)
            pe.wait_ge(ld_win["vbgb"], 16)
            for m in range(MB):
                project(f"GB{m}", "vbgb", DB + m * P, P, TALL)
                project(f"VB{m}", "vbgb", m * P, P, TALL)
            pe.wait_ge(ld_win["vr"], 16)
            project_rows("V2", 2, 0)
            project_rows("V0", 0, 0)
            pe.wait_ge(xc_ready, MA)
            pe.wait_ge(ld_wbd, 16 * 20)
            for g, name in enumerate(("RG", "IG")):
                for m in range(MA):
                    ks = [k for k in range(MA) if abs(k - m) <= 1]
                    job(f"{name}{m}", lambda b: chain(b[:, 0:TALL], [(wbd[:, g, k, m * P:(m + 1) * P], xc[:, k, :]) for k in ks]))
            project_rows("V1", 1, 0)
            project_rows("R2", 2, DC)
            project_rows("R0", 0, DC)
            project_rows("R1", 1, DC)

            cols0 = [cols[0], cols[1], (2 * P, TALL)]

            def keys_job(c):
                n = rows0[c]
                job(f"KT{c}", lambda b: transposes([(b[0:n, p * P:(p + 1) * P], k_sb[:, p, cols0[c][0]:cols0[c][1]], P)
                                                    for p in range(2)]))

            def scores_jobs(c):
                c0, c1 = cols[c]
                n = rows[c]
                for o, par in enumerate("eo"):
                    def emit(b):
                        for p in range(2):
                            r = slice(64 * o, 64 * o + DK)
                            ins = pe.matmul(b[0:n, p * n:(p + 1) * n], kc[r, p, c0:c1], qc[r, p, c0:c1], start=True, stop=True)
                        return ins
                    job(f"SC{c}{par}", emit)

            def outputs_jobs(c):
                c0, c1 = cols[c]
                n = rows[c]
                copied(pe, f"SC{c}e")
                copied(pe, f"SC{c}o")
                for o, par in enumerate("eo"):
                    def emit(b):
                        for p in range(2):
                            h, r = 2 * p + o, slice(64 * o, 64 * o + DK)
                            out = b[0:n, p * DV:(p + 1) * DV]
                            s = sc[:, h, :] if c < 2 else sc2[0:SAMP, h, :]
                            pe.matmul(out, s, v_sb[0:n, c, h * DV:(h + 1) * DV], start=True, stop=False)
                            if c < 2:
                                ins = pe.matmul(out, q_sb[r, p, c0:c1], Sp[r, p, :], start=False, stop=True)
                            else:
                                for a in range(NSEQ):
                                    ins = pe.matmul(out, qm[r, p, a * SAMP:(a + 1) * SAMP], S0[r, p, a, :], start=False,
                                                    stop=a == NSEQ - 1)
                        return ins
                    job(f"O{c}{par}", emit)

            def state_job(name, c, r0, r1):
                copied(pe, f"KT{c}")

                def emit(b):
                    for h in range(NH):
                        base, p = head(h)
                        ins = pe.matmul(b[base:base + 64, p * DV:(p + 1) * DV], kT_sb[r0:r1, c, p, base:base + 64],
                                        v_sb[r0:r1, c, h * DV:(h + 1) * DV], start=True, stop=True)
                    return ins
                job(name, emit)

            def sample_state_jobs(p):
                pe.wait_ge(vm_ready, p + 1)
                for a in range(2):
                    def emit(b):
                        for q in range(2):
                            ins = pe.matmul(b[64 * q:64 * q + 64, 0:4 * DV], kT_sb[0:SAMP, 2, p, 64 * q:64 * q + 64],
                                            vm[0:SAMP, q, 4 * a:4 * a + 4, :], start=True, stop=True)
                        return ins
                    job(f"W{p}{a}", emit)

            def y_c_job(t, n_ready):
                pe.wait_ge(o_ready, n_ready)
                n = rows[t]
                job(f"YC{t}", lambda b: transposes([(b[:, k * P:k * P + n], o_sb[0:n, t, k * P:(k + 1) * P], n) for k in range(MC)]))

            pe.wait_ge(qk_decayed, 4)
            keys_job(2)
            scores_jobs(2)
            pe.wait_ge(uc_ready, 1)
            job("MU", lambda b: chain(b[:, 0:TOUT], [(ones[:, :], uc[:, m, :]) for m in range(MB)]))
            pe.wait_ge(ld_win["ga"], 16)
            project("GA0", "ga", 0, P, TOUT)
            copied(pe, "V2")
            state_job("STM", 2, SAMP, T2)
            keys_job(0)
            scores_jobs(0)
            pe.wait_ge(sq_ready, 1)
            job("VAR", lambda b: chain(b[:, 0:TOUT], [(ones[:, :], sgb[:, m, 0:TOUT]) for m in range(MB)]))
            project("GA1", "ga", P, P, TOUT)
            copied(pe, "V0")
            copied(pe, "STM")
            outputs_jobs(0)
            keys_job(1)
            state_job("ST0", 0, 0, P)
            scores_jobs(1)
            project("GA2", "ga", 2 * P, P, TOUT)
            pe.wait_ge(ld_S0, 16 * NH)
            outputs_jobs(2)
            copied(pe, "V1")
            copied(pe, "ST0")
            outputs_jobs(1)
            state_job("ST1", 1, 0, P)
            pe.wait_ge(outcols_ready, 2)
            job("OA", lambda b: transposes([(b[0:36, m * P:(m + 1) * P], oaT[:, m, :], P) for m in range(MA)]))
            job("OB", lambda b: transposes([(b[0:62, m * P:(m + 1) * P], obT[:, m, :], P) for m in range(MB)]))
            sample_state_jobs(0)
            y_c_job(0, 1)
            y_c_job(2, 2)
            sample_state_jobs(1)
            y_c_job(1, 3)
            pe.wait_ge(ya_ready, MA)
            pe.wait_ge(yb_ready, MB)
            pe.wait_ge(ld_wout[0], 16)
            pe.wait_ge(ld_wout[1], 16)
            for t in (0, 1, 2):
                copied(pe, f"YC{t}")
            for t in range(3):
                c0, c1 = cols[t]
                for c in range(2):
                    job(f"P{t}{c}", lambda b: chain(b[0:rows[t], :], [(yT[:, k, c0:c1], wout[:, k, c * 512:(c + 1) * 512])
                                                                     for k in range(KT)]))
            for name, t, k0, nk in (("H0a", 0, 0, 4), ("H0b", 0, 4, 4), ("H1a", 1, 0, 4), ("H1b", 1, 4, 4), ("H2", 2, 0, 8)):
                pe.wait_ge(h1_ready, t + 1)
                w = rows[t]
                job(name, lambda b: transposes([(b[:, k * w:(k + 1) * w], xt[0:w, t, (k0 + k) * P:(k0 + k + 1) * P], w)
                                                for k in range(nk)]))
            pe.wait_ge(ld_moe, 64)
            for name in ("H0a", "H0b", "H1a", "H1b", "H2"):
                copied(pe, name)

            def logits(b):
                for t in range(3):
                    ins = chain(b[0:rows[t], t * NE:(t + 1) * NE], [(hT[:, k, cols[t][0]:cols[t][1]], wr[:, k, :])
                                                                    for k in range(KT)])
                return ins
            job("LG", logits)

            def places(b):
                for t in range(3):
                    chain(b[:, t * NE:(t + 1) * NE], [(ones[:, :], M[:, u, :]) for u in range(t)] + [(upper[:, :], M[:, t, :])])
                return chain(b[:, 3 * NE:4 * NE], [(ones[:, :], M[:, u, :]) for u in range(3)])
            pe.wait_ge(mask_ready, 1)
            job("POS", places)
            pe.wait_ge(gates_ready, 1)
            job("GT", lambda b: transposes([(b[0:NE, t * P:(t + 1) * P], gates[:, t, :], P) for t in range(3)]))
            copied(pe, "GT")
            for t in range(3):
                for c in range(2):
                    job(f"Y{t}{c}", lambda b: pe.matmul(b[0:rows[t], :], gT[0:NE, t * P:t * P + rows[t]],
                                                        b2_sb[0:NE, c * 512:(c + 1) * 512], start=True, stop=True))
            assert job.n == len(JOBS)
            for name in JOBS[-8:]:
                copied(pe, name)

            def gather():
                for k in range(KT):
                    for t in range(3):
                        ins = pe.matmul(bank[2][:, k * CAP:(k + 1) * CAP], xt[:, t, k * P:(k + 1) * P], pick[:, t, :],
                                        start=t == 0, stop=t == 2)
                ins.then_inc(gather_full, 1)

            pe.wait_ge(pick_ready, 1)
            gather()
            n_pass = pe.value_load(npass[0:1, 0:1], min_val=1, max_val=PASSES)
            with pe.Fori(0, n_pass) as r:
                with pe.Fori(0, PAIRS) as p:
                    pi = r * PAIRS + p
                    for j in range(2):
                        n = 2 * pi + j
                        pe.wait_ge(bsel_ready, n + 1)
                        for g in range(2):
                            for h in range(2):
                                c = (2 * g + h) * 512
                                pe.matmul(bank[g][64 * h:64 * h + 64, :], bsel[:, j, :], b1_sb[:, c:c + 512],
                                          start=True, stop=False)
                        pe.wait_ge(xT_ready, n + 1)
                        for k in range(KT):
                            pe.wait_ge(w_full[k], 16 * n + 16)
                            for g in range(2):
                                for h in range(2):
                                    c = k * SLOT + (2 * g + h) * 512
                                    ins = pe.matmul(bank[g][64 * h:64 * h + 64, :], xTk[:, j, k, :], ring[:, c:c + 512],
                                                    start=False, stop=k == KT - 1)
                            ins.then_inc(w_used, 1)
                        if j == 1:
                            pe.wait_ge(put_ready, n + 1)
                            for t in range(3):
                                ins = pe.transpose(bank[5][:, t * P:(t + 1) * P], put[:, t, :], ident[:, :])
                            ins.then_inc(putT_full, 1)
                        pe.wait_ge(pick_ready, n + 2)
                        gather()
                        pe.wait_ge(act_ready, n + 1)
                        for k in range(4):
                            ins = pe.transpose(bank[3][:, k * P:(k + 1) * P], act_sb[:, k * P:(k + 1) * P], ident[:, :])
                        ins.then_inc(actT_full, 1)
                        pe.wait_ge(actT_ready, n + 1)
                        if j == 1:
                            pe.wait_ge(out_ready, 2 * n)
                        for k in range(KT):
                            if k % 2 == 0:
                                pe.wait_ge(w_full[8 + k // 2], 16 * n + 16)
                            for h in range(2):
                                c = 8 * SLOT + k * D + h * 512
                                a = actT[:, k % 4, (k // 4) * CAP:(k // 4 + 1) * CAP]
                                ins = pe.matmul(bank[4][64 * h:64 * h + 64, :], a, ring[:, c:c + 512],
                                                start=k == 0, stop=k == KT - 1)
                            if k % 2 == 1:
                                ins.then_inc(w_used, 1)
                    pe.wait_ge(putT_ready, pi + 1)
                    pe.wait_ge(out_ready, 4 * pi + 4)
                    for q in range(6):
                        t, h = divmod(q, 2)
                        if q >= 2:
                            pe.wait_ge(y_added, 6 * pi + q - 1)
                        pe.matmul(bank[6 + q % 2][0:rows[t], :], putT[:, t * P:t * P + rows[t]], eout[:, h, :],
                                  start=True, stop=True).then_inc(comb_full, 1)


_INS = ["x_prompt", "x_sample", "state_conv_a", "state_rglru", "state_conv_b", "state_gla", "meta_tokens", "ln0_g", "ln0_b",
        "w_in", "conv_a_w", "conv_a_b", "w_rg", "b_rg", "w_ig", "b_ig", "lru_lambda", "conv_b_w", "conv_b_b", "ln_b_g",
        "ln_b_b", "w_gate2", "b_gate", "gla_norm_g", "w_out", "ln1_g", "ln1_b", "router_w", "router_b", "moe_w1",
        "moe_b1", "moe_w2", "moe_b2", "ln2_g", "ln2_b"]
_OUTS = [(1, SEQ, D), (NSEQ, DSEQ, D), (1, 1, WA - 1, DA), (1, 1, DA), (1, 1, WB - 1, DB), (1, 1, NH, DK, DV),
         (1, NSEQ, WA - 1, DA), (1, NSEQ, DA), (1, NSEQ, WB - 1, DB), (1, NSEQ, NH, DK, DV)]


def kernel(**inputs):
    import numpy as _np
    import concourse.bacc as _bacc
    from concourse.bass_utils import run_bass_kernel_spmd as _run

    nc = _bacc.Bacc("TRN2", target_bir_lowering=False, num_devices=1)
    arrays, args = {}, []
    for name in _INS:
        a = _np.ascontiguousarray(inputs[name])
        arrays[f"in_{name}_dram"] = a
        args.append(nc.dram_tensor(f"in_{name}_dram", a.shape, mybir.dt.from_np(a.dtype), kind="ExternalInput").ap())
    for i, shape in enumerate(_OUTS):
        args.append(nc.dram_tensor(f"out_{i}_dram", shape, F32, kind="ExternalOutput").ap())
    build_kernel(nc, *args)
    r = _run(nc, [arrays], core_ids=[0])
    return tuple(r.results[0][f"out_{i}_dram"] for i in range(len(_OUTS)))
```

```python
from contextlib import ExitStack

import concourse.bass as bass
from concourse import mybir
from concourse.alu_op_type import AluOpType as ALU

F32 = mybir.dt.float32
I32 = mybir.dt.int32
U32 = mybir.dt.uint32
ACT = mybir.ActivationFunctionType
AX = mybir.AxisListType

P = 128
D = 1024
KT = D // P
SEQ, META = 256, 16
NSEQ, DSEQ = 8, 4
SAMP = NSEQ * DSEQ
TOUT = SEQ + SAMP
TALL = TOUT + META
T2 = SAMP + META
DA, DB, DC = 384, 256, 384
MA, MB, MC = DA // P, DB // P, DC // P
WA, WB = 4, 31
BLK = 48
NH, DK, DV = 4, 48, 96
DQK = NH * DK
RANK = 16
TAU = 16.0
NE, TOPK = 32, 4
DF = 1024
LIMIT, SALPHA = 7.0, 1.702
ALPHA = 2.0 ** 0.25
EPS = 1e-5
RG_C = 8.0

C_XA, C_GA, C_VB, C_GB = 0, DA, 2 * DA, 2 * DA + DB
C_Q = 2 * DA + 2 * DB
C_K = C_Q + DQK
C_V = C_K + DQK
C_R = C_V + DC
C_Z = C_R + DC
DIN = C_Z + RANK

PIECES = 12
SLOTS = 16
GROUP = 4
SLOT = 2048
CAP = 64
PASSES = -(-TOUT // CAP)
PAIRS = NE // 2

JOBS = ["LNC", "X0a", "X0b", "X1a", "X1b", "X2", "Z", "Q0", "G0", "G1", "Q1", "K0", "K1", "SA", "SB", "SS",
        "XA0", "XA1", "XA2", "GB0", "VB0", "GB1", "VB1", "VR2", "V0", "RG0", "RG1", "RG2", "IG0", "IG1", "IG2",
        "V1", "GA0", "GA1", "GA2", "KT2", "SC2e", "SC2o", "R0", "STM", "KT0", "SC0e", "SC0o", "R1", "O0e", "O0o",
        "KT1", "ST0", "SC1e", "SC1o", "O2e", "O2o", "MU", "VAR", "O1e", "O1o", "ST1", "OA", "OB", "W00", "W01",
        "YC2", "YC0", "W10", "W11", "P2", "YC1", "P00", "P01", "H2", "LG2", "P10", "P11", "H0a", "H0b", "LG0",
        "H1a", "H1b", "LG1", "POS"]
J = {name: n for n, name in enumerate(JOBS)}


ST_OUT = 1 + 2 * NH + 4 + 1 + NSEQ


class Steps:

    def __init__(self, eng, own):
        self.eng, self.own, self.count, self.last = eng, own, {}, None

    def do(self, ins, sem=None):
        if isinstance(sem, tuple):
            ins.then_inc(sem[0], 1)
            self.last = sem
            return
        sem = self.own if sem is None else sem
        ins.then_inc(sem, 1)
        self.count[id(sem)] = self.count.get(id(sem), 0) + 1
        self.last = (sem, self.count[id(sem)])

    def settle(self):
        self.eng.wait_ge(*self.last)

    def then(self, ins, sem=None):
        self.do(ins, sem)
        self.settle()


def build_kernel(nc, x_prompt, x_sample, state_conv_a, state_rglru, state_conv_b, state_gla, meta_tokens, ln0_g, ln0_b,
                 w_in, conv_a_w, conv_a_b, w_rg, b_rg, w_ig, b_ig, lru_lambda, conv_b_w, conv_b_b, ln_b_g, ln_b_b,
                 w_gate2, b_gate, gla_norm_g, w_out, ln1_g, ln1_b, router_w, router_b, moe_w1, moe_b1, moe_w2, moe_b2,
                 ln2_g, ln2_b, y_prompt, y_sample, o_conv_a_p, o_rglru_p, o_conv_b_p, o_gla_p, o_conv_a_s, o_rglru_s,
                 o_conv_b_s, o_gla_s):
    with ExitStack() as ctx:
        def sb(name, shape, dt=F32):
            return ctx.enter_context(nc.sbuf_tensor(name, shape, dt))

        def sem(name):
            return ctx.enter_context(nc.semaphore(name))

        W_MEM = 43900
        ring = sb("ring", [P, W_MEM])
        xt = sb("xt", [P, 3, D])
        lnbc = sb("lnbc", [P, 2, D])
        hT = sb("hT", [P, KT, TALL])
        ident = sb("ident", [P, P])
        ones = sb("ones", [P, P])
        upper = sb("upper", [P, P])
        smask = sb("smask", [SAMP, SAMP])
        sseq = sb("sseq", [SAMP, NSEQ])
        stat = sb("stat", [P, 3, 2, 6])
        mv = sb("mv", [P, 3, 2])
        rst = sb("rst", [P, 3, 2])
        npass_f = sb("npass_f", [P, 8])
        npass = sb("npass", [P, 1], I32)
        wr = sb("wr", [P, KT, NE])
        rb = sb("rb", [P, NE])
        io32 = sb("io32", [P, NE])
        io64 = sb("io64", [P, CAP])
        iraw = sb("iraw", [P, CAP], I32)
        selx = sb("selx", [P, NE + 1])
        r2 = sb("r2", [P, DC])
        valid = sb("valid", [P, 3])

        top = {"mixer": PIECES * SLOT, "moe": SLOTS * SLOT}

        def part(phase, *shape):
            n = 1
            for s in shape:
                n *= s
            a = top[phase]
            top[phase] = a + n
            assert top[phase] <= W_MEM, (phase, top[phase])
            v = ring[:, a:a + n]
            if len(shape) == 2:
                v = v.rearrange("p (a b) -> p a b", b=shape[1])
            if len(shape) == 3:
                v = v.rearrange("p (a b c) -> p a b c", b=shape[1], c=shape[2])
            return v

        yT = part("mixer", KT, TOUT)
        colA = part("mixer", MA, 40)
        colB = part("mixer", MB, 34)
        lncol = part("mixer", 16)
        wbd_flat = part("mixer", 2 * MA * DA)
        wbd = wbd_flat.rearrange("p (g k c) -> p g k c", g=2, k=MA)
        o_sb = wbd_flat[:, 0:MC * DC].rearrange("p (t c) -> p t c", t=3)
        r_sb = wbd_flat[:, MC * DC:(MC + 2) * DC].rearrange("p (t c) -> p t c", t=2)
        tsq = part("mixer", MA, TALL)
        tsq_flat = tsq.rearrange("p a b -> p (a b)")
        cneg = part("mixer", 4, MA)
        uP = part("mixer", MB, WB - 1 + META + SEQ)
        uS = part("mixer", MB, NSEQ, WB - 1 + DSEQ)
        uc = part("mixer", MB, TOUT)
        sgb = part("mixer", MB, TALL)
        brst = part("mixer", TOUT)
        q_sb = part("mixer", 2, TOUT)
        k_sb = part("mixer", 2, TALL)
        gl = part("mixer", 2, TALL)
        G = part("mixer", 2, TALL)
        qc = part("mixer", 2, TOUT)
        kc = part("mixer", 2, TOUT)
        qm = part("mixer", 2, NSEQ * (SAMP + DSEQ))
        vm_at = top["mixer"] - 2 * TOUT * 2 - 2 * NSEQ * (SAMP + DSEQ)
        vm = ring[:, vm_at:vm_at + 2 * NSEQ * DV].rearrange("p (q s e) -> p q s e", q=2, s=NSEQ)
        kT_sb = part("mixer", 3, 2, P)
        v_sb = part("mixer", 3, DC)
        sc = part("mixer", NH, P)
        sc2 = part("mixer", NH, SAMP)
        S0 = part("mixer", 2, NSEQ, DV)
        Sp = part("mixer", 2, DV)
        e_flat = part("mixer", 4 * TALL)
        E = [e_flat[:, n * 2 * TALL:(n + 1) * 2 * TALL].rearrange("p (a b) -> p a b", a=2) for n in range(2)]
        packA = e_flat[0:40, 0:DA]
        packB = e_flat[0:34, DA:DA + DB]
        packS = e_flat[0:120, DA + DB:DA + 3 * DB].rearrange("p (a b) -> p a b", a=2)
        wg2 = part("mixer", DQK + 16)
        bg = part("mixer", 2)
        gcol = part("mixer", 2, 8)
        eg = part("mixer", 2, 2 + NSEQ)
        gnorm = part("mixer", DV)
        rsq = part("mixer", 3, NH)
        rmask = part("mixer", TALL)
        zT = part("mixer", TALL)
        lnrow = part("mixer", P)
        packOA = e_flat[0:36, 0:DA]
        packOB = e_flat[0:62, DA:DA + DB]
        oaT = e_flat[:, DA + DB:DA + DB + MA * 36].rearrange("p (a b) -> p a b", a=MA)
        obT = e_flat[:, DA + DB + MA * 36:DA + DB + MA * 36 + MB * 62].rearrange("p (a b) -> p a b", a=MB)
        at = [10 * SLOT]

        def in_ring(*shape):
            n = 1
            for s in shape:
                n *= s
            a = at[0]
            at[0] += n
            assert at[0] <= PIECES * SLOT
            v = ring[:, a:a + n]
            if len(shape) == 2:
                return v.rearrange("p (a b) -> p a b", b=shape[1])
            return v.rearrange("p (a b c) -> p a b c", b=shape[1], c=shape[2])

        xaP = in_ring(MA, WA - 1 + META + SEQ)
        xaS = in_ring(MA, NSEQ, WA - 1 + DSEQ)
        xc = in_ring(MA, TALL)
        ra = in_ring(MA, TALL)
        iu = in_ring(MA, TALL)
        blocks = [("z", C_Z, RANK), ("qk", C_Q, 2 * DQK + 16), ("xa", C_XA, DA), ("vbgb", C_VB, 2 * DB),
                  ("vr", C_V, 2 * DC), ("ga", C_GA, DA)]
        last_job = {"z": "Z", "qk": "K1", "xa": "XA2", "vbgb": "VB1", "vr": "R1", "ga": "GA2"}
        placed = {name: (c0, n) for name, c0, n in blocks}
        win, spans, off = {}, [], 0
        for name in ("qk", "vr", "ga", "vbgb", "xa", "z"):
            n = placed[name][1]
            spans.append((off, off + KT * n, last_job[name]))
            win[name] = ring[:, off:off + KT * n].rearrange("p (k n) -> p k n", n=n)
            off += KT * n
        assert off <= 10 * SLOT

        def freed_by(a, b):
            return max((job for x, y, job in spans if x < b and a < y), key=J.get)

        wout = ring[:, 8 * SLOT:12 * SLOT].rearrange("p (k n) -> p k n", n=D)

        p2 = ring[:, vm_at:vm_at + D]
        Y = part("moe", 3, D)
        xT = hT.rearrange("p a b -> p (a b)")[:, 0:2 * KT * 2 * CAP].rearrange("p (q k c) -> p q k c", q=2, k=KT)
        pick = part("moe", 3, 2 * CAP)
        put = part("moe", 3, 2 * CAP)
        putT = part("moe", 3 * P)
        eout = part("moe", 2, 512)
        g1 = part("moe", 512)
        l1 = part("moe", 512)
        sg = part("moe", 512)
        actT = part("moe", 4, P)
        b1_sb = part("moe", 2 * DF)
        bsel = part("moe", 2, CAP)
        posm = part("moe", 3, PASSES * NE + 2)
        gates = part("moe", 3, NE)
        lg = part("moe", 3, NE)
        v8 = part("moe", 3, 8)
        i8 = part("moe", 3 * 8)
        i8u = i8.bitcast(U32).rearrange("p (a b) -> p a b", a=3)
        i8f = part("moe", 3, TOPK)
        e4 = part("moe", 3, TOPK)
        sm = part("moe", 3, 4)
        oh = part("moe", 3, TOPK * NE)
        ohg = part("moe", 3, TOPK * NE)
        M = part("moe", 3, NE)
        nmx = part("moe", 4)

        bank = [ctx.enter_context(nc.psum_tensor(f"bank{n}", [P, 512], F32)) for n in range(8)]

        bank_full = sem("bank_full")
        bank_read = [sem(f"bank_read{n}") for n in range(8)]
        dve_step, act_step, pool_step = sem("dve_step"), sem("act_step"), sem("pool_step")
        zeroed_x2 = sem("zeroed_x2")
        consts_ready = sem("consts_ready")
        ld_x = [sem(f"ld_x{t}") for t in range(3)]
        ld_ln = sem("ld_ln")
        ld_lncol = sem("ld_lncol")
        ld_packA, ld_packB, ld_packS = sem("ld_packA"), sem("ld_packB"), sem("ld_packS")
        ld_gate, ld_gnorm = sem("ld_gate"), sem("ld_gnorm")
        ld_wbd, ld_S0 = sem("ld_wbd"), sem("ld_S0")
        ld_win = {name: sem(f"ld_win_{name}") for name, _, _ in blocks}
        ld_wout = [sem("ld_wout0"), sem("ld_wout1")]
        ld_moe = sem("ld_moe")
        w_full = [sem(f"w_full{s}") for s in range(SLOTS)]
        w_used = sem("w_used")
        var_ready, std_ready = sem("var_ready"), sem("std_ready")
        ln0_stats, xhat_ready, h0_ready = sem("ln0_stats"), sem("xhat_ready"), sem("h0_ready")
        cleared = sem("cleared")
        colA_moved = sem("colA_moved")
        softplus_done, G_ready = sem("softplus_done"), sem("G_ready")
        exp_ready, exp_used = sem("exp_ready"), sem("exp_used")
        qk_decayed = sem("qk_decayed")
        eg_ready = sem("eg_ready")
        xc_ready, lam_in, lam_exp, lam_ready = sem("xc_ready"), sem("lam_in"), sem("lam_exp"), sem("lam_ready")
        rg_root_in, rg_root = sem("rg_root_in"), sem("rg_root")
        b_root, o_root_in, o_root = sem("b_root"), sem("o_root_in"), sem("o_root")
        a_ready, h_ready = sem("a_ready"), sem("h_ready")
        uc_ready, sq_ready, dn_ready, yb_ready = sem("uc_ready"), sem("sq_ready"), sem("dn_ready"), sem("yb_ready")
        vm_ready, ya_ready, o_ready = sem("vm_ready"), sem("ya_ready"), sem("o_ready")
        outcols_ready = sem("outcols_ready")
        ln1_stats, xhat1_ready, h1_ready = sem("ln1_stats"), sem("xhat1_ready"), sem("h1_ready")
        top_ready, top_exp = sem("top_ready"), sem("top_exp")
        mask_ready, routed, y_zeroed = sem("mask_ready"), sem("routed"), sem("y_zeroed")
        gates_ready = sem("gates_ready")
        moe_consts, moe_cleared, ix_ready = sem("moe_consts"), sem("moe_cleared"), sem("ix_ready")
        ld_router = sem("ld_router")
        st_out, out_stored = sem("st_out"), sem("out_stored")
        pick_ready, bsel_ready, put_ready = sem("pick_ready"), sem("bsel_ready"), sem("put_ready")
        gather_full, xT_ready = sem("gather_full"), sem("xT_ready")
        g1_ready, l1_ready, t_done = sem("g1_ready"), sem("l1_ready"), sem("t_done")
        sg_ready, act_ready = sem("sg_ready"), sem("act_ready")
        actT_full, actT_ready = sem("actT_full"), sem("actT_ready")
        putT_full, putT_ready = sem("putT_full"), sem("putT_ready")
        out_ready = sem("out_ready")
        comb_full, y_added = sem("comb_full"), sem("y_added")
        y_scaled, ln2_stats, y_hat, y_done = sem("y_scaled"), sem("ln2_stats"), sem("y_hat"), sem("y_done")

        def filled(eng, job):
            eng.wait_ge(bank_full, J[job] + 1)

        def copied(eng, job):
            eng.wait_ge(bank_read[J[job] % 8], J[job] // 8 + 1)

        def bk(job):
            return bank[J[job] % 8]

        def read_of(job):
            return bank_read[J[job] % 8], J[job] // 8 + 1

        block = ctx.enter_context(nc.Block())

        rows = [P, P, SAMP]
        rows0 = [P, P, T2]
        cols = [(0, P), (P, 2 * P), (2 * P, 2 * P + SAMP)]

        def head(h):
            return 64 * (h % 2), h // 2

        def w1_piece(e, s):
            return moe_w1[0, bass.ds(e, 1), s * P:(s + 1) * P, :].rearrange("a p c -> p (a c)")

        def w2_piece(e, s):
            r = (s - 8) * 2 * P
            return moe_w2[0, bass.ds(e, 1), r:r + 2 * P, :].rearrange("a (t p) c -> p (a t) c", p=P)

        @block.sync
        def _(sp):
            sp.dma_start(xt[:, 0, :], x_prompt[0, 0:P, :]).then_inc(ld_x[0], 16)
            sp.dma_start(xt[:, 1, :], x_prompt[0, P:2 * P, :]).then_inc(ld_x[1], 16)
            sp.dma_start(lnrow[0:8, :], ln0_g.rearrange("(k p) -> k p", p=P)).then_inc(ld_lncol, 16)
            sp.wait_ge(zeroed_x2, 1)
            sp.dma_start(xt[0:SAMP, 2, :], x_sample.rearrange("b t c -> (b t) c")).then_inc(ld_x[2], 16)
            sp.dma_start(xt[SAMP:T2, 2, :], meta_tokens).then_inc(ld_x[2], 16)
            def load_win(name):
                c0, n = placed[name]
                sp.dma_start(win[name], w_in[0, :, c0:c0 + n].rearrange("(k p) n -> p k n", p=P)).then_inc(ld_win[name], 16)

            sp.dma_start(lnrow[8:16, :], ln0_b.rearrange("(k p) -> k p", p=P)).then_inc(ld_lncol, 16)
            load_win("z")
            load_win("qk")
            sp.dma_start(packA[0:4, :], conv_a_w[0]).then_inc(ld_packA, 16)
            for n, a in enumerate((conv_a_b, b_rg, b_ig, lru_lambda)):
                sp.dma_start(packA[4 + n:5 + n, :], a).then_inc(ld_packA, 16)
            sp.dma_start(packA[8:16, :], state_rglru[0]).then_inc(ld_packA, 16)
            sp.dma_start(packA[16:40, :], state_conv_a[0].rearrange("s k c -> (s k) c")).then_inc(ld_packA, 16)
            load_win("xa")
            sp.dma_start(packB[0:WB, :], conv_b_w[0]).then_inc(ld_packB, 16)
            for n, a in enumerate((conv_b_b, ln_b_g, ln_b_b)):
                sp.dma_start(packB[WB + n:WB + n + 1, :], a).then_inc(ld_packB, 16)
            sp.dma_start(packS, state_conv_b[0].rearrange("(a s) k c -> (s k) a c", a=2)).then_inc(ld_packS, 16)
            load_win("vbgb")
            load_win("vr")
            load_win("ga")
            sp.dma_start(lnbc[:, 0, :], ln0_g.rearrange("(a c) -> a c", a=1).to_broadcast([P, D])).then_inc(ld_ln, 16)
            sp.dma_start(lnbc[:, 1, :], ln0_b.rearrange("(a c) -> a c", a=1).to_broadcast([P, D])).then_inc(ld_ln, 16)
            sp.dma_start(wr[:, :, :], router_w[0].rearrange("(k p) e -> p k e", p=P)).then_inc(ld_router, 16)
            sp.dma_start(rb[:, :], router_b.to_broadcast([P, NE])).then_inc(ld_router, 16)

            filled(sp, freed_by(8 * SLOT, 10 * SLOT))
            sp.dma_start(wout[:, 0:4, :], w_out[0, 0:4 * P, :].rearrange("(k p) n -> p k n", p=P)).then_inc(ld_wout[0], 16)
            w1_order = sorted(range(8), key=lambda s: J[freed_by(s * SLOT, (s + 1) * SLOT)])

            def load_first(s):
                filled(sp, freed_by(s * SLOT, (s + 1) * SLOT))
                sp.dma_start(ring[:, s * SLOT:(s + 1) * SLOT], moe_w1[0, 0, s * P:(s + 1) * P, :]).then_inc(w_full[s], 16)

            for s in w1_order[0:6]:
                load_first(s)
            sp.wait_ge(ya_ready, MA)
            sp.wait_ge(outcols_ready, 2)
            sp.dma_start(wout[:, 4:8, :], w_out[0, 4 * P:8 * P, :].rearrange("(k p) n -> p k n", p=P)).then_inc(ld_wout[1], 16)
            for s in w1_order[6:8]:
                load_first(s)
            sp.wait_ge(h0_ready, 3)
            sp.dma_start(lnbc[:, 0, :], ln1_g.to_broadcast([P, D])).then_inc(ld_ln, 16)
            sp.dma_start(lnbc[:, 1, :], ln1_b.to_broadcast([P, D])).then_inc(ld_ln, 16)
            filled(sp, "P11")
            for s in range(8, PIECES):
                sp.dma_start(ring[:, s * SLOT:(s + 1) * SLOT].rearrange("p (t c) -> p t c", t=2),
                             moe_w2[0, 0, (s - 8) * 2 * P:(s - 7) * 2 * P, :].rearrange("(t p) c -> p t c", p=P)
                             ).then_inc(w_full[s], 16)
            sp.wait_ge(moe_cleared, 5)
            sp.dma_start(b1_sb[0:NE, :], moe_b1[0]).then_inc(ld_moe, 16)
            sp.dma_start(eout[0:NE, :, :], moe_b2[0].rearrange("e (h c) -> e h c", h=2)).then_inc(ld_moe, 16)
            for s in range(PIECES, SLOTS):
                sp.dma_start(ring[:, s * SLOT:(s + 1) * SLOT], moe_w1[0, 1, (s - PIECES) * P:(s - PIECES + 1) * P, :]
                             ).then_inc(w_full[s], 16)
            sp.wait_ge(h1_ready, 3)
            sp.dma_start(lnbc[:, 0, :], ln2_g.to_broadcast([P, D])).then_inc(ld_ln, 16)
            sp.dma_start(lnbc[:, 1, :], ln2_b.to_broadcast([P, D])).then_inc(ld_ln, 16)

            def load_group(e, n, first=0):
                for i in range(GROUP):
                    if (i + 1) * PIECES <= first:
                        continue
                    ei = e + i if isinstance(e, int) else sp.snap(e + i)
                    for c in range(PIECES):
                        k = i * PIECES + c
                        if k < first:
                            continue
                        s = k % SLOTS
                        src = w1_piece(ei, c) if c < 8 else w2_piece(ei, c)
                        dst = ring[:, s * SLOT:(s + 1) * SLOT]
                        if c >= 8:
                            dst = dst.rearrange("p (t c) -> p t c", t=2)
                        sp.wait_ge(w_used, PIECES * n + k - SLOTS + 1)
                        sp.dma_start(dst, src).then_inc(w_full[s], 16)

            load_group(0, 0, SLOTS)
            with sp.Fori(1, NE // GROUP) as g:
                load_group(GROUP * g, GROUP * g)
            sp.wait_ge(routed, 2)
            n_pass = sp.value_load(npass[0:1, 0:1], min_val=1, max_val=PASSES)
            with sp.If(n_pass > 1):
                with sp.Fori(1, n_pass) as r:
                    with sp.Fori(0, NE // GROUP) as g:
                        load_group(GROUP * g, NE * r + GROUP * g)
            for t in range(3):
                sp.wait_ge(y_done, t + 1)
                dst = y_prompt[0, t * P:(t + 1) * P, :] if t < 2 else y_sample.rearrange("b t c -> (b t) c")
                sp.dma_start(dst, Y[0:rows[t], t, :]).then_inc(out_stored, 16)
            sp.wait_ge(out_stored, 48)
            sp.wait_ge(st_out, 16 * ST_OUT)

        @block.gpsimd
        def _(pool):
            st = Steps(pool, pool_step)
            st.do(pool.memset(xt[:, 2, :], 0.0), zeroed_x2)
            st.do(pool.memset(ident[:, :], 0.0))
            st.do(pool.memset(ones[:, :], 1.0))
            st.do(pool.memset(bg[:, :], 0.0), cleared)
            st.then(pool.memset(wg2[:, :], 0.0))
            st.then(pool.affine_select(out=ident[:, :], in_=ident[:, :], compare_op=ALU.not_equal, fill=1.0, base=0,
                                       pattern=[[-1, P]], channel_multiplier=1), consts_ready)
            pool.dma_start(wg2[0:RANK, 0:DQK], w_gate2[0]).then_inc(ld_gate, 16)
            for h in range(NH):
                b, p = head(h)
                pool.dma_start(bg[b:b + DK, p:p + 1], b_gate[0, h * DK:(h + 1) * DK].rearrange("(a b) -> a b", b=1)
                               ).then_inc(ld_gate, 16)
            st.do(pool.memset(xaP[:, :, 0:WA - 1], 0.0), cleared)
            st.do(pool.memset(uP[:, :, 0:WB - 1], 0.0), cleared)
            st.do(pool.memset(qm[:, :, :], 0.0), cleared)
            st.do(pool.memset(S0[:, :, :, :], 0.0), cleared)
            st.do(pool.memset(wbd_flat[:, :], 0.0))
            st.then(pool.memset(rmask[:, :], 1.0), cleared)
            for g, w in enumerate((w_rg, w_ig)):
                for h in range(NH * 2):
                    r0 = h * BLK
                    while r0 < (h + 1) * BLK:
                        r1 = min((h + 1) * BLK, (r0 // P + 1) * P)
                        pool.dma_start(wbd[r0 % P:r0 % P + r1 - r0, g, r0 // P, h * BLK:(h + 1) * BLK],
                                       w[0, h, r0 - h * BLK:r1 - h * BLK, :]).then_inc(ld_wbd, 16)
                        r0 = r1
            for h in range(NH):
                b, p = head(h)
                pool.dma_start(S0[b:b + DK, p, :, :], state_gla[0, :, h, :, :].rearrange("s d e -> d s e")
                               ).then_inc(ld_S0, 16)
            pool.dma_start(gnorm[:, :], gla_norm_g[0:1, :].to_broadcast([P, DV])).then_inc(ld_gnorm, 16)
            st.do(pool.memset(rmask[:, 0:2 * P:P], 0.0), cleared)
            st.do(pool.memset(rmask[:, 2 * P:TOUT:DSEQ], 0.0), cleared)
            st.do(pool.memset(rmask[:, TOUT:TOUT + 1], 0.0), cleared)
            st.do(pool.memset(upper[:, :], 1.0))
            st.do(pool.memset(smask[:, :], 1.0))
            st.then(pool.memset(sseq[:, :], 1.0))
            st.do(pool.affine_select(out=upper[:, :], in_=upper[:, :], compare_op=ALU.is_ge, fill=0.0, base=0,
                                     pattern=[[1, P]], channel_multiplier=-1), consts_ready)
            v = smask[:, :].rearrange("p (a b) -> p a b", b=DSEQ)
            st.then(pool.affine_select(out=v, in_=v, compare_op=ALU.is_ge, fill=0.0, base=0,
                                       pattern=[[DSEQ, NSEQ], [1, DSEQ]], channel_multiplier=-1))
            st.do(pool.affine_select(out=v, in_=v, compare_op=ALU.is_ge, fill=0.0, base=0,
                                     pattern=[[-DSEQ, NSEQ], [0, DSEQ]], channel_multiplier=1), consts_ready)
            st.then(pool.affine_select(out=sseq[:, :], in_=sseq[:, :], compare_op=ALU.is_ge, fill=0.0, base=0,
                                       pattern=[[-DSEQ, NSEQ]], channel_multiplier=1))
            st.then(pool.affine_select(out=sseq[:, :], in_=sseq[:, :], compare_op=ALU.is_ge, fill=0.0, base=DSEQ - 1,
                                       pattern=[[DSEQ, NSEQ]], channel_multiplier=-1), consts_ready)
            st.then(pool.memset(valid[:, :], 1.0))
            st.then(pool.memset(valid[:, 2:3], 0.0))
            st.do(pool.memset(valid[0:SAMP, 2:3], 1.0), moe_consts)
            st.then(pool.iota(iraw[:, 0:CAP], pattern=[[1, CAP]], base=0, channel_multiplier=0))
            st.do(pool.tensor_copy(io64[:, :], iraw[:, 0:CAP]), moe_consts)
            st.do(pool.tensor_copy(io32[:, :], iraw[:, 0:NE]), moe_consts)
            st.do(pool.tensor_copy(selx[:, 0:NE], ident[:, 0:NE]), moe_consts)
            st.do(pool.tensor_copy(selx[:, NE:NE + 1], ident[:, 0:1]), moe_consts)
            pool.wait_ge(ld_ln, 32)
            for t in range(3):
                pool.wait_ge(xhat_ready, t + 1)
                for half in ("X%da" % t, "X%db" % t) if t < 2 else ("X2",):
                    filled(pool, half)
                n = rows0[t]
                st.then(pool.tensor_tensor(xt[0:n, t, :], xt[0:n, t, :], lnbc[0:n, 0, :], ALU.mult))
                st.do(pool.tensor_tensor(xt[0:n, t, :], xt[0:n, t, :], lnbc[0:n, 1, :], ALU.add), h0_ready)
            copied(pool, "SA")
            st.do(pool.tensor_copy(xaS[:, :, :, 0:WA - 1], colA[:, :, 16:40].rearrange("p m (s k) -> p m s k", k=WA - 1)),
                  colA_moved)
            copied(pool, "IG2")
            st.do(pool.tensor_tensor(iu[:, :, :], iu[:, :, :], xc[:, :, :], ALU.mult), ix_ready)
            pool.wait_ge(h_ready, 1)
            pool.wait_ge(qk_decayed, 4)
            st.do(pool.tensor_copy(oaT[:, :, 0:1], xc[:, :, META + SEQ - 1:META + SEQ]))
            st.do(pool.tensor_copy(oaT[:, :, 1:1 + NSEQ], xc[:, :, META + SEQ + DSEQ - 1:TALL:DSEQ]))
            st.do(pool.tensor_copy(oaT[:, :, 9:12], xaP[:, :, META + SEQ:META + SEQ + WA - 1]))
            st.do(pool.tensor_copy(oaT[:, :, 12:36].rearrange("p m (s k) -> p m s k", k=WA - 1), xaS[:, :, :, DSEQ:DSEQ + WA - 1]),
                  outcols_ready)
            st.do(pool.tensor_copy(obT[:, :, 0:WB - 1], uP[:, :, META + SEQ:META + SEQ + WB - 1]))
            st.do(pool.tensor_copy(obT[:, :, WB - 1:62].rearrange("p m (s k) -> p m s k", k=DSEQ), uS[:, :, :, WB - 1:WB - 1 + DSEQ]),
                  outcols_ready)
            pool.dma_start(o_conv_b_s[0, :, 0:WB - 1 - DSEQ, :], state_conv_b[0, :, DSEQ:WB - 1, :]).then_inc(st_out, 16)
            copied(pool, "ST1")
            copied(pool, "W11")
            for h in range(NH):
                b, p = head(h)
                pool.dma_start(o_gla_p[0, 0, h, :, :], Sp[b:b + DK, p, :]).then_inc(st_out, 16)
                pool.dma_start(o_gla_s[0, :, h, :, :].rearrange("s d e -> d s e"), S0[b:b + DK, p, :, :]).then_inc(st_out, 16)
            copied(pool, "OA")
            pool.dma_start(o_rglru_p[0, :, :], packOA[0:1, :]).then_inc(st_out, 16)
            pool.dma_start(o_rglru_s[0, :, :], packOA[1:1 + NSEQ, :]).then_inc(st_out, 16)
            pool.dma_start(o_conv_a_p[0, 0, :, :], packOA[9:12, :]).then_inc(st_out, 16)
            pool.dma_start(o_conv_a_s[0].rearrange("s k c -> (s k) c"), packOA[12:36, :]).then_inc(st_out, 16)
            copied(pool, "OB")
            pool.dma_start(o_conv_b_p[0, 0, :, :], packOB[0:WB - 1, :]).then_inc(st_out, 16)
            for n in range(NSEQ):
                r = WB - 1 + n * DSEQ
                pool.dma_start(o_conv_b_s[0, n, WB - 1 - DSEQ:WB - 1, :], packOB[r:r + DSEQ, :]).then_inc(st_out, 16)
            pool.wait_ge(st_out, 16 * ST_OUT)
            filled(pool, "YC1")
            pool.wait_ge(ln1_stats, 1)
            st.do(pool.memset(lg[:, 2, :], 0.0), moe_cleared)
            st.do(pool.memset(posm[:, :, PASSES * NE:], -1.0), moe_cleared)
            st.do(pool.memset(b1_sb[:, :], 0.0), moe_cleared)
            st.do(pool.memset(eout[:, :, :], 0.0), moe_cleared)
            st.do(pool.memset(putT[:, :], 0.0), moe_cleared)
            st.do(pool.memset(Y[:, :, :], 0.0), y_zeroed)

        @block.scalar
        def _(act):
            st = Steps(act, act_step)

            def root(t, i, k):
                n = rows0[t]
                if k:
                    n = rows[t]
                act.wait_ge(var_ready, 3 * k + i + 1)
                st.do(act.activation(rst[0:n, t, 0:1], rst[0:n, t, 0:1], ACT.Sqrt), std_ready)

            for t in range(3):
                n = rows0[t]
                root(t, t, 0)
                act.wait_ge(ln0_stats, t + 1)
                st.do(act.activation(xt[0:n, t, :], xt[0:n, t, :], ACT.Identity, bias=rst[0:n, t, 1:2], scale=rst[0:n, t, 0:1]),
                      xhat_ready)
            copied(act, "LNC")
            for job, t, k0 in (("X0a", 0, 0), ("X1a", 1, 0)):
                filled(act, job)
                for k in range(4):
                    st.do(act.activation(hT[:, k0 + k, cols[t][0]:cols[t][1]], bk(job)[:, k * P:(k + 1) * P], ACT.Identity,
                                         bias=lncol[:, 8 + k0 + k:9 + k0 + k], scale=lncol[:, k0 + k:k0 + k + 1]),
                          read_of(job) if k == 3 else None)
            filled(act, "Z")
            st.do(act.activation(zT[0:RANK, :], bk("Z")[0:RANK, 0:TALL], ACT.Copy), read_of("Z"))
            filled(act, "Q0")
            st.do(act.activation(q_sb[:, 0, :], bk("Q0")[:, 0:TOUT], ACT.Copy, scale=DK ** -0.5), read_of("Q0"))
            copied(act, "G0")
            copied(act, "G1")
            st.then(act.activation(E[0], gl, ACT.Abs))
            st.then(act.activation(E[0], E[0], ACT.Exp, scale=-1.0))
            st.do(act.activation(E[0], E[0], ACT.Ln, bias=1.0), softplus_done)
            act.wait_ge(lam_in, 1)
            st.then(act.activation(cneg[:, 2, :], cneg[:, 2, :], ACT.Exp, scale=-1.0))
            st.do(act.activation(cneg[:, 2, :], cneg[:, 2, :], ACT.Ln, bias=1.0), lam_exp)
            filled(act, "Q1")
            st.do(act.activation(q_sb[:, 1, :], bk("Q1")[:, 0:TOUT], ACT.Copy, scale=DK ** -0.5), read_of("Q1"))
            for p in range(2):
                filled(act, f"K{p}")
                st.do(act.activation(k_sb[:, p, :], bk(f"K{p}")[:, 0:TALL], ACT.Copy), read_of(f"K{p}"))
            act.wait_ge(cleared, 9)
            filled(act, "SS")
            v = bk("SS")[:, 0:480].rearrange("p (a m s k) -> p a m s k", a=2, m=MB, k=WB - 1)
            for n in range(4):
                a, m = divmod(n, 2)
                st.do(act.activation(uS[:, m, 4 * a:4 * a + 4, 0:WB - 1], v[:, a, m, :, :], ACT.Copy),
                      read_of("SS") if n == 3 else None)
            for m in range(MA):
                b = bk(f"XA{m}")
                filled(act, f"XA{m}")
                st.do(act.activation(xaP[:, m, WA - 1:WA - 1 + META], b[:, TOUT:TALL], ACT.Copy))
                st.do(act.activation(xaP[:, m, WA - 1 + META:], b[:, 0:SEQ], ACT.Copy))
                st.do(act.activation(xaS[:, m, :, WA - 1:], b[:, SEQ:TOUT].rearrange("p (s t) -> p s t", t=DSEQ), ACT.Copy),
                      read_of(f"XA{m}"))
            act.wait_ge(G_ready, 1)
            it = 1.0 / TAU

            def exps(e, sign, biased, bias0, whole):
                for p in range(2):
                    for n, (c0, c1) in enumerate(biased):
                        st.do(act.activation(e[:, p, c0:c1], G[:, p, c0:c1], ACT.Exp, bias=gcol[:, p, bias0 + n:bias0 + n + 1],
                                             scale=sign * it))
                st.do(act.activation(e[:, :, whole[0]:whole[1]], G[:, :, whole[0]:whole[1]] if whole[2] is None else whole[2],
                                     ACT.Exp, scale=sign * it if whole[2] is None else it), exp_ready)

            exps(E[0], 1.0, cols[0:2], 0, (SEQ, TOUT, None))
            exps(E[1], -1.0, cols[0:2], 2, (SEQ, TOUT, None))
            act.wait_ge(exp_used, 1)
            st.do(act.activation(E[0][:, :, 0:TOUT], G[:, :, 0:TOUT], ACT.Exp, scale=it), exp_ready)
            st.do(act.activation(eg[:, :, 0:2], G[:, :, P - 1:2 * P:P], ACT.Exp, scale=it))
            st.do(act.activation(eg[:, :, 2:], G[:, :, SEQ + DSEQ - 1:TOUT:DSEQ], ACT.Exp, scale=it), eg_ready)
            act.wait_ge(exp_used, 2)
            exps(E[1], -1.0, cols[0:2] + [(TOUT, TALL)], 4, (SEQ, TOUT, gl[:, :, SEQ:TOUT]))
            for m in range(MB):
                filled(act, f"GB{m}")
                st.do(act.activation(sgb[:, m, :], bk(f"GB{m}")[:, 0:TALL], ACT.Sigmoid), read_of(f"GB{m}"))
            filled(act, "VR2")
            st.do(act.activation(v_sb[0:T2, 2, :], bk("VR2")[0:T2, 0:DC], ACT.Copy))
            st.do(act.activation(r2[0:SAMP, :], bk("VR2")[64:64 + SAMP, 0:DC], ACT.Silu), read_of("VR2"))
            filled(act, "V0")
            st.do(act.activation(v_sb[:, 0, :], bk("V0")[:, 0:DC], ACT.Copy), read_of("V0"))
            for g, dst in (("RG", ra), ("IG", iu)):
                for m in range(MA):
                    filled(act, f"{g}{m}")
                    c = 5 if g == "RG" else 6
                    st.do(act.activation(dst[:, m, :], bk(f"{g}{m}")[:, 0:TALL], ACT.Sigmoid, bias=colA[:, m, c:c + 1]),
                          read_of(f"{g}{m}"))
            filled(act, "V1")
            st.do(act.activation(v_sb[:, 1, :], bk("V1")[:, 0:DC], ACT.Copy), read_of("V1"))
            act.wait_ge(lam_ready, 1)
            st.settle()
            for m in range(MA):
                st.do(act.activation(tsq[:, m, :], ra[:, m, :], ACT.Tanh, scale=cneg[:, 1, m:m + 1]))
            st.settle()
            for m in range(MA):
                st.do(act.activation(ra[:, m, :], ra[:, m, :], ACT.Exp, scale=cneg[:, 0, m:m + 1]), a_ready)
            act.wait_ge(rg_root_in, 1)
            st.do(act.activation(tsq[:, :, :], tsq[:, :, :], ACT.Sqrt), rg_root)

            def gelu(m):
                filled(act, f"GA{m}")
                st.do(act.activation(yT[:, m, :], bk(f"GA{m}")[:, 0:TOUT], ACT.Gelu_apprx_tanh), read_of(f"GA{m}"))

            def transposed_o(t):
                filled(act, f"YC{t}")
                st.do(act.activation(yT[:, MA + MB:, cols[t][0]:cols[t][1]],
                                     bk(f"YC{t}")[:, 0:MC * P].rearrange("p (k c) -> p k c", c=P)[:, :, 0:rows[t]], ACT.Copy),
                      read_of(f"YC{t}"))

            for m in range(MA):
                gelu(m)
            for t in range(2):
                filled(act, f"R{t}")
                st.do(act.activation(r_sb[0:rows[t], t, :], bk(f"R{t}")[0:rows[t], 0:DC], ACT.Silu), read_of(f"R{t}"))
            copied(act, "MU")
            st.do(act.activation(sgb[:, :, 0:TOUT], uc[:, :, :], ACT.Square), sq_ready)
            copied(act, "VAR")
            st.do(act.activation(brst[:, :], brst[:, :], ACT.Sqrt), b_root)
            act.wait_ge(o_root_in, 1)
            st.do(act.activation(rsq[:, :, :], rsq[:, :, :], ACT.Sqrt), o_root)
            act.wait_ge(dn_ready, 1)
            for m in range(MB):
                st.do(act.activation(yT[:, MA + m, :], uc[:, m, :], ACT.Silu, scale=colB[:, m, WB + 1:WB + 2],
                                     bias=colB[:, m, WB + 2:WB + 3]), yb_ready)
            for job, dst, n, w in (("OA", packOA, 36, DA), ("OB", packOB, 62, DB)):
                filled(act, job)
                st.do(act.activation(dst, bk(job)[0:n, 0:w], ACT.Copy), read_of(job))
            transposed_o(2)
            transposed_o(0)
            filled(act, "P2")
            st.do(act.activation(p2[0:SAMP, 0:512], bk("P2")[0:SAMP, :], ACT.Copy))
            st.do(act.activation(p2[0:SAMP, 512:D], bk("P2")[64:64 + SAMP, :], ACT.Copy), read_of("P2"))
            transposed_o(1)
            def normalise(n, t):
                root(t, n, 1)
                act.wait_ge(ln1_stats, n + 1)
                r = rows[t]
                st.do(act.activation(xt[0:r, t, :], xt[0:r, t, :], ACT.Identity, bias=rst[0:r, t, 1:2], scale=rst[0:r, t, 0:1]),
                      xhat1_ready)

            def transposed_h(job, t, k0, nk):
                filled(act, job)
                w = rows[t]
                st.do(act.activation(hT[:, k0:k0 + nk, cols[t][0]:cols[t][1]],
                                     bk(job)[:, 0:nk * w].rearrange("p (k c) -> p k c", c=w), ACT.Copy), read_of(job))

            def exp_top(n, t):
                act.wait_ge(top_ready, n + 1)
                st.do(act.activation(e4[:, t, :], v8[:, t, 0:TOPK], ACT.Exp, bias=sm[:, t, 0:1]), top_exp)

            normalise(0, 2)
            transposed_h("H2", 2, 0, 8)
            normalise(1, 0)
            transposed_h("H0a", 0, 0, 4)
            transposed_h("H0b", 0, 4, 4)
            normalise(2, 1)
            transposed_h("H1a", 1, 0, 4)
            transposed_h("H1b", 1, 4, 4)
            for n, t in enumerate((2, 0, 1)):
                exp_top(n, t)
            act.wait_ge(routed, 2)
            n_pass = act.value_load(npass[0:1, 0:1], min_val=1, max_val=PASSES)
            act.wait_ge(putT_full, 1)
            act.wait_ge(moe_cleared, 5)
            act.activation(putT[0:NE, 0:2 * P], bank[3][0:NE, 0:2 * P], ACT.Copy).then_inc(out_ready, 1)
            act.activation(putT[0:NE, 2 * P:3 * P], bank[3][0:NE, 2 * P:3 * P], ACT.Copy).then_inc(putT_ready, 1)
            with act.Fori(0, n_pass) as r:
                with act.Fori(0, NE // GROUP) as g:
                    for q in range(2):
                        pi = r * PAIRS + 2 * g + q
                        for j in range(2):
                            n = 2 * pi + j
                            act.wait_ge(g1_ready, n + 1)
                            act.activation(sg[:, :], g1[:, :], ACT.Sigmoid, scale=SALPHA).then_inc(sg_ready, 1)
                            act.wait_ge(actT_full, n + 1)
                            act.activation(actT[:, :, :], bank[3][:, :].rearrange("p (k c) -> p k c", c=P), ACT.Copy
                                           ).then_inc(actT_ready, 1)
                            if j == 1:
                                act.wait_ge(putT_full, pi + 2)
                                act.activation(putT[:, :], bank[3][:, 0:3 * P], ACT.Copy).then_inc(putT_ready, 1)
                            act.wait_ge(w_used, PIECES * n + PIECES)
                            for h in range(2):
                                act.activation(eout[64 * j:64 * j + 64, h, :], bank[4][64 * h:64 * h + 64, :], ACT.Copy
                                               ).then_inc(out_ready, 1)
            for t in range(3):
                n = rows[t]
                root(t, t, 2)
                act.wait_ge(ln2_stats, t + 1)
                act.activation(Y[0:n, t, :], Y[0:n, t, :], ACT.Identity, bias=rst[0:n, t, 1:2], scale=rst[0:n, t, 0:1]
                               ).then_inc(y_hat, 1)

        @block.vector
        def _(dve):
            st = Steps(dve, dve_step)

            def row_stats(src, t, n, signal):
                for c in range(2):
                    st.do(dve.bn_stats(stat[0:n, t, c, :], src[0:n, t, c * 512:(c + 1) * 512]))
                st.settle()
                st.then(dve.bn_aggr(mv[0:n, t, :], stat[0:n, t, :, :].rearrange("p a b -> p (a b)")))
                st.do(dve.tensor_scalar(rst[0:n, t, 0:1], mv[0:n, t, 1:2], EPS, None, ALU.add), var_ready)
                dve.wait_ge(std_ready, st.count[id(var_ready)])
                st.then(dve.reciprocal(rst[0:n, t, 0:1], rst[0:n, t, 0:1]))
                st.do(dve.scalar_tensor_tensor(rst[0:n, t, 1:2], mv[0:n, t, 0:1], -1.0, rst[0:n, t, 0:1], ALU.mult, ALU.mult),
                      signal)

            st.do(dve.memset(rsq[:, :, :], 1.0))
            for t in range(3):
                dve.wait_ge(ld_x[t], 16 if t < 2 else 32)
                row_stats(xt, t, rows0[t], ln0_stats)
            filled(dve, "LNC")
            st.then(dve.tensor_copy(lncol[:, :], bk("LNC")[:, 0:16]), read_of("LNC"))

            def scaled(job, t, k0, nk, w):
                filled(dve, job)
                c0 = cols[t][0]
                for k in range(nk):
                    st.do(dve.tensor_scalar(hT[:, k0 + k, c0:c0 + w], bk(job)[:, k * w:(k + 1) * w],
                                            lncol[:, k0 + k:k0 + k + 1], lncol[:, 8 + k0 + k:9 + k0 + k], ALU.mult, ALU.add),
                          read_of(job) if k == nk - 1 else None)

            scaled("X0b", 0, 4, 4, P)
            scaled("X1b", 1, 4, 4, P)
            scaled("X2", 2, 0, 8, T2)
            filled(dve, "SA")
            st.then(dve.tensor_copy(colA[:, :, :], bk("SA")[:, 0:MA * 40].rearrange("p (m c) -> p m c", m=MA)), read_of("SA"))
            filled(dve, "SB")
            st.then(dve.tensor_copy(colB[:, :, :], bk("SB")[:, 0:MB * 34].rearrange("p (m c) -> p m c", m=MB)), read_of("SB"))
            lam = colA[:, :, 7]
            st.then(dve.tensor_scalar(cneg[:, 3, :], lam, -1.0, 0.0, ALU.mult, ALU.max))
            st.do(dve.scalar_tensor_tensor(cneg[:, 2, :], cneg[:, 3, :], 2.0, lam, ALU.mult, ALU.add), lam_in)
            dve.wait_ge(ld_gate, 16 * 5)
            for p in range(2):
                filled(dve, f"G{p}")
                st.do(dve.tensor_scalar(gl[:, p, :], bk(f"G{p}")[:, 0:TALL], bg[:, p:p + 1], None, ALU.add), read_of(f"G{p}"))
            dve.wait_ge(softplus_done, 1)
            st.then(dve.scalar_tensor_tensor(gl[:, :, :], gl[:, :, :], 0.0, E[0], ALU.min, ALU.subtract))
            dve.wait_ge(cleared, 9)
            for p in range(2):
                st.do(dve.tensor_tensor_scan(G[:, p, :], rmask[:, :], gl[:, p, :], 0.0, ALU.mult, ALU.add))
            st.settle()
            it = 1.0 / TAU
            st.do(dve.tensor_scalar(gcol[:, :, 0:2], G[:, :, 63:192:P], -it, None, ALU.mult))
            st.do(dve.tensor_scalar(gcol[:, :, 2:4], G[:, :, 63:192:P], it, None, ALU.mult))
            st.do(dve.tensor_scalar(gcol[:, :, 4:6], G[:, :, P - 1:2 * P:P], it, None, ALU.mult))
            st.do(dve.tensor_scalar(gcol[:, :, 6:7], G[:, :, TALL - 1:TALL], it, None, ALU.mult))
            for p in range(2):
                last = G[:, p, SEQ + DSEQ - 1:TOUT:DSEQ]
                st.do(dve.tensor_tensor(gl[:, p, SEQ:TOUT].rearrange("p (s t) -> p s t", t=DSEQ),
                                        last.unsqueeze(2).to_broadcast([P, NSEQ, DSEQ]),
                                        G[:, p, SEQ:TOUT].rearrange("p (s t) -> p s t", t=DSEQ), ALU.subtract),
                      G_ready if p else None)
            dve.wait_ge(lam_exp, 1)
            st.then(dve.tensor_tensor(cneg[:, 2, :], cneg[:, 2, :], cneg[:, 3, :], ALU.add))
            st.do(dve.tensor_scalar(cneg[:, 0, :], cneg[:, 2, :], -RG_C, None, ALU.mult))
            st.do(dve.tensor_scalar(cneg[:, 1, :], cneg[:, 2, :], RG_C, None, ALU.mult), lam_ready)
            dve.wait_ge(colA_moved, 1)
            dve.wait_ge(cleared, 9)
            for m in range(MA):
                copied(dve, f"XA{m}")
                dp, ds_ = xc[:, m, 0:META + SEQ], xc[:, m, META + SEQ:].rearrange("p (s t) -> p s t", t=DSEQ)
                for k in range(WA):
                    w = colA[:, m, k:k + 1]
                    sp_, ss_ = xaP[:, m, k:k + META + SEQ], xaS[:, m, :, k:k + DSEQ]
                    if k == 0:
                        st.do(dve.tensor_scalar(dp, sp_, w, colA[:, m, 4:5], ALU.mult, ALU.add))
                        st.do(dve.tensor_scalar(ds_, ss_, w, colA[:, m, 4:5], ALU.mult, ALU.add))
                    else:
                        st.do(dve.scalar_tensor_tensor(dp, sp_, w, dp, ALU.mult, ALU.add))
                        st.do(dve.scalar_tensor_tensor(ds_, ss_, w, ds_, ALU.mult, ALU.add), xc_ready if k == WA - 1 else None)
                    st.settle()
            dve.wait_ge(exp_ready, 1)
            copied(dve, "Q0")
            copied(dve, "Q1")
            st.do(dve.tensor_tensor(qc[:, :, :], q_sb[:, :, :], E[0][:, :, 0:TOUT], ALU.mult), exp_used)
            dve.wait_ge(exp_ready, 2)
            copied(dve, "K0")
            copied(dve, "K1")
            st.then(dve.tensor_tensor(kc[:, :, :], k_sb[:, :, 0:TOUT], E[1][:, :, 0:TOUT], ALU.mult), exp_used)
            dve.wait_ge(exp_ready, 3)
            st.then(dve.tensor_tensor(q_sb[:, :, :], q_sb[:, :, :], E[0][:, :, 0:TOUT], ALU.mult), qk_decayed)
            for p in range(2):
                st.do(dve.tensor_copy(qm[:, p, :].rearrange("p (s c) -> p s c", s=NSEQ)[:, :, 0:DSEQ],
                                      q_sb[:, p, SEQ:TOUT].rearrange("p (s t) -> p s t", t=DSEQ)), qk_decayed)
            dve.wait_ge(exp_ready, 4)
            st.then(dve.tensor_tensor(k_sb[:, :, :], k_sb[:, :, :], E[1], ALU.mult), qk_decayed)
            for m in range(MB):
                b = bk(f"VB{m}")
                filled(dve, f"VB{m}")
                copied(dve, f"GB{m}")
                st.do(dve.tensor_tensor(uP[:, m, WB - 1:WB - 1 + META], b[:, TOUT:TALL], sgb[:, m, TOUT:TALL], ALU.mult))
                st.do(dve.tensor_tensor(uP[:, m, WB - 1 + META:], b[:, 0:SEQ], sgb[:, m, 0:SEQ], ALU.mult))
                st.do(dve.tensor_tensor(uS[:, m, :, WB - 1:], b[:, SEQ:TOUT].rearrange("p (s t) -> p s t", t=DSEQ),
                                        sgb[:, m, SEQ:TOUT].rearrange("p (s t) -> p s t", t=DSEQ), ALU.mult), read_of(f"VB{m}"))
            st.settle()

            def taps(k0, k1):
                for k in range(k0, k1):
                    for m in range(MB):
                        src, w = uP[:, m, META + k:META + k + SEQ], colB[:, m, k:k + 1]
                        if k == 0:
                            st.do(dve.tensor_scalar(uc[:, m, 0:SEQ], src, w, colB[:, m, WB:WB + 1], ALU.mult, ALU.add))
                        else:
                            if m == 0:
                                st.settle()
                            st.do(dve.scalar_tensor_tensor(uc[:, m, 0:SEQ], src, w, uc[:, m, 0:SEQ], ALU.mult, ALU.add),
                                  uc_ready if (k, m) == (WB - 1, MB - 1) else None)
                st.settle()

            copied(dve, "SS")
            st.settle()
            for m in range(MB):
                for t in range(DSEQ):
                    prod = brst[:, 0:NSEQ * WB].rearrange("p (s k) -> p s k", k=WB)
                    st.then(dve.tensor_tensor(prod, uS[:, m, :, t:t + WB],
                                              colB[:, m, 0:WB].unsqueeze(1).to_broadcast([P, NSEQ, WB]), ALU.mult))
                    st.then(dve.tensor_reduce(uc[:, m, SEQ + t:TOUT:DSEQ], prod, AX.X, ALU.add))
                st.do(dve.tensor_scalar(uc[:, m, SEQ:TOUT], uc[:, m, SEQ:TOUT], colB[:, m, WB:WB + 1], None, ALU.add))
            taps(0, 20)
            dve.wait_ge(ix_ready, 1)
            dve.wait_ge(a_ready, MA)
            st.then(dve.tensor_tensor(xc[:, :, :], ra[:, :, :], ra[:, :, :], ALU.mult))
            st.then(dve.scalar_tensor_tensor(tsq[:, :, :], xc[:, :, :], 1.0, tsq[:, :, :], ALU.add, ALU.mult), rg_root_in)
            taps(20, 23)
            dve.wait_ge(rg_root, 1)
            st.then(dve.tensor_tensor(iu[:, :, :], iu[:, :, :], tsq[:, :, :], ALU.mult))
            starts = slice(META + SEQ, TALL, DSEQ)
            st.then(dve.tensor_tensor(tsq[:, :, 0:NSEQ], ra[:, :, starts], colA[:, :, 8:16], ALU.mult))
            st.then(dve.tensor_tensor(iu[:, :, starts], iu[:, :, starts], tsq[:, :, 0:NSEQ], ALU.add))
            st.do(dve.memset(ra[:, :, starts], 0.0))
            st.then(dve.memset(ra[:, :, 0:1], 0.0))
            st.then(dve.tensor_tensor_scan(xc.rearrange("p m t -> p (m t)"), ra.rearrange("p m t -> p (m t)"),
                                           iu.rearrange("p m t -> p (m t)"), 0.0, ALU.mult, ALU.add), h_ready)

            def keys_out(c):
                filled(dve, f"KT{c}")
                n = rows0[c]
                st.do(dve.tensor_copy(kT_sb[0:n, c, :, :], bk(f"KT{c}")[0:n, 0:2 * P].rearrange("p (a b) -> p a b", a=2)),
                      read_of(f"KT{c}"))

            def scores_out(c):
                for par, o in (("e", 0), ("o", 1)):
                    job = f"SC{c}{par}"
                    filled(dve, job)
                    if c < 2:
                        dst = sc[:, o::2, :]
                        src = bk(job)[:, 0:2 * P].rearrange("p (a b) -> p a b", a=2)
                        msk = upper[:, :].unsqueeze(1).to_broadcast([P, 2, P])
                    else:
                        dst = sc2[0:SAMP, o::2, :]
                        src = bk(job)[0:SAMP, 0:2 * SAMP].rearrange("p (a b) -> p a b", a=2)
                        msk = smask[:, :].unsqueeze(1).to_broadcast([SAMP, 2, SAMP])
                    st.do(dve.tensor_tensor(dst, src, msk, ALU.mult), read_of(job))

            def state_out(job, c):
                filled(dve, job)
                for p in range(2):
                    src = bk(job)[:, p * DV:(p + 1) * DV]
                    if c is None:
                        ins = dve.tensor_copy(Sp[:, p, :], src)
                    else:
                        ins = dve.scalar_tensor_tensor(Sp[:, p, :], Sp[:, p, :], eg[:, p, c:c + 1], src, ALU.mult, ALU.add)
                    st.do(ins, read_of(job) if p else None)

            def outputs_out(c):
                n = rows[c]
                for par, o in (("e", 0), ("o", 1)):
                    job = f"O{c}{par}"
                    filled(dve, job)
                    st.do(dve.tensor_copy(o_sb[0:n, c, :].rearrange("p (a b e) -> p a b e", b=2, e=DV)[:, :, o, :],
                                          bk(job)[0:n, 0:2 * DV].rearrange("p (a e) -> p a e", a=2)), read_of(job))

            def mean_squares():
                for c in (0, 2, 1):
                    n = rows[c]
                    o4 = o_sb[0:n, c, :].rearrange("p (h e) -> p h e", e=DV)
                    v4 = tsq_flat[0:n, 0:DC].rearrange("p (h e) -> p h e", e=DV)
                    st.then(dve.tensor_tensor(v4, o4, o4, ALU.mult))
                    st.then(dve.tensor_reduce(rsq[0:n, c, :], v4, AX.X, ALU.add))
                st.then(dve.tensor_scalar(rsq[:, :, :], rsq[:, :, :], 1.0 / DV, EPS, ALU.mult, ALU.add), o_root_in)

            def finish_outputs(c):
                n = rows[c]
                o4 = o_sb[0:n, c, :].rearrange("p (h e) -> p h e", e=DV)
                st.then(dve.tensor_tensor(o4, o4, rsq[0:n, c, :].unsqueeze(2).to_broadcast([n, NH, DV]), ALU.mult))
                st.then(dve.tensor_tensor(o4, o4, gnorm[0:n, :].unsqueeze(1).to_broadcast([n, NH, DV]), ALU.mult))
                copied(dve, f"R{c}" if c < 2 else "VR2")
                st.do(dve.tensor_tensor(o_sb[0:n, c, :], o_sb[0:n, c, :], r_sb[0:n, c, :] if c < 2 else r2[0:n, :], ALU.mult), o_ready)

            def values_by_sequence(p):
                for q in range(2):
                    h = 2 * p + q
                    st.do(dve.tensor_tensor(vm[0:SAMP, q, :, :],
                                            v_sb[0:SAMP, 2, h * DV:(h + 1) * DV].unsqueeze(1).to_broadcast([SAMP, NSEQ, DV]),
                                            sseq[:, :].unsqueeze(2).to_broadcast([SAMP, NSEQ, DV]), ALU.mult),
                          vm_ready if q else None)

            def sample_state_out(p):
                for a in range(2):
                    job = f"W{p}{a}"
                    filled(dve, job)
                    v = S0[:, p, 4 * a:4 * a + 4, :]
                    st.do(dve.tensor_tensor(v, v, bk(job)[:, 0:4 * DV].rearrange("p (s e) -> p s e", e=DV), ALU.add),
                          read_of(job))

            keys_out(2)
            dve.wait_ge(consts_ready, 4)
            scores_out(2)
            for m in range(MA):
                copied(dve, f"GA{m}")
                st.do(dve.tensor_tensor(yT[:, m, :], yT[:, m, :], xc[:, m, META:], ALU.mult), ya_ready)
            st.settle()
            state_out("STM", None)
            keys_out(0)
            scores_out(0)
            taps(23, 25)
            dve.wait_ge(eg_ready, 1)
            outputs_out(0)
            keys_out(1)
            state_out("ST0", 0)
            scores_out(1)
            taps(25, WB)
            outputs_out(2)
            filled(dve, "MU")
            for m in range(MB):
                st.do(dve.scalar_tensor_tensor(uc[:, m, :], bk("MU")[:, 0:TOUT], -1.0 / DB, uc[:, m, :], ALU.mult, ALU.add),
                      read_of("MU") if m else None)
            for p in range(2):
                st.do(dve.tensor_tensor(S0[:, p, :, :], S0[:, p, :, :], eg[:, p, 2:].unsqueeze(2).to_broadcast([P, NSEQ, DV]),
                                        ALU.mult))
            filled(dve, "VAR")
            st.do(dve.tensor_scalar(brst[:, :], bk("VAR")[:, 0:TOUT], 1.0 / DB, EPS, ALU.mult, ALU.add), read_of("VAR"))
            outputs_out(1)
            st.settle()
            mean_squares()
            values_by_sequence(0)
            state_out("ST1", 1)
            dve.wait_ge(b_root, 1)
            st.then(dve.reciprocal(brst[:, :], brst[:, :]))
            st.do(dve.tensor_tensor(uc[:, :, :], uc[:, :, :], brst[:, :].unsqueeze(1).to_broadcast([P, MB, TOUT]), ALU.mult),
                  dn_ready)
            dve.wait_ge(ld_gnorm, 16)
            dve.wait_ge(o_root, 1)
            st.then(dve.reciprocal(rsq[:, :, :], rsq[:, :, :]))
            finish_outputs(2)
            sample_state_out(0)
            finish_outputs(0)
            values_by_sequence(1)
            finish_outputs(1)
            sample_state_out(1)

            def ln1(i, t):
                n = rows[t]
                dve.wait_ge(h0_ready, t + 1)
                if t == 2:
                    copied(dve, "P2")
                    st.do(dve.scalar_tensor_tensor(xt[0:n, t, :], xt[0:n, t, :], ALPHA, p2[0:n, :], ALU.mult, ALU.add))
                else:
                    for c in range(2):
                        job, w = f"P{t}{c}", slice(c * 512, (c + 1) * 512)
                        filled(dve, job)
                        st.do(dve.scalar_tensor_tensor(xt[0:n, t, w], xt[0:n, t, w], ALPHA, bk(job)[0:n, :], ALU.mult, ALU.add),
                              read_of(job))
                st.settle()
                row_stats(xt, t, n, ln1_stats)
                dve.wait_ge(xhat1_ready, i + 1)
                dve.wait_ge(ld_ln, 64)
                st.then(dve.tensor_tensor(xt[0:n, t, :], xt[0:n, t, :], lnbc[0:n, 0, :], ALU.mult))
                st.do(dve.tensor_tensor(xt[0:n, t, :], xt[0:n, t, :], lnbc[0:n, 1, :], ALU.add), h1_ready)

            def top(t):
                n = rows[t]
                filled(dve, f"LG{t}")
                st.then(dve.tensor_tensor(lg[0:n, t, :], bk(f"LG{t}")[0:n, 0:NE], rb[0:n, :], ALU.add), read_of(f"LG{t}"))
                st.then(dve.max(v8[:, t, :], lg[:, t, :]))
                st.do(dve.tensor_scalar(sm[:, t, 0:1], v8[:, t, 0:1], -1.0, None, ALU.mult), top_ready)
                st.then(dve.max_index(i8u[:, t, :], v8[:, t, :], lg[:, t, :]))
                st.then(dve.tensor_copy(i8f[:, t, :], i8u[:, t, 0:TOPK]))
                st.then(dve.tensor_tensor(oh[:, t, :].rearrange("p (k e) -> p k e", e=NE),
                                          io32[:, :].unsqueeze(1).to_broadcast([P, TOPK, NE]),
                                          i8f[:, t, :].unsqueeze(2).to_broadcast([P, TOPK, NE]), ALU.is_equal))
                st.then(dve.tensor_reduce(M[:, t, :], oh[:, t, :].rearrange("p (k e) -> p e k", e=NE), AX.X, ALU.add))
                st.do(dve.tensor_scalar(M[:, t, :], M[:, t, :], valid[:, t:t + 1], None, ALU.mult), mask_ready)

            ln1(0, 2)
            dve.wait_ge(moe_cleared, 4)
            dve.wait_ge(moe_consts, 5)
            dve.wait_ge(ld_router, 32)
            top(2)
            ln1(1, 0)
            ln1(2, 1)
            top(0)
            top(1)
            filled(dve, "POS")
            st.then(dve.tensor_tensor(M[:, :, :], bk("POS")[:, 0:3 * NE].rearrange("p (t e) -> p t e", e=NE), M[:, :, :],
                                      ALU.mult))
            st.do(dve.reduce_max(nmx[:, 0:1], bk("POS")[:, 3 * NE:4 * NE], AX.X), read_of("POS"))
            for r in range(PASSES):
                st.do(dve.tensor_scalar(posm[:, :, r * NE:(r + 1) * NE], M[:, :, :], -1.0 - CAP * r, None, ALU.add),
                      routed if r == PASSES - 1 else None)
            st.settle()
            def make_pick(m):
                for j in range(2):
                    for t in range(3):
                        ins = dve.tensor_scalar(pick[:, t, j * CAP:(j + 1) * CAP], io64[:, :], posm[:, t, bass.ds(m + j, 1)], None,
                                                ALU.is_equal)
                ins.then_inc(pick_ready, 1)

            def batch_out(parity):
                for b in range(2):
                    dve.tensor_copy(xT[:, parity, 4 * b:4 * b + 4, :], bank[(2, 5)[b]][:, :].rearrange("p (k c) -> p k c", c=2 * CAP)
                                    ).then_inc(xT_ready, 1)

            def add_pair(q, n_before):
                t, c = divmod(q, 2)
                dst = Y[0:rows[t], t, c * 512:(c + 1) * 512]
                dve.wait_ge(comb_full, n_before + q + 1)
                dve.tensor_tensor(dst, dst, bank[6 + q % 2][0:rows[t], :], ALU.add).then_inc(y_added, 1)

            def make_bsel(e, j):
                dve.tensor_scalar(bsel[:, j, :], ones[:, 0:CAP], selx[:, bass.ds(e, 1)], None, ALU.mult).then_inc(bsel_ready, 1)

            make_pick(0)
            make_bsel(0, 0)
            for r in range(1, PASSES):
                st.do(dve.tensor_scalar(npass_f[:, r:r + 1], nmx[:, 0:1], float(CAP * r), None, ALU.is_gt))
            st.settle()
            st.then(dve.tensor_reduce(npass_f[:, 0:1], npass_f[:, 1:PASSES], AX.X, ALU.add))
            st.then(dve.tensor_scalar(npass_f[:, 0:1], npass_f[:, 0:1], 1.0, None, ALU.add))
            st.then(dve.tensor_copy(npass[:, :], npass_f[:, 0:1]), routed)
            dve.wait_ge(top_exp, 3)
            st.then(dve.tensor_reduce(sm[:, :, 1], e4[:, :, :], AX.X, ALU.add))
            st.then(dve.reciprocal(sm[:, :, 2], sm[:, :, 1]))
            st.then(dve.tensor_tensor(e4[:, :, :], e4[:, :, :], sm[:, :, 2:3].to_broadcast([P, 3, TOPK]), ALU.mult))
            st.then(dve.tensor_tensor(ohg.rearrange("p t (k e) -> p (t k) e", e=NE), oh.rearrange("p t (k e) -> p (t k) e", e=NE),
                                      e4.rearrange("p t k -> p (t k)").unsqueeze(2).to_broadcast([P, 3 * TOPK, NE]), ALU.mult))
            st.then(dve.tensor_reduce(gates[:, :, :], ohg.rearrange("p t (k e) -> p t e k", e=NE), AX.X, ALU.add), gates_ready)
            dve.wait_ge(gather_full, 1)
            batch_out(0)
            dve.wait_ge(y_zeroed, 1)
            n_pass = dve.value_load(npass[0:1, 0:1], min_val=1, max_val=PASSES)
            with dve.Fori(0, n_pass) as r:
                with dve.Fori(0, NE // GROUP) as g:
                    for q in range(2):
                        pi = r * PAIRS + 2 * g + q
                        dve.wait_ge(gather_full, pi + 1)
                        make_pick(2 * pi + 2)
                        for j in range(2):
                            n, e = 2 * pi + j, GROUP * g + 2 * q + j
                            dve.wait_ge(w_used, PIECES * n + KT)
                            dve.tensor_scalar(g1[:, :], bank[0][:, :], LIMIT, None, ALU.min).then_inc(g1_ready, 1)
                            dve.tensor_scalar(l1[:, :], bank[1][:, :], LIMIT, -LIMIT, ALU.min, ALU.max).then_inc(l1_ready, 1)
                            dve.wait_ge(l1_ready, n + 1)
                            dve.scalar_tensor_tensor(l1[:, :], l1[:, :], 1.0, g1[:, :], ALU.add, ALU.mult).then_inc(t_done, 1)
                            dve.wait_ge(t_done, n + 1)
                            dve.wait_ge(sg_ready, n + 1)
                            dve.tensor_tensor(l1[:, :], l1[:, :], sg[:, :], ALU.mult).then_inc(act_ready, 1)
                            make_bsel(e + 1, 1 - j)
                            for t in range(3):
                                ins = dve.tensor_scalar(put[:, t, j * CAP:(j + 1) * CAP], io64[:, :], posm[:, t, bass.ds(n, 1)],
                                                        gates[:, t, bass.ds(e, 1)], ALU.is_equal, ALU.mult)
                            ins.then_inc(put_ready, 1)
                            if j == 0:
                                for c in range(6):
                                    add_pair(c, 6 * pi)
                        dve.wait_ge(gather_full, pi + 2)
                        batch_out(1 - q)
            for c in range(6):
                add_pair(c, n_pass * (6 * PAIRS))
            dve.wait_ge(y_added, n_pass * (6 * PAIRS) + 6)
            for t in range(3):
                n = rows[t]
                st.then(dve.scalar_tensor_tensor(Y[0:n, t, :], xt[0:n, t, :], ALPHA, Y[0:n, t, :], ALU.mult, ALU.add))
                row_stats(Y, t, n, ln2_stats)
            dve.wait_ge(ld_ln, 96)
            for t in range(3):
                n = rows[t]
                dve.wait_ge(y_hat, t + 1)
                st.then(dve.tensor_tensor(Y[0:n, t, :], Y[0:n, t, :], lnbc[0:n, 0, :], ALU.mult))
                st.do(dve.tensor_tensor(Y[0:n, t, :], Y[0:n, t, :], lnbc[0:n, 1, :], ALU.add), y_done)

        @block.tensor
        def _(pe):
            def job(name, emit):
                n = J[name]
                assert n == job.n, name
                job.n += 1
                if n >= 8:
                    copied(pe, JOBS[n - 8])
                emit(bk(name)).then_inc(bank_full, 1)

            job.n = 0

            def chain(out, pairs):
                for n, (a, b) in enumerate(pairs):
                    ins = pe.matmul(out, a, b, start=n == 0, stop=n == len(pairs) - 1)
                return ins

            def transposes(parts):
                for out, src, k in parts:
                    ins = pe.transpose(out, src, ident[0:k, 0:k])
                return ins

            pe.wait_ge(consts_ready, 1)
            pe.wait_ge(ld_lncol, 32)
            job("LNC", lambda b: transposes([(b[:, 0:16], lnrow[0:16, :], 16)]))

            def x_job(name, t, k0, nk, w):
                pe.wait_ge(xhat_ready, t + 1)
                job(name, lambda b: transposes([(b[:, k * w:(k + 1) * w], xt[0:w, t, (k0 + k) * P:(k0 + k + 1) * P], w)
                                                for k in range(nk)]))

            x_job("X0a", 0, 0, 4, P)
            x_job("X0b", 0, 4, 4, P)
            x_job("X1a", 1, 0, 4, P)
            x_job("X1b", 1, 4, 4, P)
            x_job("X2", 2, 0, 8, T2)
            for name in ("X0a", "X0b", "X1a", "X1b", "X2"):
                copied(pe, name)

            def project(name, block_, c, w, n):
                job(name, lambda b: chain(b[0:w, 0:n], [(win[block_][:, k, c:c + w], hT[:, k, 0:n]) for k in range(KT)]))

            def project_heads(name, c, n):
                def emit(b):
                    for k in range(KT):
                        for q in range(2):
                            cc = c + q * DK
                            ins = pe.matmul(b[64 * q:64 * q + 64, 0:n], win["qk"][:, k, cc:cc + 64], hT[:, k, 0:n],
                                            start=k == 0, stop=k == KT - 1)
                    return ins
                job(name, emit)

            def project_rows(name, t, c):
                c0 = cols[t][0]
                n = rows[t]
                job(name, lambda b: chain(b[0:n, 0:DC], [(hT[:, k, c0:c0 + n], win["vr"][:, k, c:c + DC]) for k in range(KT)]))

            pe.wait_ge(ld_win["z"], 16)
            project("Z", "z", 0, RANK, TALL)
            pe.wait_ge(ld_win["qk"], 16)
            project_heads("Q0", 0, TOUT)
            copied(pe, "Z")
            pe.wait_ge(ld_gate, 16 * 5)
            for p in range(2):
                def emit(b, p=p):
                    for q in range(2):
                        c = (2 * p + q) * DK
                        ins = pe.matmul(b[64 * q:64 * q + 64, 0:TALL], wg2[0:RANK, c:c + 64], zT[0:RANK, :], start=True, stop=True)
                    return ins
                job(f"G{p}", emit)
            project_heads("Q1", 2 * DK, TOUT)
            project_heads("K0", DQK, TALL)
            project_heads("K1", DQK + 2 * DK, TALL)
            pe.wait_ge(ld_packA, 16 * 7)
            job("SA", lambda b: transposes([(b[:, m * 40:(m + 1) * 40], packA[:, m * P:(m + 1) * P], 40) for m in range(MA)]))
            pe.wait_ge(ld_packB, 16 * 4)
            job("SB", lambda b: transposes([(b[:, m * 34:(m + 1) * 34], packB[:, m * P:(m + 1) * P], 34) for m in range(MB)]))
            pe.wait_ge(ld_packS, 16)
            job("SS", lambda b: transposes([(b[:, (2 * a + m) * 120:(2 * a + m + 1) * 120], packS[:, a, m * P:(m + 1) * P], 120)
                                            for a in range(2) for m in range(MB)]))
            pe.wait_ge(ld_win["xa"], 16)
            for m in range(MA):
                project(f"XA{m}", "xa", m * P, P, TALL)
            pe.wait_ge(ld_win["vbgb"], 16)
            for m in range(MB):
                project(f"GB{m}", "vbgb", DB + m * P, P, TALL)
                project(f"VB{m}", "vbgb", m * P, P, TALL)
            pe.wait_ge(ld_win["vr"], 16)
            def emit_vr2(b):
                for k in range(KT):
                    for q in range(2):
                        ins = pe.matmul(b[64 * q:64 * q + T2, 0:DC], hT[:, k, SEQ:TALL], win["vr"][:, k, q * DC:(q + 1) * DC],
                                        start=k == 0, stop=k == KT - 1)
                return ins
            job("VR2", emit_vr2)
            project_rows("V0", 0, 0)
            pe.wait_ge(xc_ready, MA)
            pe.wait_ge(ld_wbd, 16 * 20)
            for g, name in enumerate(("RG", "IG")):
                for m in range(MA):
                    ks = [k for k in range(MA) if abs(k - m) <= 1]
                    job(f"{name}{m}", lambda b: chain(b[:, 0:TALL], [(wbd[:, g, k, m * P:(m + 1) * P], xc[:, k, :]) for k in ks]))
            project_rows("V1", 1, 0)
            pe.wait_ge(ld_win["ga"], 16)
            for m in range(MA):
                project(f"GA{m}", "ga", m * P, P, TOUT)

            cols0 = [cols[0], cols[1], (2 * P, TALL)]

            def keys_job(c):
                n = rows0[c]
                job(f"KT{c}", lambda b: transposes([(b[0:n, p * P:(p + 1) * P], k_sb[:, p, cols0[c][0]:cols0[c][1]], P)
                                                    for p in range(2)]))

            def scores_jobs(c):
                c0, c1 = cols[c]
                n = rows[c]
                for o, par in enumerate("eo"):
                    def emit(b):
                        for p in range(2):
                            r = slice(64 * o, 64 * o + DK)
                            ins = pe.matmul(b[0:n, p * n:(p + 1) * n], kc[r, p, c0:c1], qc[r, p, c0:c1], start=True, stop=True)
                        return ins
                    job(f"SC{c}{par}", emit)

            def outputs_jobs(c):
                c0, c1 = cols[c]
                n = rows[c]
                copied(pe, f"SC{c}e")
                copied(pe, f"SC{c}o")
                for o, par in enumerate("eo"):
                    def emit(b):
                        for p in range(2):
                            h, r = 2 * p + o, slice(64 * o, 64 * o + DK)
                            out = b[0:n, p * DV:(p + 1) * DV]
                            s = sc[:, h, :] if c < 2 else sc2[0:SAMP, h, :]
                            pe.matmul(out, s, v_sb[0:n, c, h * DV:(h + 1) * DV], start=True, stop=False)
                            if c < 2:
                                ins = pe.matmul(out, q_sb[r, p, c0:c1], Sp[r, p, :], start=False, stop=True)
                            else:
                                for a in range(NSEQ):
                                    ins = pe.matmul(out, qm[r, p, a * SAMP:(a + 1) * SAMP], S0[r, p, a, :], start=False,
                                                    stop=a == NSEQ - 1)
                        return ins
                    job(f"O{c}{par}", emit)

            def state_job(name, c, r0, r1):
                copied(pe, f"KT{c}")

                def emit(b):
                    for h in range(NH):
                        base, p = head(h)
                        ins = pe.matmul(b[base:base + 64, p * DV:(p + 1) * DV], kT_sb[r0:r1, c, p, base:base + 64],
                                        v_sb[r0:r1, c, h * DV:(h + 1) * DV], start=True, stop=True)
                    return ins
                job(name, emit)

            def sample_state_jobs(p):
                pe.wait_ge(vm_ready, p + 1)
                for a in range(2):
                    def emit(b):
                        for q in range(2):
                            ins = pe.matmul(b[64 * q:64 * q + 64, 0:4 * DV], kT_sb[0:SAMP, 2, p, 64 * q:64 * q + 64],
                                            vm[0:SAMP, q, 4 * a:4 * a + 4, :], start=True, stop=True)
                        return ins
                    job(f"W{p}{a}", emit)

            def y_c_job(t, n_ready):
                pe.wait_ge(o_ready, n_ready)
                n = rows[t]
                job(f"YC{t}", lambda b: transposes([(b[:, k * P:k * P + n], o_sb[0:n, t, k * P:(k + 1) * P], n) for k in range(MC)]))

            pe.wait_ge(qk_decayed, 4)
            keys_job(2)
            scores_jobs(2)
            project_rows("R0", 0, DC)
            copied(pe, "VR2")
            state_job("STM", 2, SAMP, T2)
            keys_job(0)
            scores_jobs(0)
            project_rows("R1", 1, DC)
            copied(pe, "V0")
            copied(pe, "STM")
            outputs_jobs(0)
            keys_job(1)
            state_job("ST0", 0, 0, P)
            scores_jobs(1)
            pe.wait_ge(ld_S0, 16 * NH)
            outputs_jobs(2)
            pe.wait_ge(uc_ready, 1)
            job("MU", lambda b: chain(b[:, 0:TOUT], [(ones[:, :], uc[:, m, :]) for m in range(MB)]))
            pe.wait_ge(sq_ready, 1)
            job("VAR", lambda b: chain(b[:, 0:TOUT], [(ones[:, :], sgb[:, m, 0:TOUT]) for m in range(MB)]))
            copied(pe, "V1")
            copied(pe, "ST0")
            outputs_jobs(1)
            state_job("ST1", 1, 0, P)
            pe.wait_ge(outcols_ready, 2)
            job("OA", lambda b: transposes([(b[0:36, m * P:(m + 1) * P], oaT[:, m, :], P) for m in range(MA)]))
            job("OB", lambda b: transposes([(b[0:62, m * P:(m + 1) * P], obT[:, m, :], P) for m in range(MB)]))
            sample_state_jobs(0)
            y_c_job(2, 1)
            y_c_job(0, 2)
            sample_state_jobs(1)
            pe.wait_ge(ya_ready, MA)
            pe.wait_ge(yb_ready, MB)
            pe.wait_ge(ld_wout[0], 16)
            pe.wait_ge(ld_wout[1], 16)
            copied(pe, "YC2")

            def emit_p2(b):
                for k in range(KT):
                    for c in range(2):
                        ins = pe.matmul(b[64 * c:64 * c + SAMP, :], yT[:, k, SEQ:TOUT], wout[:, k, c * 512:(c + 1) * 512],
                                        start=k == 0, stop=k == KT - 1)
                return ins
            job("P2", emit_p2)
            y_c_job(1, 3)

            def p_jobs(t):
                copied(pe, f"YC{t}")
                for c in range(2):
                    job(f"P{t}{c}", lambda b: chain(b[:, :], [(yT[:, k, cols[t][0]:cols[t][1]], wout[:, k, c * 512:(c + 1) * 512])
                                                              for k in range(KT)]))

            def h_job(name, t, k0, nk, n_ready):
                pe.wait_ge(h1_ready, n_ready)
                w = rows[t]
                job(name, lambda b: transposes([(b[:, k * w:(k + 1) * w], xt[0:w, t, (k0 + k) * P:(k0 + k + 1) * P], w)
                                                for k in range(nk)]))

            def logits_job(t, *parts):
                for name in parts:
                    copied(pe, name)
                job(f"LG{t}", lambda b: chain(b[0:rows[t], 0:NE], [(hT[:, k, cols[t][0]:cols[t][1]], wr[:, k, :])
                                                                   for k in range(KT)]))

            p_jobs(0)
            pe.wait_ge(ld_router, 32)
            h_job("H2", 2, 0, 8, 1)
            logits_job(2, "H2")
            p_jobs(1)
            h_job("H0a", 0, 0, 4, 2)
            h_job("H0b", 0, 4, 4, 2)
            logits_job(0, "H0a", "H0b")
            h_job("H1a", 1, 0, 4, 3)
            h_job("H1b", 1, 4, 4, 3)
            logits_job(1, "H1a", "H1b")

            def places(b):
                for t in range(3):
                    chain(b[:, t * NE:(t + 1) * NE], [(ones[:, :], M[:, u, :]) for u in range(t)] + [(upper[:, :], M[:, t, :])])
                return chain(b[:, 3 * NE:4 * NE], [(ones[:, :], M[:, u, :]) for u in range(3)])
            pe.wait_ge(mask_ready, 3)
            job("POS", places)
            assert job.n == len(JOBS)
            for name in JOBS[-8:]:
                copied(pe, name)
            pe.wait_ge(ld_moe, 32)

            def gather():
                for k in range(KT):
                    out = bank[(2, 5)[k // 4]][:, (k % 4) * 2 * CAP:(k % 4 + 1) * 2 * CAP]
                    for t in range(3):
                        ins = pe.matmul(out, xt[:, t, k * P:(k + 1) * P], pick[:, t, :], start=t == 0, stop=t == 2)
                ins.then_inc(gather_full, 1)

            def combine(pi):
                pe.wait_ge(putT_ready, pi + 1)
                pe.wait_ge(out_ready, 4 * pi + 1)
                for c in range(6):
                    t, h = divmod(c, 2)
                    if c >= 2:
                        pe.wait_ge(y_added, 6 * pi + c - 1)
                    pe.matmul(bank[6 + c % 2][0:rows[t], :], putT[:, t * P:t * P + rows[t]], eout[:, h, :],
                              start=True, stop=True).then_inc(comb_full, 1)

            pe.wait_ge(pick_ready, 1)
            gather()
            pe.wait_ge(gates_ready, 1)
            for t in range(3):
                ins = pe.transpose(bank[3][0:NE, t * P:(t + 1) * P], gates[:, t, :], ident[:, :])
            ins.then_inc(putT_full, 1)
            pe.wait_ge(routed, 2)
            n_pass = pe.value_load(npass[0:1, 0:1], min_val=1, max_val=PASSES)
            with pe.Fori(0, n_pass) as r:
                with pe.Fori(0, NE // GROUP) as g:
                    uses = (r * (NE // GROUP) + g) * (GROUP * PIECES // SLOTS)
                    for q in range(2):
                        pi = r * PAIRS + 2 * g + q
                        for j in range(2):
                            n = 2 * pi + j

                            def slot_of(c):
                                k = (2 * q + j) * PIECES + c
                                pe.wait_ge(w_full[k % SLOTS], 16 * (uses + k // SLOTS + 1))
                                return k % SLOTS * SLOT

                            pe.wait_ge(bsel_ready, n + 1)
                            for b in range(2):
                                for h in range(2):
                                    c = (2 * b + h) * 512
                                    pe.matmul(bank[b][64 * h:64 * h + 64, :], bsel[:, j, :], b1_sb[:, c:c + 512],
                                              start=True, stop=False)
                            if j == 0:
                                pe.wait_ge(xT_ready, 2 * pi + 2)
                            for k in range(KT):
                                at_ = slot_of(k)
                                for b in range(2):
                                    for h in range(2):
                                        c = at_ + (2 * b + h) * 512
                                        ins = pe.matmul(bank[b][64 * h:64 * h + 64, :], xT[:, q, k, j * CAP:(j + 1) * CAP],
                                                        ring[:, c:c + 512], start=False, stop=k == KT - 1)
                                ins.then_inc(w_used, 1)
                            if j == 0:
                                combine(pi)
                            else:
                                pe.wait_ge(pick_ready, pi + 2)
                                gather()
                            pe.wait_ge(act_ready, n + 1)
                            for k in range(4):
                                ins = pe.transpose(bank[3][:, k * P:(k + 1) * P], l1[:, k * P:(k + 1) * P], ident[:, :])
                            ins.then_inc(actT_full, 1)
                            pe.wait_ge(actT_ready, n + 1)
                            if j == 1:
                                pe.wait_ge(put_ready, n + 1)
                                for t in range(3):
                                    ins = pe.transpose(bank[3][:, t * P:(t + 1) * P], put[:, t, :], ident[:, :])
                                ins.then_inc(putT_full, 1)
                                pe.wait_ge(out_ready, 2 * n + 1)
                            for k in range(KT):
                                if k % 2 == 0:
                                    at_ = slot_of(8 + k // 2)
                                for h in range(2):
                                    c = at_ + k % 2 * D + h * 512
                                    a = actT[:, k % 4, (k // 4) * CAP:(k // 4 + 1) * CAP]
                                    ins = pe.matmul(bank[4][64 * h:64 * h + 64, :], a, ring[:, c:c + 512],
                                                    start=k == 0, stop=k == KT - 1)
                                if k % 2 == 1:
                                    ins.then_inc(w_used, 1)
            combine(n_pass * PAIRS)


_INS = ["x_prompt", "x_sample", "state_conv_a", "state_rglru", "state_conv_b", "state_gla", "meta_tokens", "ln0_g", "ln0_b",
        "w_in", "conv_a_w", "conv_a_b", "w_rg", "b_rg", "w_ig", "b_ig", "lru_lambda", "conv_b_w", "conv_b_b", "ln_b_g",
        "ln_b_b", "w_gate2", "b_gate", "gla_norm_g", "w_out", "ln1_g", "ln1_b", "router_w", "router_b", "moe_w1",
        "moe_b1", "moe_w2", "moe_b2", "ln2_g", "ln2_b"]
_OUTS = [(1, SEQ, D), (NSEQ, DSEQ, D), (1, 1, WA - 1, DA), (1, 1, DA), (1, 1, WB - 1, DB), (1, 1, NH, DK, DV),
         (1, NSEQ, WA - 1, DA), (1, NSEQ, DA), (1, NSEQ, WB - 1, DB), (1, NSEQ, NH, DK, DV)]


def kernel(**inputs):
    import numpy as _np
    import concourse.bacc as _bacc
    from concourse.bass_utils import run_bass_kernel_spmd as _run

    nc = _bacc.Bacc("TRN2", target_bir_lowering=False, num_devices=1)
    arrays, args = {}, []
    for name in _INS:
        a = _np.ascontiguousarray(inputs[name])
        arrays[f"in_{name}_dram"] = a
        args.append(nc.dram_tensor(f"in_{name}_dram", a.shape, mybir.dt.from_np(a.dtype), kind="ExternalInput").ap())
    for i, shape in enumerate(_OUTS):
        args.append(nc.dram_tensor(f"out_{i}_dram", shape, F32, kind="ExternalOutput").ap())
    build_kernel(nc, *args)
    r = _run(nc, [arrays], core_ids=[0])
    return tuple(r.results[0][f"out_{i}_dram"] for i in range(len(_OUTS)))
```

```python
from contextlib import ExitStack

import concourse.bass as bass
from concourse import mybir
from concourse.alu_op_type import AluOpType as ALU

F32 = mybir.dt.float32
I32 = mybir.dt.int32
U32 = mybir.dt.uint32
ACT = mybir.ActivationFunctionType
AX = mybir.AxisListType

P = 128
D = 1024
KT = D // P
SEQ, META = 256, 16
NSEQ, DSEQ = 8, 4
SAMP = NSEQ * DSEQ
TOUT = SEQ + SAMP
TALL = TOUT + META
T2 = SAMP + META
DA, DB, DC = 384, 256, 384
MA, MB, MC = DA // P, DB // P, DC // P
WA, WB = 4, 31
BLK = 48
NH, DK, DV = 4, 48, 96
DQK = NH * DK
RANK = 16
TAU = 16.0
NE, TOPK = 32, 4
DF = 1024
LIMIT, SALPHA = 7.0, 1.702
ALPHA = 2.0 ** 0.25
EPS = 1e-5
RG_C = 8.0

C_XA, C_GA, C_VB, C_GB = 0, DA, 2 * DA, 2 * DA + DB
C_Q = 2 * DA + 2 * DB
C_K = C_Q + DQK
C_V = C_K + DQK
C_R = C_V + DC
C_Z = C_R + DC
DIN = C_Z + RANK

PIECES = 12
SLOTS = 16
GROUP = 4
SLOT = 2048
CAP = 64
PASSES = -(-TOUT // CAP)
PAIRS = NE // 2
TILES = (2, 0, 1)

JOBS = ["LNC", "X0a", "X0b", "X1a", "X1b", "X2", "Z", "Q0", "G0", "G1", "Q1", "K0", "K1", "SA", "SB", "SS",
        "XA0", "XA1", "XA2", "GB0", "VB0", "GB1", "VB1", "VR2", "V0", "RG0", "RG1", "RG2", "IG0", "IG1", "IG2",
        "V1", "GA0", "GA1", "GA2", "KT2", "SC2e", "SC2o", "R0", "STM", "KT0", "SC0e", "SC0o", "R1", "O0e", "O0o",
        "KT1", "ST0", "SC1e", "SC1o", "O2q", "O2s", "O1e", "O1o", "ST1", "OA", "OB", "MU", "W00", "W01", "VAR", "YC2",
        "YC0", "P2", "YC1", "W10", "W11", "P00", "P01", "H2", "LG2", "P10", "P11", "H0a", "H0b", "LG0",
        "H1a", "H1b", "LG1", "POS"]
J = {name: n for n, name in enumerate(JOBS)}


ST_OUT = 1 + 2 * NH + 4 + 1 + NSEQ


class Steps:

    def __init__(self, eng, own):
        self.eng, self.own, self.count, self.last = eng, own, {}, None

    def do(self, ins, sem=None):
        if isinstance(sem, tuple):
            ins.then_inc(sem[0], 1)
            self.last = sem
            return
        sem = self.own if sem is None else sem
        ins.then_inc(sem, 1)
        self.count[id(sem)] = self.count.get(id(sem), 0) + 1
        self.last = (sem, self.count[id(sem)])

    def settle(self):
        self.eng.wait_ge(*self.last)

    def then(self, ins, sem=None):
        self.do(ins, sem)
        self.settle()


def build_kernel(nc, x_prompt, x_sample, state_conv_a, state_rglru, state_conv_b, state_gla, meta_tokens, ln0_g, ln0_b,
                 w_in, conv_a_w, conv_a_b, w_rg, b_rg, w_ig, b_ig, lru_lambda, conv_b_w, conv_b_b, ln_b_g, ln_b_b,
                 w_gate2, b_gate, gla_norm_g, w_out, ln1_g, ln1_b, router_w, router_b, moe_w1, moe_b1, moe_w2, moe_b2,
                 ln2_g, ln2_b, y_prompt, y_sample, o_conv_a_p, o_rglru_p, o_conv_b_p, o_gla_p, o_conv_a_s, o_rglru_s,
                 o_conv_b_s, o_gla_s):
    with ExitStack() as ctx:
        def sb(name, shape, dt=F32):
            return ctx.enter_context(nc.sbuf_tensor(name, shape, dt))

        def sem(name):
            return ctx.enter_context(nc.semaphore(name))

        W_MEM = 44340
        ring = sb("ring", [P, W_MEM])
        xt = sb("xt", [P, 3, D])
        lnbc = sb("lnbc", [P, 2, D])
        hT = sb("hT", [P, KT, TALL])
        ident = sb("ident", [P, P])
        ones = sb("ones", [P, P])
        upper = sb("upper", [P, P])
        smask = sb("smask", [SAMP, SAMP])
        sseq = sb("sseq", [SAMP, NSEQ])
        stat = sb("stat", [P, 3, 2, 6])
        mv = sb("mv", [P, 3, 2])
        rst = sb("rst", [P, 3, 2])
        npass_f = sb("npass_f", [P, 8])
        npass = sb("npass", [P, 1], I32)
        wr = sb("wr", [P, KT, NE])
        rb = sb("rb", [P, NE])
        io32 = sb("io32", [P, NE])
        io64 = sb("io64", [P, CAP])
        selx = sb("selx", [P, NE + 1])
        r2 = sb("r2", [P, DC])
        iraw = r2[:, 0:CAP].bitcast(I32)
        valid = sb("valid", [P, 3])

        top = {"mixer": PIECES * SLOT, "moe": SLOTS * SLOT}

        def part(phase, *shape):
            n = 1
            for s in shape:
                n *= s
            a = top[phase]
            top[phase] = a + n
            assert top[phase] <= W_MEM, (phase, top[phase])
            v = ring[:, a:a + n]
            if len(shape) == 2:
                v = v.rearrange("p (a b) -> p a b", b=shape[1])
            if len(shape) == 3:
                v = v.rearrange("p (a b c) -> p a b c", b=shape[1], c=shape[2])
            return v

        colA = part("mixer", MA, 40)
        colB = part("mixer", MB, 34)
        lncol = part("mixer", 16)
        wbd_flat = part("mixer", 2 * MA * DA)
        wbd = wbd_flat.rearrange("p (g k c) -> p g k c", g=2, k=MA)
        o_sb = wbd_flat[:, 0:MC * DC].rearrange("p (t c) -> p t c", t=3)
        r_sb = wbd_flat[:, MC * DC:(MC + 2) * DC].rearrange("p (t c) -> p t c", t=2)
        tsq = part("mixer", MA, TALL)
        tsq_flat = tsq.rearrange("p a b -> p (a b)")
        cneg = part("mixer", 4, MA)
        uP = part("mixer", MB, WB - 1 + META + SEQ)
        uS = part("mixer", MB, NSEQ, WB - 1 + DSEQ)
        uc = part("mixer", MB, TOUT)
        sgb = part("mixer", MB, TALL)
        brst = part("mixer", TOUT)
        q_sb = part("mixer", 2, TOUT)
        k_sb = part("mixer", 2, TALL)
        gl = part("mixer", 2, TALL)
        zT = part("mixer", TALL)
        lnrow = zT[:, 0:P]
        eg = part("mixer", 2, 2 + NSEQ)
        assert top["mixer"] <= SLOTS * SLOT
        top["mixer"] = SLOTS * SLOT
        yT = part("mixer", KT, SEQ + 64)
        G = part("mixer", 2, TALL)
        qc = part("mixer", 2, TOUT)
        kc = part("mixer", 2, TOUT)
        qm = part("mixer", 2, NSEQ * (2 * SAMP + DSEQ))
        vm_at = top["mixer"] - 2 * TOUT * 2 - 2 * NSEQ * (2 * SAMP + DSEQ)
        vm = ring[:, vm_at:vm_at + 2 * NSEQ * DV].rearrange("p (q s e) -> p q s e", q=2, s=NSEQ)
        kT_sb = part("mixer", 3, 2, P)
        v_sb = part("mixer", 3, DC)
        sc = part("mixer", NH, P)
        sc2 = part("mixer", NH, SAMP)
        S0 = part("mixer", 2, NSEQ, DV)
        Sp = part("mixer", 2, DV)
        e_flat = part("mixer", 4 * TALL)
        E = [e_flat[:, n * 2 * TALL:(n + 1) * 2 * TALL].rearrange("p (a b) -> p a b", a=2) for n in range(2)]
        packA = e_flat[0:40, 0:DA]
        packB = e_flat[0:34, DA:DA + DB]
        packS = e_flat[0:120, DA + DB:DA + 3 * DB].rearrange("p (a b) -> p a b", a=2)
        wg2 = part("mixer", DQK + 16)
        bg = part("mixer", 2)
        gcol = part("mixer", 2, 8)
        gnorm = part("mixer", DV)
        rsq = part("mixer", 3, NH)
        rmask = part("mixer", TALL)
        packOA = e_flat[0:36, 0:DA]
        packOB = e_flat[0:62, DA:DA + DB]
        oaT = e_flat[:, DA + DB:DA + DB + MA * 36].rearrange("p (a b) -> p a b", a=MA)
        obT = e_flat[:, DA + DB + MA * 36:DA + DB + MA * 36 + MB * 62].rearrange("p (a b) -> p a b", a=MB)
        at = [10 * SLOT]

        def in_ring(*shape):
            n = 1
            for s in shape:
                n *= s
            a = at[0]
            at[0] += n
            assert at[0] <= PIECES * SLOT
            v = ring[:, a:a + n]
            if len(shape) == 2:
                return v.rearrange("p (a b) -> p a b", b=shape[1])
            return v.rearrange("p (a b c) -> p a b c", b=shape[1], c=shape[2])

        xaP = in_ring(MA, WA - 1 + META + SEQ)
        xaS = in_ring(MA, NSEQ, WA - 1 + DSEQ)
        xc = in_ring(MA, TALL)
        ra = in_ring(MA, TALL)
        iu = in_ring(MA, TALL)
        blocks = [("z", C_Z, RANK), ("qk", C_Q, 2 * DQK + 16), ("xa", C_XA, DA), ("vbgb", C_VB, 2 * DB),
                  ("vr", C_V, 2 * DC), ("ga", C_GA, DA)]
        last_job = {"z": "Z", "qk": "K1", "xa": "XA2", "vbgb": "VB1", "vr": "R1", "ga": "GA2"}
        placed = {name: (c0, n) for name, c0, n in blocks}
        win, spans, off = {}, [], 0
        for name in ("qk", "vr", "ga", "vbgb", "xa", "z"):
            n = placed[name][1]
            spans.append((off, off + KT * n, last_job[name]))
            win[name] = ring[:, off:off + KT * n].rearrange("p (k n) -> p k n", n=n)
            off += KT * n
        assert off <= 10 * SLOT

        def freed_by(a, b):
            return max((job for x, y, job in spans if x < b and a < y), key=J.get)

        wout = ring[:, 8 * SLOT:12 * SLOT].rearrange("p (k n) -> p k n", n=D)

        p2 = ring[:, vm_at:vm_at + D]
        Y = part("moe", 3, D)
        xT = hT.rearrange("p a b -> p (a b)")[:, 0:2 * KT * 2 * CAP].rearrange("p (q k c) -> p q k c", q=2, k=KT)
        pick = part("moe", 3, 2 * CAP)
        put = part("moe", 3, 2 * CAP)
        putT = part("moe", 3 * P)
        eout = part("moe", 2, 512)
        g1 = part("moe", 512)
        l1 = part("moe", 512)
        sg = part("moe", 512)
        actT = part("moe", 4, P)
        b1_sb = part("moe", 2 * DF)
        bsel = part("moe", 2, CAP)
        posm = part("moe", 3, PASSES * NE + 2)
        gates = part("moe", 3, NE)
        lg = part("moe", 3, NE)
        v8 = part("moe", 3, 8)
        i8 = part("moe", 3 * 8)
        i8u = i8.bitcast(U32).rearrange("p (a b) -> p a b", a=3)
        i8f = part("moe", 3, TOPK)
        e4 = part("moe", 3, TOPK)
        sm = part("moe", 3, 4)
        oh = part("moe", 3, TOPK * NE)
        ohg = part("moe", 3, TOPK * NE)
        M = part("moe", 3, NE)
        nmx = part("moe", 4)

        bank = [ctx.enter_context(nc.psum_tensor(f"bank{n}", [P, 512], F32)) for n in range(8)]

        bank_full = sem("bank_full")
        bank_read = [sem(f"bank_read{n}") for n in range(8)]
        dve_step, act_step, pool_step = sem("dve_step"), sem("act_step"), sem("pool_step")
        zeroed_x2 = sem("zeroed_x2")
        consts_ready = sem("consts_ready")
        ld_x = [sem(f"ld_x{t}") for t in range(3)]
        ld_ln = sem("ld_ln")
        ld_lncol = sem("ld_lncol")
        ld_packA, ld_packB, ld_packS = sem("ld_packA"), sem("ld_packB"), sem("ld_packS")
        ld_gate, ld_gnorm = sem("ld_gate"), sem("ld_gnorm")
        ld_wbd, ld_S0 = sem("ld_wbd"), sem("ld_S0")
        ld_win = {name: sem(f"ld_win_{name}") for name, _, _ in blocks}
        ld_wout = [sem("ld_wout0"), sem("ld_wout1")]
        ld_moe = sem("ld_moe")
        w_full = [sem(f"w_full{s}") for s in range(SLOTS)]
        w_used = sem("w_used")
        var_ready, std_ready = sem("var_ready"), sem("std_ready")
        ln0_stats, xhat_ready, h0_ready = sem("ln0_stats"), sem("xhat_ready"), sem("h0_ready")
        cleared = sem("cleared")
        colA_moved = sem("colA_moved")
        softplus_done, G_ready = sem("softplus_done"), sem("G_ready")
        exp_ready, exp_used = sem("exp_ready"), sem("exp_used")
        qk_decayed = sem("qk_decayed")
        eg_ready = sem("eg_ready")
        xc_ready, lam_in, lam_exp, lam_ready = sem("xc_ready"), sem("lam_in"), sem("lam_exp"), sem("lam_ready")
        rg_root_in, rg_root = sem("rg_root_in"), sem("rg_root")
        b_root, o_root_in, o_root = sem("b_root"), sem("o_root_in"), sem("o_root")
        a_ready, h_ready = sem("a_ready"), sem("h_ready")
        uc_ready, sq_ready, dn_ready, yb_ready = sem("uc_ready"), sem("sq_ready"), sem("dn_ready"), sem("yb_ready")
        rg_ready, S0_decayed = sem("rg_ready"), sem("S0_decayed")
        vm_ready, ya_ready, o_ready = sem("vm_ready"), sem("ya_ready"), sem("o_ready")
        outcols_ready = sem("outcols_ready")
        h1_ready = sem("h1_ready")
        top_ready, top_exp = sem("top_ready"), sem("top_exp")
        mask_ready, routed, y_started = sem("mask_ready"), sem("routed"), sem("y_started")
        gates_ready, counts_full = sem("gates_ready"), sem("counts_full")
        moe_consts, moe_cleared, ix_ready = sem("moe_consts"), sem("moe_cleared"), sem("ix_ready")
        ld_router = sem("ld_router")
        st_out, out_stored = sem("st_out"), sem("out_stored")
        pick_ready, bsel_ready, put_ready = sem("pick_ready"), sem("bsel_ready"), sem("put_ready")
        gather_full, xT_ready = sem("gather_full"), sem("xT_ready")
        g1_ready, l1_ready, t_done = sem("g1_ready"), sem("l1_ready"), sem("t_done")
        sg_ready, act_ready = sem("sg_ready"), sem("act_ready")
        actT_full, actT_ready = sem("actT_full"), sem("actT_ready")
        putT_full, putT_ready = sem("putT_full"), sem("putT_ready")
        out_ready = sem("out_ready")
        comb_full, y_added = sem("comb_full"), sem("y_added")
        ln2_stats, y_hat = sem("ln2_stats"), sem("y_hat")
        y_done = [sem(f"y_done{t}") for t in range(3)]

        def filled(eng, job):
            eng.wait_ge(bank_full, J[job] + 1)

        def copied(eng, job):
            eng.wait_ge(bank_read[J[job] % 8], J[job] // 8 + 1)

        def bk(job):
            return bank[J[job] % 8]

        def read_of(job):
            return bank_read[J[job] % 8], J[job] // 8 + 1

        block = ctx.enter_context(nc.Block())

        rows = [P, P, SAMP]
        rows0 = [P, P, T2]
        cols = [(0, P), (P, 2 * P), (2 * P, 2 * P + SAMP)]

        def head(h):
            return 64 * (h % 2), h // 2

        def w1_piece(e, s):
            return moe_w1[0, bass.ds(e, 1), s * P:(s + 1) * P, :].rearrange("a p c -> p (a c)")

        def w2_piece(e, s):
            r = (s - 8) * 2 * P
            return moe_w2[0, bass.ds(e, 1), r:r + 2 * P, :].rearrange("a (t p) c -> p (a t) c", p=P)

        @block.sync
        def _(sp):
            sp.dma_start(xt[:, 0, :], x_prompt[0, 0:P, :]).then_inc(ld_x[0], 16)
            sp.dma_start(xt[:, 1, :], x_prompt[0, P:2 * P, :]).then_inc(ld_x[1], 16)
            sp.dma_start(lnrow[0:8, :], ln0_g.rearrange("(k p) -> k p", p=P)).then_inc(ld_lncol, 16)
            sp.wait_ge(zeroed_x2, 1)
            sp.dma_start(xt[0:SAMP, 2, :], x_sample.rearrange("b t c -> (b t) c")).then_inc(ld_x[2], 16)
            sp.dma_start(xt[SAMP:T2, 2, :], meta_tokens).then_inc(ld_x[2], 16)
            def load_win(name):
                c0, n = placed[name]
                sp.dma_start(win[name], w_in[0, :, c0:c0 + n].rearrange("(k p) n -> p k n", p=P)).then_inc(ld_win[name], 16)

            sp.dma_start(lnrow[8:16, :], ln0_b.rearrange("(k p) -> k p", p=P)).then_inc(ld_lncol, 16)
            load_win("z")
            load_win("qk")
            sp.dma_start(packA[0:4, :], conv_a_w[0]).then_inc(ld_packA, 16)
            for n, a in enumerate((conv_a_b, b_rg, b_ig, lru_lambda)):
                sp.dma_start(packA[4 + n:5 + n, :], a).then_inc(ld_packA, 16)
            sp.dma_start(packA[8:16, :], state_rglru[0]).then_inc(ld_packA, 16)
            sp.dma_start(packA[16:40, :], state_conv_a[0].rearrange("s k c -> (s k) c")).then_inc(ld_packA, 16)
            load_win("xa")
            sp.dma_start(packB[0:WB, :], conv_b_w[0]).then_inc(ld_packB, 16)
            for n, a in enumerate((conv_b_b, ln_b_g, ln_b_b)):
                sp.dma_start(packB[WB + n:WB + n + 1, :], a).then_inc(ld_packB, 16)
            sp.dma_start(packS, state_conv_b[0].rearrange("(a s) k c -> (s k) a c", a=2)).then_inc(ld_packS, 16)
            load_win("vbgb")
            load_win("vr")
            load_win("ga")
            sp.dma_start(lnbc[:, 0, :], ln0_g.rearrange("(a c) -> a c", a=1).to_broadcast([P, D])).then_inc(ld_ln, 16)
            sp.dma_start(lnbc[:, 1, :], ln0_b.rearrange("(a c) -> a c", a=1).to_broadcast([P, D])).then_inc(ld_ln, 16)
            sp.dma_start(wr[:, :, :], router_w[0].rearrange("(k p) e -> p k e", p=P)).then_inc(ld_router, 16)
            sp.dma_start(rb[:, :], router_b.to_broadcast([P, NE])).then_inc(ld_router, 16)

            filled(sp, freed_by(8 * SLOT, 10 * SLOT))
            sp.dma_start(wout[:, 0:4, :], w_out[0, 0:4 * P, :].rearrange("(k p) n -> p k n", p=P)).then_inc(ld_wout[0], 16)
            w1_order = sorted(range(8), key=lambda s: J[freed_by(s * SLOT, (s + 1) * SLOT)])

            def load_first(s):
                filled(sp, freed_by(s * SLOT, (s + 1) * SLOT))
                sp.dma_start(ring[:, s * SLOT:(s + 1) * SLOT], moe_w1[0, 0, s * P:(s + 1) * P, :]).then_inc(w_full[s], 16)

            for s in w1_order[0:6]:
                load_first(s)
            sp.wait_ge(ya_ready, MA)
            sp.wait_ge(outcols_ready, 2)
            sp.dma_start(wout[:, 4:8, :], w_out[0, 4 * P:8 * P, :].rearrange("(k p) n -> p k n", p=P)).then_inc(ld_wout[1], 16)
            for s in w1_order[6:8]:
                load_first(s)
            sp.wait_ge(h0_ready, 3)
            sp.dma_start(lnbc[:, 0, :], ln1_g.to_broadcast([P, D])).then_inc(ld_ln, 16)
            sp.dma_start(lnbc[:, 1, :], ln1_b.to_broadcast([P, D])).then_inc(ld_ln, 16)
            filled(sp, "YC1")
            sp.wait_ge(yb_ready, MB)
            sp.wait_ge(S0_decayed, 2)
            copied(sp, "ST1")
            for s in range(PIECES, SLOTS):
                sp.dma_start(ring[:, s * SLOT:(s + 1) * SLOT], moe_w1[0, 1, (s - PIECES) * P:(s - PIECES + 1) * P, :]
                             ).then_inc(w_full[s], 16)
            sp.wait_ge(moe_cleared, 5)
            sp.dma_start(b1_sb[0:NE, :], moe_b1[0]).then_inc(ld_moe, 16)
            sp.dma_start(eout[0:NE, :, :], moe_b2[0].rearrange("e (h c) -> e h c", h=2)).then_inc(ld_moe, 16)
            filled(sp, "P11")
            for s in range(8, PIECES):
                sp.dma_start(ring[:, s * SLOT:(s + 1) * SLOT].rearrange("p (t c) -> p t c", t=2),
                             moe_w2[0, 0, (s - 8) * 2 * P:(s - 7) * 2 * P, :].rearrange("(t p) c -> p t c", p=P)
                             ).then_inc(w_full[s], 16)
            sp.wait_ge(h1_ready, 3)
            sp.dma_start(lnbc[:, 0, :], ln2_g.to_broadcast([P, D])).then_inc(ld_ln, 16)
            sp.dma_start(lnbc[:, 1, :], ln2_b.to_broadcast([P, D])).then_inc(ld_ln, 16)

            def load_group(e, n, first=0):
                for i in range(GROUP):
                    if (i + 1) * PIECES <= first:
                        continue
                    ei = e + i if isinstance(e, int) else sp.snap(e + i)
                    for c in range(PIECES):
                        k = i * PIECES + c
                        if k < first:
                            continue
                        s = k % SLOTS
                        src = w1_piece(ei, c) if c < 8 else w2_piece(ei, c)
                        dst = ring[:, s * SLOT:(s + 1) * SLOT]
                        if c >= 8:
                            dst = dst.rearrange("p (t c) -> p t c", t=2)
                        sp.wait_ge(w_used, PIECES * n + k - SLOTS + 1)
                        sp.dma_start(dst, src).then_inc(w_full[s], 16)

            load_group(0, 0, SLOTS)
            with sp.Fori(1, NE // GROUP) as g:
                load_group(GROUP * g, GROUP * g)
            sp.wait_ge(routed, 1)
            n_pass = sp.value_load(npass[0:1, 0:1], min_val=1, max_val=PASSES)
            with sp.If(n_pass > 1):
                with sp.Fori(1, n_pass) as r:
                    with sp.Fori(0, NE // GROUP) as g:
                        load_group(GROUP * g, NE * r + GROUP * g)
            for t in TILES:
                sp.wait_ge(y_done[t], 1)
                dst = y_prompt[0, t * P:(t + 1) * P, :] if t < 2 else y_sample.rearrange("b t c -> (b t) c")
                sp.dma_start(dst, Y[0:rows[t], t, :]).then_inc(out_stored, 16)
            sp.wait_ge(out_stored, 48)
            sp.wait_ge(st_out, 16 * ST_OUT)

        @block.gpsimd
        def _(pool):
            st = Steps(pool, pool_step)
            st.do(pool.memset(xt[:, 2, :], 0.0), zeroed_x2)
            st.do(pool.memset(ident[:, :], 0.0))
            st.do(pool.memset(ones[:, :], 1.0))
            st.do(pool.memset(bg[:, :], 0.0), cleared)
            st.then(pool.memset(wg2[:, :], 0.0))
            st.then(pool.affine_select(out=ident[:, :], in_=ident[:, :], compare_op=ALU.not_equal, fill=1.0, base=0,
                                       pattern=[[-1, P]], channel_multiplier=1), consts_ready)
            pool.dma_start(wg2[0:RANK, 0:DQK], w_gate2[0]).then_inc(ld_gate, 16)
            for h in range(NH):
                b, p = head(h)
                pool.dma_start(bg[b:b + DK, p:p + 1], b_gate[0, h * DK:(h + 1) * DK].rearrange("(a b) -> a b", b=1)
                               ).then_inc(ld_gate, 16)
            st.do(pool.memset(xaP[:, :, 0:WA - 1], 0.0), cleared)
            st.do(pool.memset(uP[:, :, 0:WB - 1], 0.0), cleared)
            st.do(pool.memset(qm[:, :, :], 0.0), cleared)
            st.do(pool.memset(yT[:, :, TOUT:], 0.0), cleared)
            st.do(pool.memset(S0[:, :, :, :], 0.0), cleared)
            st.do(pool.memset(wbd_flat[:, :], 0.0))
            st.then(pool.memset(rmask[:, :], 1.0), cleared)
            for g, w in enumerate((w_rg, w_ig)):
                for h in range(NH * 2):
                    r0 = h * BLK
                    while r0 < (h + 1) * BLK:
                        r1 = min((h + 1) * BLK, (r0 // P + 1) * P)
                        pool.dma_start(wbd[r0 % P:r0 % P + r1 - r0, g, r0 // P, h * BLK:(h + 1) * BLK],
                                       w[0, h, r0 - h * BLK:r1 - h * BLK, :]).then_inc(ld_wbd, 16)
                        r0 = r1
            for h in range(NH):
                b, p = head(h)
                pool.dma_start(S0[b:b + DK, p, :, :], state_gla[0, :, h, :, :].rearrange("s d e -> d s e")
                               ).then_inc(ld_S0, 16)
            pool.dma_start(gnorm[:, :], gla_norm_g[0:1, :].to_broadcast([P, DV])).then_inc(ld_gnorm, 16)
            st.do(pool.memset(rmask[:, 0:2 * P:P], 0.0), cleared)
            st.do(pool.memset(rmask[:, 2 * P:TOUT:DSEQ], 0.0), cleared)
            st.do(pool.memset(rmask[:, TOUT:TOUT + 1], 0.0), cleared)
            st.do(pool.memset(upper[:, :], 1.0))
            st.do(pool.memset(smask[:, :], 1.0))
            st.then(pool.memset(sseq[:, :], 1.0))
            st.do(pool.affine_select(out=upper[:, :], in_=upper[:, :], compare_op=ALU.is_ge, fill=0.0, base=0,
                                     pattern=[[1, P]], channel_multiplier=-1), consts_ready)
            v = smask[:, :].rearrange("p (a b) -> p a b", b=DSEQ)
            st.then(pool.affine_select(out=v, in_=v, compare_op=ALU.is_ge, fill=0.0, base=0,
                                       pattern=[[DSEQ, NSEQ], [1, DSEQ]], channel_multiplier=-1))
            st.do(pool.affine_select(out=v, in_=v, compare_op=ALU.is_ge, fill=0.0, base=0,
                                     pattern=[[-DSEQ, NSEQ], [0, DSEQ]], channel_multiplier=1), consts_ready)
            st.then(pool.affine_select(out=sseq[:, :], in_=sseq[:, :], compare_op=ALU.is_ge, fill=0.0, base=0,
                                       pattern=[[-DSEQ, NSEQ]], channel_multiplier=1))
            st.then(pool.affine_select(out=sseq[:, :], in_=sseq[:, :], compare_op=ALU.is_ge, fill=0.0, base=DSEQ - 1,
                                       pattern=[[DSEQ, NSEQ]], channel_multiplier=-1), consts_ready)
            st.then(pool.memset(valid[:, :], 1.0))
            st.then(pool.memset(valid[:, 2:3], 0.0))
            st.do(pool.memset(valid[0:SAMP, 2:3], 1.0), moe_consts)
            st.then(pool.iota(iraw[:, 0:CAP], pattern=[[1, CAP]], base=0, channel_multiplier=0))
            st.do(pool.tensor_copy(io64[:, :], iraw[:, 0:CAP]), moe_consts)
            st.do(pool.tensor_copy(io32[:, :], iraw[:, 0:NE]), moe_consts)
            st.do(pool.tensor_copy(selx[:, 0:NE], ident[:, 0:NE]), moe_consts)
            st.do(pool.tensor_copy(selx[:, NE:NE + 1], ident[:, 0:1]), moe_consts)
            pool.wait_ge(ld_ln, 32)
            for t in range(3):
                pool.wait_ge(xhat_ready, t + 1)
                for half in ("X%da" % t, "X%db" % t) if t < 2 else ("X2",):
                    filled(pool, half)
                n = rows0[t]
                st.then(pool.tensor_tensor(xt[0:n, t, :], xt[0:n, t, :], lnbc[0:n, 0, :], ALU.mult))
                st.do(pool.tensor_tensor(xt[0:n, t, :], xt[0:n, t, :], lnbc[0:n, 1, :], ALU.add), h0_ready)
            copied(pool, "SA")
            st.do(pool.tensor_copy(xaS[:, :, :, 0:WA - 1], colA[:, :, 16:40].rearrange("p m (s k) -> p m s k", k=WA - 1)),
                  colA_moved)
            copied(pool, "IG2")
            st.do(pool.tensor_tensor(iu[:, :, :], iu[:, :, :], xc[:, :, :], ALU.mult), ix_ready)
            pool.wait_ge(h_ready, 1)
            pool.wait_ge(qk_decayed, 4)
            st.do(pool.tensor_copy(oaT[:, :, 0:1], xc[:, :, META + SEQ - 1:META + SEQ]))
            st.do(pool.tensor_copy(oaT[:, :, 1:1 + NSEQ], xc[:, :, META + SEQ + DSEQ - 1:TALL:DSEQ]))
            st.do(pool.tensor_copy(oaT[:, :, 9:12], xaP[:, :, META + SEQ:META + SEQ + WA - 1]))
            st.do(pool.tensor_copy(oaT[:, :, 12:36].rearrange("p m (s k) -> p m s k", k=WA - 1), xaS[:, :, :, DSEQ:DSEQ + WA - 1]),
                  outcols_ready)
            st.do(pool.tensor_copy(obT[:, :, 0:WB - 1], uP[:, :, META + SEQ:META + SEQ + WB - 1]))
            st.do(pool.tensor_copy(obT[:, :, WB - 1:62].rearrange("p m (s k) -> p m s k", k=DSEQ), uS[:, :, :, WB - 1:WB - 1 + DSEQ]),
                  outcols_ready)
            pool.wait_ge(ld_gnorm, 16)
            copied(pool, "VR2")
            copied(pool, "R0")
            copied(pool, "R1")
            g4 = gnorm[:, :].unsqueeze(1)
            for t in range(3):
                r4 = (r_sb[:, t, :] if t < 2 else r2[0:SAMP, :]).rearrange("p (h e) -> p h e", e=DV)
                st.do(pool.tensor_tensor(r4, r4, g4[0:rows[t]].to_broadcast([rows[t], NH, DV]), ALU.mult), rg_ready)
            filled(pool, "O2q")
            pool.wait_ge(eg_ready, 1)

            def values_by_sequence(p):
                for q in range(2):
                    h = 2 * p + q
                    st.do(pool.tensor_tensor(vm[0:SAMP, q, :, :],
                                             v_sb[0:SAMP, 2, h * DV:(h + 1) * DV].unsqueeze(1).to_broadcast([SAMP, NSEQ, DV]),
                                             sseq[:, :].unsqueeze(2).to_broadcast([SAMP, NSEQ, DV]), ALU.mult),
                          vm_ready if q else None)

            values_by_sequence(0)
            for p in range(2):
                st.do(pool.tensor_tensor(S0[:, p, :, :], S0[:, p, :, :], eg[:, p, 2:].unsqueeze(2).to_broadcast([P, NSEQ, DV]),
                                         ALU.mult), S0_decayed)
            filled(pool, "W01")
            values_by_sequence(1)
            pool.dma_start(o_conv_b_s[0, :, 0:WB - 1 - DSEQ, :], state_conv_b[0, :, DSEQ:WB - 1, :]).then_inc(st_out, 16)
            copied(pool, "ST1")
            copied(pool, "W11")
            for h in range(NH):
                b, p = head(h)
                pool.dma_start(o_gla_p[0, 0, h, :, :], Sp[b:b + DK, p, :]).then_inc(st_out, 16)
                pool.dma_start(o_gla_s[0, :, h, :, :].rearrange("s d e -> d s e"), S0[b:b + DK, p, :, :]).then_inc(st_out, 16)
            copied(pool, "OA")
            pool.dma_start(o_rglru_p[0, :, :], packOA[0:1, :]).then_inc(st_out, 16)
            pool.dma_start(o_rglru_s[0, :, :], packOA[1:1 + NSEQ, :]).then_inc(st_out, 16)
            pool.dma_start(o_conv_a_p[0, 0, :, :], packOA[9:12, :]).then_inc(st_out, 16)
            pool.dma_start(o_conv_a_s[0].rearrange("s k c -> (s k) c"), packOA[12:36, :]).then_inc(st_out, 16)
            copied(pool, "OB")
            pool.dma_start(o_conv_b_p[0, 0, :, :], packOB[0:WB - 1, :]).then_inc(st_out, 16)
            for n in range(NSEQ):
                r = WB - 1 + n * DSEQ
                pool.dma_start(o_conv_b_s[0, n, WB - 1 - DSEQ:WB - 1, :], packOB[r:r + DSEQ, :]).then_inc(st_out, 16)
            pool.wait_ge(st_out, 16 * ST_OUT)
            filled(pool, "YC1")
            pool.wait_ge(h1_ready, 1)
            st.do(pool.memset(lg[:, 2, :], 0.0), moe_cleared)
            st.do(pool.memset(posm[:, :, PASSES * NE:], -1.0), moe_cleared)
            st.do(pool.memset(b1_sb[:, :], 0.0), moe_cleared)
            st.do(pool.memset(eout[:, :, :], 0.0), moe_cleared)
            st.do(pool.memset(putT[:, :], 0.0), moe_cleared)
            pool.wait_ge(h1_ready, 3)
            st.do(pool.tensor_scalar(Y[:, 0:2, :], xt[:, 0:2, :], ALPHA, None, ALU.mult))
            st.do(pool.tensor_scalar(Y[0:SAMP, 2, :], xt[0:SAMP, 2, :], ALPHA, None, ALU.mult), y_started)
            pool.wait_ge(ld_ln, 96)
            pool.wait_ge(y_hat, 1)
            st.then(pool.tensor_tensor(Y[0:SAMP, 2, :], Y[0:SAMP, 2, :], lnbc[0:SAMP, 0, :], ALU.mult))
            st.do(pool.tensor_tensor(Y[0:SAMP, 2, :], Y[0:SAMP, 2, :], lnbc[0:SAMP, 1, :], ALU.add), y_done[2])

        @block.scalar
        def _(act):
            st = Steps(act, act_step)

            def root(t, i, k):
                n = rows0[t]
                if k:
                    n = rows[t]
                act.wait_ge(var_ready, 3 * k + i + 1)
                st.do(act.activation(rst[0:n, t, 0:1], rst[0:n, t, 0:1], ACT.Sqrt), std_ready)

            for t in range(3):
                n = rows0[t]
                root(t, t, 0)
                act.wait_ge(ln0_stats, t + 1)
                st.do(act.activation(xt[0:n, t, :], xt[0:n, t, :], ACT.Identity, bias=rst[0:n, t, 1:2], scale=rst[0:n, t, 0:1]),
                      xhat_ready)
            copied(act, "LNC")
            for job, t, k0 in (("X0a", 0, 0), ("X1a", 1, 0)):
                filled(act, job)
                for k in range(4):
                    st.do(act.activation(hT[:, k0 + k, cols[t][0]:cols[t][1]], bk(job)[:, k * P:(k + 1) * P], ACT.Identity,
                                         bias=lncol[:, 8 + k0 + k:9 + k0 + k], scale=lncol[:, k0 + k:k0 + k + 1]),
                          read_of(job) if k == 3 else None)
            filled(act, "Z")
            st.do(act.activation(zT[0:RANK, :], bk("Z")[0:RANK, 0:TALL], ACT.Copy), read_of("Z"))
            filled(act, "Q0")
            st.do(act.activation(q_sb[:, 0, :], bk("Q0")[:, 0:TOUT], ACT.Copy, scale=DK ** -0.5), read_of("Q0"))
            copied(act, "G0")
            copied(act, "G1")
            st.then(act.activation(E[0], gl, ACT.Abs))
            st.then(act.activation(E[0], E[0], ACT.Exp, scale=-1.0))
            st.do(act.activation(E[0], E[0], ACT.Ln, bias=1.0), softplus_done)
            act.wait_ge(lam_in, 1)
            st.then(act.activation(cneg[:, 2, :], cneg[:, 2, :], ACT.Exp, scale=-1.0))
            st.do(act.activation(cneg[:, 2, :], cneg[:, 2, :], ACT.Ln, bias=1.0), lam_exp)
            filled(act, "Q1")
            st.do(act.activation(q_sb[:, 1, :], bk("Q1")[:, 0:TOUT], ACT.Copy, scale=DK ** -0.5), read_of("Q1"))
            for p in range(2):
                filled(act, f"K{p}")
                st.do(act.activation(k_sb[:, p, :], bk(f"K{p}")[:, 0:TALL], ACT.Copy), read_of(f"K{p}"))
            act.wait_ge(cleared, 10)
            filled(act, "SS")
            v = bk("SS")[:, 0:480].rearrange("p (a m s k) -> p a m s k", a=2, m=MB, k=WB - 1)
            for n in range(4):
                a, m = divmod(n, 2)
                st.do(act.activation(uS[:, m, 4 * a:4 * a + 4, 0:WB - 1], v[:, a, m, :, :], ACT.Copy),
                      read_of("SS") if n == 3 else None)
            for m in range(MA):
                b = bk(f"XA{m}")
                filled(act, f"XA{m}")
                st.do(act.activation(xaP[:, m, WA - 1:WA - 1 + META], b[:, TOUT:TALL], ACT.Copy))
                st.do(act.activation(xaP[:, m, WA - 1 + META:], b[:, 0:SEQ], ACT.Copy))
                st.do(act.activation(xaS[:, m, :, WA - 1:], b[:, SEQ:TOUT].rearrange("p (s t) -> p s t", t=DSEQ), ACT.Copy),
                      read_of(f"XA{m}"))
            act.wait_ge(G_ready, 1)
            it = 1.0 / TAU

            def exps(e, sign, biased, bias0, whole):
                for p in range(2):
                    for n, (c0, c1) in enumerate(biased):
                        st.do(act.activation(e[:, p, c0:c1], G[:, p, c0:c1], ACT.Exp, bias=gcol[:, p, bias0 + n:bias0 + n + 1],
                                             scale=sign * it))
                st.do(act.activation(e[:, :, whole[0]:whole[1]], G[:, :, whole[0]:whole[1]] if whole[2] is None else whole[2],
                                     ACT.Exp, scale=sign * it if whole[2] is None else it), exp_ready)

            exps(E[0], 1.0, cols[0:2], 0, (SEQ, TOUT, None))
            exps(E[1], -1.0, cols[0:2], 2, (SEQ, TOUT, None))
            act.wait_ge(exp_used, 1)
            st.do(act.activation(E[0][:, :, 0:TOUT], G[:, :, 0:TOUT], ACT.Exp, scale=it), exp_ready)
            st.do(act.activation(eg[:, :, 0:2], G[:, :, P - 1:2 * P:P], ACT.Exp, scale=it))
            st.do(act.activation(eg[:, :, 2:], G[:, :, SEQ + DSEQ - 1:TOUT:DSEQ], ACT.Exp, scale=it), eg_ready)
            act.wait_ge(exp_used, 2)
            exps(E[1], -1.0, cols[0:2] + [(TOUT, TALL)], 4, (SEQ, TOUT, gl[:, :, SEQ:TOUT]))
            for m in range(MB):
                filled(act, f"GB{m}")
                st.do(act.activation(sgb[:, m, :], bk(f"GB{m}")[:, 0:TALL], ACT.Sigmoid), read_of(f"GB{m}"))
            filled(act, "VR2")
            act.wait_ge(moe_consts, 5)
            st.do(act.activation(v_sb[0:T2, 2, :], bk("VR2")[0:T2, 0:DC], ACT.Copy))
            st.do(act.activation(r2[0:SAMP, :], bk("VR2")[64:64 + SAMP, 0:DC], ACT.Silu), read_of("VR2"))
            filled(act, "V0")
            st.do(act.activation(v_sb[:, 0, :], bk("V0")[:, 0:DC], ACT.Copy), read_of("V0"))
            for g, dst in (("RG", ra), ("IG", iu)):
                for m in range(MA):
                    filled(act, f"{g}{m}")
                    c = 5 if g == "RG" else 6
                    st.do(act.activation(dst[:, m, :], bk(f"{g}{m}")[:, 0:TALL], ACT.Sigmoid, bias=colA[:, m, c:c + 1]),
                          read_of(f"{g}{m}"))
            filled(act, "V1")
            st.do(act.activation(v_sb[:, 1, :], bk("V1")[:, 0:DC], ACT.Copy), read_of("V1"))
            act.wait_ge(lam_ready, 1)
            st.settle()
            for m in range(MA):
                st.do(act.activation(tsq[:, m, :], ra[:, m, :], ACT.Tanh, scale=cneg[:, 1, m:m + 1]))
            st.settle()
            for m in range(MA):
                st.do(act.activation(ra[:, m, :], ra[:, m, :], ACT.Exp, scale=cneg[:, 0, m:m + 1]), a_ready)
            act.wait_ge(rg_root_in, 1)
            st.do(act.activation(tsq[:, :, :], tsq[:, :, :], ACT.Sqrt), rg_root)

            def gelu(m):
                filled(act, f"GA{m}")
                st.do(act.activation(yT[:, m, 0:TOUT], bk(f"GA{m}")[:, 0:TOUT], ACT.Gelu_apprx_tanh), read_of(f"GA{m}"))

            def transposed_o(t):
                filled(act, f"YC{t}")
                st.do(act.activation(yT[:, MA + MB:, cols[t][0]:cols[t][1]],
                                     bk(f"YC{t}")[:, 0:MC * P].rearrange("p (k c) -> p k c", c=P)[:, :, 0:rows[t]], ACT.Copy),
                      read_of(f"YC{t}"))

            for m in range(MA):
                gelu(m)
            for t in range(2):
                filled(act, f"R{t}")
                st.do(act.activation(r_sb[0:rows[t], t, :], bk(f"R{t}")[0:rows[t], 0:DC], ACT.Silu), read_of(f"R{t}"))
            filled(act, "O2q")
            for o in range(2):
                st.do(act.activation(o_sb[0:SAMP, 2, :].rearrange("p (a b e) -> p a b e", b=2, e=DV)[:, :, o, :],
                                     bk("O2q")[o * SAMP:(o + 1) * SAMP, 0:2 * DV].rearrange("p (a e) -> p a e", a=2), ACT.Copy),
                      read_of("O2q") if o else None)
            for job, dst, n, w in (("OA", packOA, 36, DA), ("OB", packOB, 62, DB)):
                filled(act, job)
                st.do(act.activation(dst, bk(job)[0:n, 0:w], ACT.Copy), read_of(job))
            copied(act, "MU")
            st.do(act.activation(sgb[:, :, 0:TOUT], uc[:, :, :], ACT.Square), sq_ready)
            act.wait_ge(o_root_in, 1)
            st.do(act.activation(rsq[:, :, :], rsq[:, :, :], ACT.Sqrt), o_root)
            copied(act, "VAR")
            st.do(act.activation(brst[:, :], brst[:, :], ACT.Sqrt), b_root)
            transposed_o(2)
            transposed_o(0)
            act.wait_ge(dn_ready, 1)
            for m in range(MB):
                st.do(act.activation(yT[:, MA + m, 0:TOUT], uc[:, m, :], ACT.Silu, scale=colB[:, m, WB + 1:WB + 2],
                                     bias=colB[:, m, WB + 2:WB + 3]), yb_ready)
            transposed_o(1)
            filled(act, "P2")
            filled(act, "W11")
            st.do(act.activation(p2[0:SAMP, 0:512], bk("P2")[0:SAMP, :], ACT.Copy))
            st.do(act.activation(p2[0:SAMP, 512:D], bk("P2")[64:64 + SAMP, :], ACT.Copy), read_of("P2"))
            def transposed_h(job, t, k0, nk):
                filled(act, job)
                w = rows[t]
                st.do(act.activation(hT[:, k0:k0 + nk, cols[t][0]:cols[t][1]],
                                     bk(job)[:, 0:nk * w].rearrange("p (k c) -> p k c", c=w), ACT.Copy), read_of(job))

            def exp_top(n, t):
                act.wait_ge(top_ready, n + 1)
                st.do(act.activation(e4[:, t, :], v8[:, t, 0:TOPK], ACT.Exp, bias=sm[:, t, 0:1]), top_exp)

            root(2, 0, 1)
            transposed_h("H2", 2, 0, 8)
            root(0, 1, 1)
            transposed_h("H0a", 0, 0, 4)
            transposed_h("H0b", 0, 4, 4)
            root(1, 2, 1)
            transposed_h("H1a", 1, 0, 4)
            transposed_h("H1b", 1, 4, 4)
            for n, t in enumerate(TILES):
                exp_top(n, t)
            act.wait_ge(routed, 1)
            n_pass = act.value_load(npass[0:1, 0:1], min_val=1, max_val=PASSES)
            act.wait_ge(putT_full, 1)
            act.wait_ge(moe_cleared, 5)
            act.activation(putT[0:NE, 0:2 * P], bank[3][0:NE, 0:2 * P], ACT.Copy).then_inc(out_ready, 1)
            act.activation(putT[0:NE, 2 * P:3 * P], bank[3][0:NE, 2 * P:3 * P], ACT.Copy).then_inc(putT_ready, 1)
            with act.Fori(0, n_pass) as r:
                with act.Fori(0, NE // GROUP) as g:
                    for q in range(2):
                        pi = r * PAIRS + 2 * g + q
                        for j in range(2):
                            n = 2 * pi + j
                            act.wait_ge(g1_ready, n + 1)
                            act.activation(sg[:, :], g1[:, :], ACT.Sigmoid, scale=SALPHA).then_inc(sg_ready, 1)
                            act.wait_ge(actT_full, n + 1)
                            act.activation(actT[:, :, :], bank[3][:, :].rearrange("p (k c) -> p k c", c=P), ACT.Copy
                                           ).then_inc(actT_ready, 1)
                            if j == 1:
                                act.wait_ge(putT_full, pi + 2)
                                act.activation(putT[:, :], bank[3][:, 0:3 * P], ACT.Copy).then_inc(putT_ready, 1)
                            act.wait_ge(w_used, PIECES * n + PIECES)
                            for h in range(2):
                                act.activation(eout[64 * j:64 * j + 64, h, :], bank[4][64 * h:64 * h + 64, :], ACT.Copy
                                               ).then_inc(out_ready, 1)
            root(2, 0, 2)
            act.wait_ge(ln2_stats, 1)
            act.activation(Y[0:SAMP, 2, :], Y[0:SAMP, 2, :], ACT.Identity, bias=rst[0:SAMP, 2, 1:2], scale=rst[0:SAMP, 2, 0:1]
                           ).then_inc(y_hat, 1)
            root(0, 1, 2)
            root(1, 2, 2)

        @block.vector
        def _(dve):
            st = Steps(dve, dve_step)

            def row_stats(src, t, n, signal):
                for c in range(2):
                    st.do(dve.bn_stats(stat[0:n, t, c, :], src[0:n, t, c * 512:(c + 1) * 512]))
                st.settle()
                st.then(dve.bn_aggr(mv[0:n, t, :], stat[0:n, t, :, :].rearrange("p a b -> p (a b)")))
                st.do(dve.tensor_scalar(rst[0:n, t, 0:1], mv[0:n, t, 1:2], EPS, None, ALU.add), var_ready)
                dve.wait_ge(std_ready, st.count[id(var_ready)])
                st.then(dve.reciprocal(rst[0:n, t, 0:1], rst[0:n, t, 0:1]))
                st.do(dve.scalar_tensor_tensor(rst[0:n, t, 1:2], mv[0:n, t, 0:1], -1.0, rst[0:n, t, 0:1], ALU.mult, ALU.mult),
                      signal)

            def layer_norm(src, t, n, signal):
                for c in range(2):
                    st.do(dve.bn_stats(stat[0:n, t, c, :], src[0:n, t, c * 512:(c + 1) * 512]))
                st.settle()
                st.then(dve.bn_aggr(mv[0:n, t, :], stat[0:n, t, :, :].rearrange("p a b -> p (a b)")))
                st.do(dve.tensor_scalar(rst[0:n, t, 0:1], mv[0:n, t, 1:2], EPS, None, ALU.add), var_ready)
                st.do(dve.scalar_tensor_tensor(src[0:n, t, :], src[0:n, t, :], mv[0:n, t, 0:1], lnbc[0:n, 0, :],
                                               ALU.subtract, ALU.mult))
                dve.wait_ge(std_ready, st.count[id(var_ready)])
                st.then(dve.reciprocal(rst[0:n, t, 0:1], rst[0:n, t, 0:1]))
                st.do(dve.scalar_tensor_tensor(src[0:n, t, :], src[0:n, t, :], rst[0:n, t, 0:1], lnbc[0:n, 1, :],
                                               ALU.mult, ALU.add), signal)

            st.do(dve.memset(rsq[:, :, :], 1.0))
            for t in range(3):
                dve.wait_ge(ld_x[t], 16 if t < 2 else 32)
                row_stats(xt, t, rows0[t], ln0_stats)
            filled(dve, "LNC")
            st.then(dve.tensor_copy(lncol[:, :], bk("LNC")[:, 0:16]), read_of("LNC"))

            def scaled(job, t, k0, nk, w):
                filled(dve, job)
                c0 = cols[t][0]
                for k in range(nk):
                    st.do(dve.tensor_scalar(hT[:, k0 + k, c0:c0 + w], bk(job)[:, k * w:(k + 1) * w],
                                            lncol[:, k0 + k:k0 + k + 1], lncol[:, 8 + k0 + k:9 + k0 + k], ALU.mult, ALU.add),
                          read_of(job) if k == nk - 1 else None)

            scaled("X0b", 0, 4, 4, P)
            scaled("X1b", 1, 4, 4, P)
            scaled("X2", 2, 0, 8, T2)
            filled(dve, "SA")
            st.then(dve.tensor_copy(colA[:, :, :], bk("SA")[:, 0:MA * 40].rearrange("p (m c) -> p m c", m=MA)), read_of("SA"))
            filled(dve, "SB")
            st.then(dve.tensor_copy(colB[:, :, :], bk("SB")[:, 0:MB * 34].rearrange("p (m c) -> p m c", m=MB)), read_of("SB"))
            lam = colA[:, :, 7]
            st.then(dve.tensor_scalar(cneg[:, 3, :], lam, -1.0, 0.0, ALU.mult, ALU.max))
            st.do(dve.scalar_tensor_tensor(cneg[:, 2, :], cneg[:, 3, :], 2.0, lam, ALU.mult, ALU.add), lam_in)
            dve.wait_ge(ld_gate, 16 * 5)
            for p in range(2):
                filled(dve, f"G{p}")
                st.do(dve.tensor_scalar(gl[:, p, :], bk(f"G{p}")[:, 0:TALL], bg[:, p:p + 1], None, ALU.add), read_of(f"G{p}"))
            dve.wait_ge(softplus_done, 1)
            st.then(dve.scalar_tensor_tensor(gl[:, :, :], gl[:, :, :], 0.0, E[0], ALU.min, ALU.subtract))
            dve.wait_ge(cleared, 10)
            for p in range(2):
                st.do(dve.tensor_tensor_scan(G[:, p, :], rmask[:, :], gl[:, p, :], 0.0, ALU.mult, ALU.add))
            st.settle()
            it = 1.0 / TAU
            st.do(dve.tensor_scalar(gcol[:, :, 0:2], G[:, :, 63:192:P], -it, None, ALU.mult))
            st.do(dve.tensor_scalar(gcol[:, :, 2:4], G[:, :, 63:192:P], it, None, ALU.mult))
            st.do(dve.tensor_scalar(gcol[:, :, 4:6], G[:, :, P - 1:2 * P:P], it, None, ALU.mult))
            st.do(dve.tensor_scalar(gcol[:, :, 6:7], G[:, :, TALL - 1:TALL], it, None, ALU.mult))
            for p in range(2):
                last = G[:, p, SEQ + DSEQ - 1:TOUT:DSEQ]
                st.do(dve.tensor_tensor(gl[:, p, SEQ:TOUT].rearrange("p (s t) -> p s t", t=DSEQ),
                                        last.unsqueeze(2).to_broadcast([P, NSEQ, DSEQ]),
                                        G[:, p, SEQ:TOUT].rearrange("p (s t) -> p s t", t=DSEQ), ALU.subtract),
                      G_ready if p else None)
            dve.wait_ge(lam_exp, 1)
            st.then(dve.tensor_tensor(cneg[:, 2, :], cneg[:, 2, :], cneg[:, 3, :], ALU.add))
            st.do(dve.tensor_scalar(cneg[:, 0, :], cneg[:, 2, :], -RG_C, None, ALU.mult))
            st.do(dve.tensor_scalar(cneg[:, 1, :], cneg[:, 2, :], RG_C, None, ALU.mult), lam_ready)
            dve.wait_ge(colA_moved, 1)
            dve.wait_ge(cleared, 10)
            for m in range(MA):
                copied(dve, f"XA{m}")
                dp, ds_ = xc[:, m, 0:META + SEQ], xc[:, m, META + SEQ:].rearrange("p (s t) -> p s t", t=DSEQ)
                for k in range(WA):
                    w = colA[:, m, k:k + 1]
                    sp_, ss_ = xaP[:, m, k:k + META + SEQ], xaS[:, m, :, k:k + DSEQ]
                    if k == 0:
                        st.do(dve.tensor_scalar(dp, sp_, w, colA[:, m, 4:5], ALU.mult, ALU.add))
                        st.do(dve.tensor_scalar(ds_, ss_, w, colA[:, m, 4:5], ALU.mult, ALU.add))
                    else:
                        st.do(dve.scalar_tensor_tensor(dp, sp_, w, dp, ALU.mult, ALU.add))
                        st.do(dve.scalar_tensor_tensor(ds_, ss_, w, ds_, ALU.mult, ALU.add), xc_ready if k == WA - 1 else None)
                    st.settle()
            dve.wait_ge(exp_ready, 1)
            copied(dve, "Q0")
            copied(dve, "Q1")
            st.do(dve.tensor_tensor(qc[:, :, :], q_sb[:, :, :], E[0][:, :, 0:TOUT], ALU.mult), exp_used)
            dve.wait_ge(exp_ready, 2)
            copied(dve, "K0")
            copied(dve, "K1")
            st.then(dve.tensor_tensor(kc[:, :, :], k_sb[:, :, 0:TOUT], E[1][:, :, 0:TOUT], ALU.mult), exp_used)
            dve.wait_ge(exp_ready, 3)
            st.then(dve.tensor_tensor(q_sb[:, :, :], q_sb[:, :, :], E[0][:, :, 0:TOUT], ALU.mult), qk_decayed)
            for p in range(2):
                for h in range(2):
                    r = slice(64 * h, 64 * h + DK)
                    st.do(dve.tensor_copy(qm[r, p, :].rearrange("p (s c) -> p s c", s=NSEQ)[:, :, h * SAMP:h * SAMP + DSEQ],
                                          q_sb[r, p, SEQ:TOUT].rearrange("p (s t) -> p s t", t=DSEQ)),
                          qk_decayed if h else None)
            dve.wait_ge(exp_ready, 4)
            st.then(dve.tensor_tensor(k_sb[:, :, :], k_sb[:, :, :], E[1], ALU.mult), qk_decayed)
            for m in range(MB):
                b = bk(f"VB{m}")
                filled(dve, f"VB{m}")
                copied(dve, f"GB{m}")
                st.do(dve.tensor_tensor(uP[:, m, WB - 1:WB - 1 + META], b[:, TOUT:TALL], sgb[:, m, TOUT:TALL], ALU.mult))
                st.do(dve.tensor_tensor(uP[:, m, WB - 1 + META:], b[:, 0:SEQ], sgb[:, m, 0:SEQ], ALU.mult))
                st.do(dve.tensor_tensor(uS[:, m, :, WB - 1:], b[:, SEQ:TOUT].rearrange("p (s t) -> p s t", t=DSEQ),
                                        sgb[:, m, SEQ:TOUT].rearrange("p (s t) -> p s t", t=DSEQ), ALU.mult), read_of(f"VB{m}"))
            st.settle()

            def taps(k0, k1):
                for k in range(k0, k1):
                    for m in range(MB):
                        src, w = uP[:, m, META + k:META + k + SEQ], colB[:, m, k:k + 1]
                        if k == 0:
                            st.do(dve.tensor_scalar(uc[:, m, 0:SEQ], src, w, colB[:, m, WB:WB + 1], ALU.mult, ALU.add))
                        else:
                            if m == 0:
                                st.settle()
                            st.do(dve.scalar_tensor_tensor(uc[:, m, 0:SEQ], src, w, uc[:, m, 0:SEQ], ALU.mult, ALU.add),
                                  uc_ready if (k, m) == (WB - 1, MB - 1) else None)
                st.settle()

            copied(dve, "SS")
            st.settle()
            for m in range(MB):
                for t in range(DSEQ):
                    prod = brst[:, 0:NSEQ * WB].rearrange("p (s k) -> p s k", k=WB)
                    st.then(dve.tensor_tensor(prod, uS[:, m, :, t:t + WB],
                                              colB[:, m, 0:WB].unsqueeze(1).to_broadcast([P, NSEQ, WB]), ALU.mult))
                    st.then(dve.tensor_reduce(uc[:, m, SEQ + t:TOUT:DSEQ], prod, AX.X, ALU.add))
                st.do(dve.tensor_scalar(uc[:, m, SEQ:TOUT], uc[:, m, SEQ:TOUT], colB[:, m, WB:WB + 1], None, ALU.add))
            taps(0, 20)
            dve.wait_ge(ix_ready, 1)
            dve.wait_ge(a_ready, MA)
            st.then(dve.tensor_tensor(xc[:, :, :], ra[:, :, :], ra[:, :, :], ALU.mult))
            st.then(dve.scalar_tensor_tensor(tsq[:, :, :], xc[:, :, :], 1.0, tsq[:, :, :], ALU.add, ALU.mult), rg_root_in)
            taps(20, 23)
            dve.wait_ge(rg_root, 1)
            st.then(dve.tensor_tensor(iu[:, :, :], iu[:, :, :], tsq[:, :, :], ALU.mult))
            starts = slice(META + SEQ, TALL, DSEQ)
            st.then(dve.tensor_tensor(tsq[:, :, 0:NSEQ], ra[:, :, starts], colA[:, :, 8:16], ALU.mult))
            st.then(dve.tensor_tensor(iu[:, :, starts], iu[:, :, starts], tsq[:, :, 0:NSEQ], ALU.add))
            st.do(dve.memset(ra[:, :, starts], 0.0))
            st.then(dve.memset(ra[:, :, 0:1], 0.0))
            st.then(dve.tensor_tensor_scan(xc.rearrange("p m t -> p (m t)"), ra.rearrange("p m t -> p (m t)"),
                                           iu.rearrange("p m t -> p (m t)"), 0.0, ALU.mult, ALU.add), h_ready)

            def keys_out(c):
                filled(dve, f"KT{c}")
                n = rows0[c]
                st.do(dve.tensor_copy(kT_sb[0:n, c, :, :], bk(f"KT{c}")[0:n, 0:2 * P].rearrange("p (a b) -> p a b", a=2)),
                      read_of(f"KT{c}"))

            def scores_out(c):
                for par, o in (("e", 0), ("o", 1)):
                    job = f"SC{c}{par}"
                    filled(dve, job)
                    if c < 2:
                        dst = sc[:, o::2, :]
                        src = bk(job)[:, 0:2 * P].rearrange("p (a b) -> p a b", a=2)
                        msk = upper[:, :].unsqueeze(1).to_broadcast([P, 2, P])
                    else:
                        dst = sc2[0:SAMP, o::2, :]
                        src = bk(job)[0:SAMP, 0:2 * SAMP].rearrange("p (a b) -> p a b", a=2)
                        msk = smask[:, :].unsqueeze(1).to_broadcast([SAMP, 2, SAMP])
                    st.do(dve.tensor_tensor(dst, src, msk, ALU.mult), read_of(job))

            def state_out(job, c):
                filled(dve, job)
                for p in range(2):
                    src = bk(job)[:, p * DV:(p + 1) * DV]
                    if c is None:
                        ins = dve.tensor_copy(Sp[:, p, :], src)
                    else:
                        ins = dve.scalar_tensor_tensor(Sp[:, p, :], Sp[:, p, :], eg[:, p, c:c + 1], src, ALU.mult, ALU.add)
                    st.do(ins, read_of(job) if p else None)

            def outputs_out(c):
                n = rows[c]
                if c == 2:
                    copied(dve, "O2q")
                    filled(dve, "O2s")
                    st.do(dve.tensor_tensor(o_sb[0:n, c, :], o_sb[0:n, c, :], bk("O2s")[0:n, 0:DC], ALU.add), read_of("O2s"))
                    return
                for par, o in (("e", 0), ("o", 1)):
                    job = f"O{c}{par}"
                    filled(dve, job)
                    st.do(dve.tensor_copy(o_sb[0:n, c, :].rearrange("p (a b e) -> p a b e", b=2, e=DV)[:, :, o, :],
                                          bk(job)[0:n, 0:2 * DV].rearrange("p (a e) -> p a e", a=2)), read_of(job))

            def mean_squares(c):
                n = rows[c]
                o4 = o_sb[0:n, c, :].rearrange("p (h e) -> p h e", e=DV)
                v4 = tsq_flat[0:n, 0:DC].rearrange("p (h e) -> p h e", e=DV)
                st.then(dve.tensor_tensor(v4, o4, o4, ALU.mult))
                st.then(dve.tensor_reduce(rsq[0:n, c, :], v4, AX.X, ALU.add))

            def finish_outputs(c):
                n = rows[c]
                o4 = o_sb[0:n, c, :].rearrange("p (h e) -> p h e", e=DV)
                st.then(dve.tensor_tensor(o4, o4, rsq[0:n, c, :].unsqueeze(2).to_broadcast([n, NH, DV]), ALU.mult))
                st.do(dve.tensor_tensor(o_sb[0:n, c, :], o_sb[0:n, c, :], r_sb[0:n, c, :] if c < 2 else r2[0:n, :], ALU.mult), o_ready)

            def sample_state_out(p):
                for a in range(2):
                    job = f"W{p}{a}"
                    filled(dve, job)
                    v = S0[:, p, 4 * a:4 * a + 4, :]
                    st.do(dve.tensor_tensor(v, v, bk(job)[:, 0:4 * DV].rearrange("p (s e) -> p s e", e=DV), ALU.add),
                          read_of(job))

            keys_out(2)
            dve.wait_ge(consts_ready, 4)
            scores_out(2)
            for m in range(MA):
                copied(dve, f"GA{m}")
                st.do(dve.tensor_tensor(yT[:, m, 0:TOUT], yT[:, m, 0:TOUT], xc[:, m, META:], ALU.mult), ya_ready)
            st.settle()
            state_out("STM", None)
            keys_out(0)
            scores_out(0)
            taps(23, 25)
            dve.wait_ge(eg_ready, 1)
            outputs_out(0)
            keys_out(1)
            state_out("ST0", 0)
            scores_out(1)
            taps(25, WB)
            outputs_out(1)
            outputs_out(2)
            st.settle()
            mean_squares(0)
            filled(dve, "MU")
            for m in range(MB):
                st.do(dve.scalar_tensor_tensor(uc[:, m, :], bk("MU")[:, 0:TOUT], -1.0 / DB, uc[:, m, :], ALU.mult, ALU.add),
                      read_of("MU") if m else None)
            mean_squares(2)
            mean_squares(1)
            st.then(dve.tensor_scalar(rsq[:, :, :], rsq[:, :, :], 1.0 / DV, EPS, ALU.mult, ALU.add), o_root_in)
            state_out("ST1", 1)
            filled(dve, "VAR")
            st.do(dve.tensor_scalar(brst[:, :], bk("VAR")[:, 0:TOUT], 1.0 / DB, EPS, ALU.mult, ALU.add), read_of("VAR"))
            dve.wait_ge(o_root, 1)
            st.then(dve.reciprocal(rsq[:, :, :], rsq[:, :, :]))
            dve.wait_ge(rg_ready, 3)
            finish_outputs(2)
            finish_outputs(0)
            dve.wait_ge(b_root, 1)
            st.then(dve.reciprocal(brst[:, :], brst[:, :]))
            st.do(dve.tensor_tensor(uc[:, :, :], uc[:, :, :], brst[:, :].unsqueeze(1).to_broadcast([P, MB, TOUT]), ALU.mult),
                  dn_ready)
            finish_outputs(1)
            dve.wait_ge(S0_decayed, 2)
            sample_state_out(0)
            sample_state_out(1)

            def ln1(i, t):
                n = rows[t]
                dve.wait_ge(h0_ready, t + 1)
                if t == 2:
                    copied(dve, "P2")
                    st.do(dve.scalar_tensor_tensor(xt[0:n, t, :], xt[0:n, t, :], ALPHA, p2[0:n, :], ALU.mult, ALU.add))
                else:
                    for c in range(2):
                        job, w = f"P{t}{c}", slice(c * 512, (c + 1) * 512)
                        filled(dve, job)
                        st.do(dve.scalar_tensor_tensor(xt[0:n, t, w], xt[0:n, t, w], ALPHA, bk(job)[0:n, :], ALU.mult, ALU.add),
                              read_of(job))
                st.settle()
                dve.wait_ge(ld_ln, 64)
                layer_norm(xt, t, n, h1_ready)

            def top(t):
                n = rows[t]
                filled(dve, f"LG{t}")
                st.then(dve.tensor_tensor(lg[0:n, t, :], bk(f"LG{t}")[0:n, 0:NE], rb[0:n, :], ALU.add), read_of(f"LG{t}"))
                st.then(dve.max(v8[:, t, :], lg[:, t, :]))
                st.do(dve.tensor_scalar(sm[:, t, 0:1], v8[:, t, 0:1], -1.0, None, ALU.mult), top_ready)
                st.then(dve.max_index(i8u[:, t, :], v8[:, t, :], lg[:, t, :]))
                st.then(dve.tensor_copy(i8f[:, t, :], i8u[:, t, 0:TOPK]))
                st.then(dve.tensor_tensor(oh[:, t, :].rearrange("p (k e) -> p k e", e=NE),
                                          io32[:, :].unsqueeze(1).to_broadcast([P, TOPK, NE]),
                                          i8f[:, t, :].unsqueeze(2).to_broadcast([P, TOPK, NE]), ALU.is_equal))
                st.then(dve.tensor_reduce(M[:, t, :], oh[:, t, :].rearrange("p (k e) -> p e k", e=NE), AX.X, ALU.add))
                st.do(dve.tensor_scalar(M[:, t, :], M[:, t, :], valid[:, t:t + 1], None, ALU.mult), mask_ready)

            def make_bsel(e, j):
                dve.tensor_scalar(bsel[:, j, :], ones[:, 0:CAP], selx[:, bass.ds(e, 1)], None, ALU.mult).then_inc(bsel_ready, 1)

            ln1(0, 2)
            ln1(1, 0)
            dve.wait_ge(moe_cleared, 2)
            dve.wait_ge(moe_consts, 5)
            dve.wait_ge(ld_router, 32)
            make_bsel(0, 0)
            top(2)
            ln1(2, 1)
            top(0)
            top(1)
            def make_pick(m):
                for j in range(2):
                    for t in range(3):
                        ins = dve.tensor_scalar(pick[:, t, j * CAP:(j + 1) * CAP], io64[:, :], posm[:, t, bass.ds(m + j, 1)], None,
                                                ALU.is_equal)
                ins.then_inc(pick_ready, 1)

            def batch_out(parity, b):
                dve.tensor_copy(xT[:, parity, 4 * b:4 * b + 4, :], bank[(2, 5)[b]][:, :].rearrange("p (k c) -> p k c", c=2 * CAP)
                                ).then_inc(xT_ready, 1)

            def add_pair(q, n_before):
                t, c = TILES[q // 2], q % 2
                dst = Y[0:rows[t], t, c * 512:(c + 1) * 512]
                dve.wait_ge(comb_full, n_before + q + 1)
                dve.tensor_tensor(dst, dst, bank[6 + q % 2][0:rows[t], :], ALU.add).then_inc(y_added, 1)

            dve.wait_ge(top_exp, 3)
            st.then(dve.tensor_reduce(sm[:, :, 1], e4[:, :, :], AX.X, ALU.add))
            st.then(dve.reciprocal(sm[:, :, 2], sm[:, :, 1]))
            st.then(dve.tensor_tensor(e4[:, :, :], e4[:, :, :], sm[:, :, 2:3].to_broadcast([P, 3, TOPK]), ALU.mult))
            st.then(dve.tensor_tensor(ohg.rearrange("p t (k e) -> p (t k) e", e=NE), oh.rearrange("p t (k e) -> p (t k) e", e=NE),
                                      e4.rearrange("p t k -> p (t k)").unsqueeze(2).to_broadcast([P, 3 * TOPK, NE]), ALU.mult))
            st.do(dve.tensor_reduce(gates[:, :, :], ohg.rearrange("p t (k e) -> p t e k", e=NE), AX.X, ALU.add), gates_ready)
            filled(dve, "POS")
            st.settle()
            place = ohg[:, 0, 0:3 * NE].rearrange("p (t e) -> p t e", e=NE)
            st.then(dve.tensor_tensor(place, bk("POS")[:, 0:3 * NE].rearrange("p (t e) -> p t e", e=NE), M[:, :, :], ALU.mult))
            for r in range(PASSES):
                st.do(dve.tensor_scalar(posm[:, :, r * NE:(r + 1) * NE], place, -1.0 - CAP * r, None, ALU.add))
                if r == 0:
                    st.settle()
                    make_pick(0)
            dve.wait_ge(counts_full, 1)
            st.then(dve.reduce_max(nmx[:, 0:1], bank[4][:, 0:NE], AX.X))
            for r in range(1, PASSES):
                st.do(dve.tensor_scalar(npass_f[:, r:r + 1], nmx[:, 0:1], float(CAP * r), None, ALU.is_gt))
            st.settle()
            st.then(dve.tensor_reduce(npass_f[:, 0:1], npass_f[:, 1:PASSES], AX.X, ALU.add))
            st.then(dve.tensor_scalar(npass_f[:, 0:1], npass_f[:, 0:1], 1.0, None, ALU.add))
            st.then(dve.tensor_copy(npass[:, :], npass_f[:, 0:1]), routed)
            dve.wait_ge(gather_full, 1)
            batch_out(0, 0)
            dve.wait_ge(y_started, 1)
            n_pass = dve.value_load(npass[0:1, 0:1], min_val=1, max_val=PASSES)
            with dve.Fori(0, n_pass) as r:
                with dve.Fori(0, NE // GROUP) as g:
                    for q in range(2):
                        pi = r * PAIRS + 2 * g + q
                        dve.wait_ge(gather_full, 2 * pi + 2)
                        batch_out(q, 1)
                        make_pick(2 * pi + 2)
                        for j in range(2):
                            n, e = 2 * pi + j, GROUP * g + 2 * q + j
                            dve.wait_ge(w_used, PIECES * n + KT)
                            dve.tensor_scalar(g1[:, :], bank[0][:, :], LIMIT, None, ALU.min).then_inc(g1_ready, 1)
                            dve.tensor_scalar(l1[:, :], bank[1][:, :], LIMIT, -LIMIT, ALU.min, ALU.max).then_inc(l1_ready, 1)
                            dve.wait_ge(l1_ready, n + 1)
                            dve.scalar_tensor_tensor(l1[:, :], l1[:, :], 1.0, g1[:, :], ALU.add, ALU.mult).then_inc(t_done, 1)
                            dve.wait_ge(t_done, n + 1)
                            dve.wait_ge(sg_ready, n + 1)
                            dve.tensor_tensor(l1[:, :], l1[:, :], sg[:, :], ALU.mult).then_inc(act_ready, 1)
                            make_bsel(e + 1, 1 - j)
                            for t in range(3):
                                ins = dve.tensor_scalar(put[:, t, j * CAP:(j + 1) * CAP], io64[:, :], posm[:, t, bass.ds(n, 1)],
                                                        gates[:, t, bass.ds(e, 1)], ALU.is_equal, ALU.mult)
                            ins.then_inc(put_ready, 1)
                            if j == 0:
                                for c in range(6):
                                    add_pair(c, 6 * pi)
                        dve.wait_ge(gather_full, 2 * pi + 3)
                        batch_out(1 - q, 0)
            dve.wait_ge(ld_ln, 96)
            for i, t in enumerate(TILES):
                for c in range(2):
                    add_pair(2 * i + c, n_pass * (6 * PAIRS))
                dve.wait_ge(y_added, n_pass * (6 * PAIRS) + 2 * i + 2)
                if t == 2:
                    row_stats(Y, t, rows[t], ln2_stats)
                else:
                    layer_norm(Y, t, rows[t], y_done[t])

        @block.tensor
        def _(pe):
            def job(name, emit):
                n = J[name]
                assert n == job.n, name
                job.n += 1
                if n >= 8:
                    copied(pe, JOBS[n - 8])
                emit(bk(name)).then_inc(bank_full, 1)

            job.n = 0

            def chain(out, pairs):
                for n, (a, b) in enumerate(pairs):
                    ins = pe.matmul(out, a, b, start=n == 0, stop=n == len(pairs) - 1)
                return ins

            def transposes(parts):
                for out, src, k in parts:
                    ins = pe.transpose(out, src, ident[0:k, 0:k])
                return ins

            pe.wait_ge(consts_ready, 1)
            pe.wait_ge(ld_lncol, 32)
            job("LNC", lambda b: transposes([(b[:, 0:16], lnrow[0:16, :], 16)]))

            def x_job(name, t, k0, nk, w):
                pe.wait_ge(xhat_ready, t + 1)
                job(name, lambda b: transposes([(b[:, k * w:(k + 1) * w], xt[0:w, t, (k0 + k) * P:(k0 + k + 1) * P], w)
                                                for k in range(nk)]))

            x_job("X0a", 0, 0, 4, P)
            x_job("X0b", 0, 4, 4, P)
            x_job("X1a", 1, 0, 4, P)
            x_job("X1b", 1, 4, 4, P)
            x_job("X2", 2, 0, 8, T2)
            for name in ("X0a", "X0b", "X1a", "X1b", "X2"):
                copied(pe, name)

            def project(name, block_, c, w, n):
                job(name, lambda b: chain(b[0:w, 0:n], [(win[block_][:, k, c:c + w], hT[:, k, 0:n]) for k in range(KT)]))

            def project_heads(name, c, n):
                def emit(b):
                    for k in range(KT):
                        for q in range(2):
                            cc = c + q * DK
                            ins = pe.matmul(b[64 * q:64 * q + 64, 0:n], win["qk"][:, k, cc:cc + 64], hT[:, k, 0:n],
                                            start=k == 0, stop=k == KT - 1)
                    return ins
                job(name, emit)

            def project_rows(name, t, c):
                c0 = cols[t][0]
                n = rows[t]
                job(name, lambda b: chain(b[0:n, 0:DC], [(hT[:, k, c0:c0 + n], win["vr"][:, k, c:c + DC]) for k in range(KT)]))

            pe.wait_ge(ld_win["z"], 16)
            project("Z", "z", 0, RANK, TALL)
            pe.wait_ge(ld_win["qk"], 16)
            project_heads("Q0", 0, TOUT)
            copied(pe, "Z")
            pe.wait_ge(ld_gate, 16 * 5)
            for p in range(2):
                def emit(b, p=p):
                    for q in range(2):
                        c = (2 * p + q) * DK
                        ins = pe.matmul(b[64 * q:64 * q + 64, 0:TALL], wg2[0:RANK, c:c + 64], zT[0:RANK, :], start=True, stop=True)
                    return ins
                job(f"G{p}", emit)
            project_heads("Q1", 2 * DK, TOUT)
            project_heads("K0", DQK, TALL)
            project_heads("K1", DQK + 2 * DK, TALL)
            pe.wait_ge(ld_packA, 16 * 7)
            job("SA", lambda b: transposes([(b[:, m * 40:(m + 1) * 40], packA[:, m * P:(m + 1) * P], 40) for m in range(MA)]))
            pe.wait_ge(ld_packB, 16 * 4)
            job("SB", lambda b: transposes([(b[:, m * 34:(m + 1) * 34], packB[:, m * P:(m + 1) * P], 34) for m in range(MB)]))
            pe.wait_ge(ld_packS, 16)
            job("SS", lambda b: transposes([(b[:, (2 * a + m) * 120:(2 * a + m + 1) * 120], packS[:, a, m * P:(m + 1) * P], 120)
                                            for a in range(2) for m in range(MB)]))
            pe.wait_ge(ld_win["xa"], 16)
            for m in range(MA):
                project(f"XA{m}", "xa", m * P, P, TALL)
            pe.wait_ge(ld_win["vbgb"], 16)
            for m in range(MB):
                project(f"GB{m}", "vbgb", DB + m * P, P, TALL)
                project(f"VB{m}", "vbgb", m * P, P, TALL)
            pe.wait_ge(ld_win["vr"], 16)
            def emit_vr2(b):
                for k in range(KT):
                    for q in range(2):
                        ins = pe.matmul(b[64 * q:64 * q + T2, 0:DC], hT[:, k, SEQ:TALL], win["vr"][:, k, q * DC:(q + 1) * DC],
                                        start=k == 0, stop=k == KT - 1)
                return ins
            job("VR2", emit_vr2)
            project_rows("V0", 0, 0)
            pe.wait_ge(xc_ready, MA)
            pe.wait_ge(ld_wbd, 16 * 20)
            for g, name in enumerate(("RG", "IG")):
                for m in range(MA):
                    ks = [k for k in range(MA) if abs(k - m) <= 1]
                    job(f"{name}{m}", lambda b: chain(b[:, 0:TALL], [(wbd[:, g, k, m * P:(m + 1) * P], xc[:, k, :]) for k in ks]))
            project_rows("V1", 1, 0)
            pe.wait_ge(ld_win["ga"], 16)
            for m in range(MA):
                project(f"GA{m}", "ga", m * P, P, TOUT)

            cols0 = [cols[0], cols[1], (2 * P, TALL)]

            def keys_job(c):
                n = rows0[c]
                job(f"KT{c}", lambda b: transposes([(b[0:n, p * P:(p + 1) * P], k_sb[:, p, cols0[c][0]:cols0[c][1]], P)
                                                    for p in range(2)]))

            def scores_jobs(c):
                c0, c1 = cols[c]
                n = rows[c]
                for o, par in enumerate("eo"):
                    def emit(b):
                        for p in range(2):
                            r = slice(64 * o, 64 * o + DK)
                            ins = pe.matmul(b[0:n, p * n:(p + 1) * n], kc[r, p, c0:c1], qc[r, p, c0:c1], start=True, stop=True)
                        return ins
                    job(f"SC{c}{par}", emit)

            def outputs_jobs(c):
                c0, c1 = cols[c]
                n = rows[c]
                copied(pe, f"SC{c}e")
                copied(pe, f"SC{c}o")
                if c == 2:
                    def emit_q(b):
                        for p in range(2):
                            for a in range(NSEQ):
                                ins = pe.matmul(b[0:2 * SAMP, p * DV:(p + 1) * DV], qm[:, p, a * 2 * SAMP:(a + 1) * 2 * SAMP],
                                                S0[:, p, a, :], start=a == 0, stop=a == NSEQ - 1)
                        return ins

                    def emit_s(b):
                        for h in range(NH):
                            ins = pe.matmul(b[0:SAMP, h * DV:(h + 1) * DV], sc2[0:SAMP, h, :], v_sb[0:SAMP, 2, h * DV:(h + 1) * DV],
                                            start=True, stop=True)
                        return ins
                    job("O2q", emit_q)
                    job("O2s", emit_s)
                    return
                for o, par in enumerate("eo"):
                    def emit(b):
                        for p in range(2):
                            h, r = 2 * p + o, slice(64 * o, 64 * o + DK)
                            out = b[0:n, p * DV:(p + 1) * DV]
                            pe.matmul(out, sc[:, h, :], v_sb[0:n, c, h * DV:(h + 1) * DV], start=True, stop=False)
                            ins = pe.matmul(out, q_sb[r, p, c0:c1], Sp[r, p, :], start=False, stop=True)
                        return ins
                    job(f"O{c}{par}", emit)

            def state_job(name, c, r0, r1):
                copied(pe, f"KT{c}")

                def emit(b):
                    for h in range(NH):
                        base, p = head(h)
                        ins = pe.matmul(b[base:base + 64, p * DV:(p + 1) * DV], kT_sb[r0:r1, c, p, base:base + 64],
                                        v_sb[r0:r1, c, h * DV:(h + 1) * DV], start=True, stop=True)
                    return ins
                job(name, emit)

            def sample_state_jobs(p):
                pe.wait_ge(vm_ready, p + 1)
                for a in range(2):
                    def emit(b):
                        for q in range(2):
                            ins = pe.matmul(b[64 * q:64 * q + 64, 0:4 * DV], kT_sb[0:SAMP, 2, p, 64 * q:64 * q + 64],
                                            vm[0:SAMP, q, 4 * a:4 * a + 4, :], start=True, stop=True)
                        return ins
                    job(f"W{p}{a}", emit)

            def y_c_job(t, n_ready):
                pe.wait_ge(o_ready, n_ready)
                n = rows[t]
                job(f"YC{t}", lambda b: transposes([(b[:, k * P:k * P + n], o_sb[0:n, t, k * P:(k + 1) * P], n) for k in range(MC)]))

            pe.wait_ge(qk_decayed, 4)
            keys_job(2)
            scores_jobs(2)
            project_rows("R0", 0, DC)
            copied(pe, "VR2")
            state_job("STM", 2, SAMP, T2)
            keys_job(0)
            scores_jobs(0)
            project_rows("R1", 1, DC)
            copied(pe, "V0")
            copied(pe, "STM")
            outputs_jobs(0)
            keys_job(1)
            state_job("ST0", 0, 0, P)
            scores_jobs(1)
            pe.wait_ge(ld_S0, 16 * NH)
            outputs_jobs(2)
            copied(pe, "V1")
            copied(pe, "ST0")
            outputs_jobs(1)
            state_job("ST1", 1, 0, P)
            pe.wait_ge(outcols_ready, 2)
            job("OA", lambda b: transposes([(b[0:36, m * P:(m + 1) * P], oaT[:, m, :], P) for m in range(MA)]))
            job("OB", lambda b: transposes([(b[0:62, m * P:(m + 1) * P], obT[:, m, :], P) for m in range(MB)]))
            pe.wait_ge(uc_ready, 1)
            job("MU", lambda b: chain(b[:, 0:TOUT], [(ones[:, :], uc[:, m, :]) for m in range(MB)]))
            sample_state_jobs(0)
            pe.wait_ge(sq_ready, 1)
            job("VAR", lambda b: chain(b[:, 0:TOUT], [(ones[:, :], sgb[:, m, 0:TOUT]) for m in range(MB)]))
            y_c_job(2, 1)
            y_c_job(0, 2)
            pe.wait_ge(ya_ready, MA)
            pe.wait_ge(ld_wout[0], 16)
            pe.wait_ge(ld_wout[1], 16)
            copied(pe, "YC2")

            def emit_p2(b):
                order = [k for k in range(KT) if not MA <= k < MA + MB] + list(range(MA, MA + MB))
                for i, k in enumerate(order):
                    if k == MA:
                        pe.wait_ge(yb_ready, MB)
                    for c in range(2):
                        ins = pe.matmul(b[64 * c:64 * c + 64, :], yT[:, k, SEQ:SEQ + 64], wout[:, k, c * 512:(c + 1) * 512],
                                        start=i == 0, stop=i == KT - 1)
                return ins
            job("P2", emit_p2)
            y_c_job(1, 3)
            sample_state_jobs(1)

            def p_jobs(t):
                copied(pe, f"YC{t}")
                for c in range(2):
                    job(f"P{t}{c}", lambda b: chain(b[:, :], [(yT[:, k, cols[t][0]:cols[t][1]], wout[:, k, c * 512:(c + 1) * 512])
                                                              for k in range(KT)]))

            def h_job(name, t, k0, nk, n_ready):
                pe.wait_ge(h1_ready, n_ready)
                w = rows[t]
                job(name, lambda b: transposes([(b[:, k * w:(k + 1) * w], xt[0:w, t, (k0 + k) * P:(k0 + k + 1) * P], w)
                                                for k in range(nk)]))

            def logits_job(t, *parts):
                def emit(b):
                    for k in range(KT):
                        if k % (KT // len(parts)) == 0:
                            copied(pe, parts[k * len(parts) // KT])
                        ins = pe.matmul(b[0:rows[t], 0:NE], hT[:, k, cols[t][0]:cols[t][1]], wr[:, k, :],
                                        start=k == 0, stop=k == KT - 1)
                    return ins
                job(f"LG{t}", emit)

            def biases(j):
                for b in range(2):
                    for h in range(2):
                        c = (2 * b + h) * 512
                        pe.matmul(bank[b][64 * h:64 * h + 64, :], bsel[:, j, :], b1_sb[:, c:c + 512], start=True, stop=False)

            p_jobs(0)
            pe.wait_ge(ld_router, 32)
            h_job("H2", 2, 0, 8, 1)
            logits_job(2, "H2")
            p_jobs(1)
            h_job("H0a", 0, 0, 4, 2)
            h_job("H0b", 0, 4, 4, 2)
            logits_job(0, "H0a", "H0b")
            copied(pe, "P11")
            copied(pe, "H0a")
            pe.wait_ge(ld_moe, 32)
            pe.wait_ge(bsel_ready, 1)
            biases(0)
            h_job("H1a", 1, 0, 4, 3)
            h_job("H1b", 1, 4, 4, 3)
            logits_job(1, "H1a", "H1b")

            def places(b):
                for i, t in enumerate(TILES):
                    for u in TILES[:i]:
                        pe.matmul(b[:, t * NE:(t + 1) * NE], ones[:, :], M[:, u, :], start=u == TILES[0], stop=False)
                    pe.wait_ge(mask_ready, i + 1)
                    ins = pe.matmul(b[:, t * NE:(t + 1) * NE], upper[:, :], M[:, t, :], start=i == 0, stop=True)
                return ins
            job("POS", places)
            assert job.n == len(JOBS)
            for name in JOBS[-8:-1]:
                copied(pe, name)
            for t in range(3):
                ins = pe.matmul(bank[4][:, 0:NE], ones[:, :], M[:, t, :], start=t == 0, stop=t == 2)
            ins.then_inc(counts_full, 1)

            def gather(half):
                for k in range(4 * half, 4 * half + 4):
                    out = bank[(2, 5)[k // 4]][:, (k % 4) * 2 * CAP:(k % 4 + 1) * 2 * CAP]
                    for t in range(3):
                        ins = pe.matmul(out, xt[:, t, k * P:(k + 1) * P], pick[:, t, :], start=t == 0, stop=t == 2)
                ins.then_inc(gather_full, 1)

            def combine(pi, c0, c1):
                for c in range(c0, c1):
                    t, h = TILES[c // 2], c % 2
                    if c >= 2:
                        pe.wait_ge(y_added, 6 * pi + c - 1)
                    pe.matmul(bank[6 + c % 2][0:rows[t], :], putT[:, t * P:t * P + rows[t]], eout[:, h, :],
                              start=True, stop=True).then_inc(comb_full, 1)

            pe.wait_ge(pick_ready, 1)
            gather(0)
            pe.wait_ge(gates_ready, 1)
            for t in range(3):
                ins = pe.transpose(bank[3][0:NE, t * P:(t + 1) * P], gates[:, t, :], ident[:, :])
            ins.then_inc(putT_full, 1)
            pe.wait_ge(routed, 1)
            n_pass = pe.value_load(npass[0:1, 0:1], min_val=1, max_val=PASSES)
            with pe.Fori(0, n_pass) as r:
                with pe.Fori(0, NE // GROUP) as g:
                    uses = (r * (NE // GROUP) + g) * (GROUP * PIECES // SLOTS)
                    for q in range(2):
                        pi = r * PAIRS + 2 * g + q
                        for j in range(2):
                            n = 2 * pi + j

                            def slot_of(c):
                                k = (2 * q + j) * PIECES + c
                                pe.wait_ge(w_full[k % SLOTS], 16 * (uses + k // SLOTS + 1))
                                return k % SLOTS * SLOT

                            for k in range(KT):
                                if j == 0 and k == 3:
                                    gather(1)
                                if j == 0 and k % 4 == 0:
                                    pe.wait_ge(xT_ready, 2 * pi + 1 + k // 4)
                                at_ = slot_of(k)
                                for b in range(2):
                                    for h in range(2):
                                        c = at_ + (2 * b + h) * 512
                                        ins = pe.matmul(bank[b][64 * h:64 * h + 64, :], xT[:, q, k, j * CAP:(j + 1) * CAP],
                                                        ring[:, c:c + 512], start=False, stop=k == KT - 1)
                                ins.then_inc(w_used, 1)
                            if j == 1:
                                pe.wait_ge(pick_ready, pi + 2)
                                gather(0)
                            else:
                                pe.wait_ge(putT_ready, pi + 1)
                                pe.wait_ge(out_ready, 4 * pi + 1)
                                combine(pi, 0, 2)
                            pe.wait_ge(act_ready, n + 1)
                            for k in range(4):
                                ins = pe.transpose(bank[3][:, k * P:(k + 1) * P], l1[:, k * P:(k + 1) * P], ident[:, :])
                            ins.then_inc(actT_full, 1)
                            pe.wait_ge(actT_ready, n + 1)
                            if j == 1:
                                pe.wait_ge(put_ready, n + 1)
                                for t in range(3):
                                    ins = pe.transpose(bank[3][:, t * P:(t + 1) * P], put[:, t, :], ident[:, :])
                                ins.then_inc(putT_full, 1)
                                pe.wait_ge(out_ready, 2 * n + 1)
                            for k in range(KT):
                                if j == 0 and k in (4, 6):
                                    combine(pi, k - 2, k)
                                if k % 2 == 0:
                                    at_ = slot_of(8 + k // 2)
                                for h in range(2):
                                    c = at_ + k % 2 * D + h * 512
                                    a = actT[:, k % 4, (k // 4) * CAP:(k // 4 + 1) * CAP]
                                    ins = pe.matmul(bank[4][64 * h:64 * h + 64, :], a, ring[:, c:c + 512],
                                                    start=k == 0, stop=k == KT - 1)
                                if k % 2 == 1:
                                    ins.then_inc(w_used, 1)
                            pe.wait_ge(bsel_ready, n + 2)
                            biases(1 - j)
            pe.wait_ge(putT_ready, n_pass * PAIRS + 1)
            pe.wait_ge(out_ready, n_pass * (4 * PAIRS) + 1)
            combine(n_pass * PAIRS, 0, 6)


_INS = ["x_prompt", "x_sample", "state_conv_a", "state_rglru", "state_conv_b", "state_gla", "meta_tokens", "ln0_g", "ln0_b",
        "w_in", "conv_a_w", "conv_a_b", "w_rg", "b_rg", "w_ig", "b_ig", "lru_lambda", "conv_b_w", "conv_b_b", "ln_b_g",
        "ln_b_b", "w_gate2", "b_gate", "gla_norm_g", "w_out", "ln1_g", "ln1_b", "router_w", "router_b", "moe_w1",
        "moe_b1", "moe_w2", "moe_b2", "ln2_g", "ln2_b"]
_OUTS = [(1, SEQ, D), (NSEQ, DSEQ, D), (1, 1, WA - 1, DA), (1, 1, DA), (1, 1, WB - 1, DB), (1, 1, NH, DK, DV),
         (1, NSEQ, WA - 1, DA), (1, NSEQ, DA), (1, NSEQ, WB - 1, DB), (1, NSEQ, NH, DK, DV)]


def kernel(**inputs):
    import numpy as _np
    import concourse.bacc as _bacc
    from concourse.bass_utils import run_bass_kernel_spmd as _run

    nc = _bacc.Bacc("TRN2", target_bir_lowering=False, num_devices=1)
    arrays, args = {}, []
    for name in _INS:
        a = _np.ascontiguousarray(inputs[name])
        arrays[f"in_{name}_dram"] = a
        args.append(nc.dram_tensor(f"in_{name}_dram", a.shape, mybir.dt.from_np(a.dtype), kind="ExternalInput").ap())
    for i, shape in enumerate(_OUTS):
        args.append(nc.dram_tensor(f"out_{i}_dram", shape, F32, kind="ExternalOutput").ap())
    build_kernel(nc, *args)
    r = _run(nc, [arrays], core_ids=[0])
    return tuple(r.results[0][f"out_{i}_dram"] for i in range(len(_OUTS)))
```
